# Optimizing a Trainium2 kernel written in Bass

```python
import jax, jax.numpy as jnp
from jax import lax
import numpy as np

D_MODEL = 1024
BATCH = 1
SEQ = 1024
DEPTH = 1

HEAD_DIM = 64
N_Q_HEADS = 8
N_KV_HEADS = 2
Q_PER_KV = N_Q_HEADS // N_KV_HEADS
ATTN_WIDTH = N_Q_HEADS * HEAD_DIM
KV_WIDTH = N_KV_HEADS * HEAD_DIM
WINDOW = 128
BLOCK = 128
ROPE_THETA = 500000.0
ROT_DIM = HEAD_DIM // 4
POOL_WINDOWS = (2, 4, 8, 16)
N_POOL_GROUPS = len(POOL_WINDOWS)
POOL_WIDTH = D_MODEL - ATTN_WIDTH
POOL_GROUP_WIDTH = POOL_WIDTH // N_POOL_GROUPS
MIX_WIDTH = ATTN_WIDTH + POOL_WIDTH
IN_PROJ_WIDTH = ATTN_WIDTH + 2 * KV_WIDTH + POOL_WIDTH
D_FF = 2816
FFN_RESIDUAL_WEIGHT = 0.5
LN_EPS = 1e-5
DEEPNORM_ALPHA = (2.0 * DEPTH) ** 0.25
DEEPNORM_BETA = (8.0 * DEPTH) ** -0.25
N_SUBLAYERS = 3
ADA_WIDTH = 3 * N_SUBLAYERS * D_MODEL
NEG_INF = -1e30

kernel_name = "hymba_swa_sink_multiscale_pool_macaron_deepnorm_adaln"

def layer_norm(x, g, b):
    xf = x.astype(jnp.float32)
    mu = jnp.mean(xf, axis=-1, keepdims=True)
    var = jnp.mean(jnp.square(xf - mu), axis=-1, keepdims=True)
    y = (xf - mu) * lax.rsqrt(var + LN_EPS)
    return (y * g.astype(jnp.float32) + b.astype(jnp.float32)).astype(x.dtype)

def modulate(h, shift, scale):
    return h * (1.0 + scale[:, None, :]) + shift[:, None, :]

def swiglu(u, w1, w3, w2):
    return (jax.nn.silu(u @ w1) * (u @ w3)) @ w2

def partial_rope(t):
    s = t.shape[1]
    inv_freq = ROPE_THETA ** (-jnp.arange(0, ROT_DIM, 2, dtype=jnp.float32) / ROT_DIM)
    ang = jnp.arange(s, dtype=jnp.float32)[:, None] * inv_freq[None, :]
    cos = jnp.cos(ang)[None, :, None, :]
    sin = jnp.sin(ang)[None, :, None, :]
    tr = t[..., :ROT_DIM].astype(jnp.float32)
    t1, t2 = tr[..., :ROT_DIM // 2], tr[..., ROT_DIM // 2:]
    rot = jnp.concatenate([t1 * cos - t2 * sin, t2 * cos + t1 * sin], axis=-1).astype(t.dtype)
    return jnp.concatenate([rot, t[..., ROT_DIM:]], axis=-1)

def sliding_window_attention(q, k, v, sinks):
    b, s = q.shape[0], q.shape[1]
    nb = s // BLOCK
    qb = q.reshape(b, nb, BLOCK, N_KV_HEADS, Q_PER_KV, HEAD_DIM)

    def band(t):
        tb = t.reshape(b, nb, BLOCK, N_KV_HEADS, HEAD_DIM)
        prev = jnp.pad(tb, ((0, 0), (1, 0), (0, 0), (0, 0), (0, 0)))[:, :-1]
        return jnp.concatenate([prev, tb], axis=2)

    kb, vb = band(k), band(v)
    scores = jnp.einsum('bnqhgd,bnkhd->bnhgqk', qb, kb).astype(jnp.float32) * (HEAD_DIM ** -0.5)
    blk = jnp.arange(nb)[:, None, None]
    qpos = blk * BLOCK + jnp.arange(BLOCK)[None, :, None]
    kpos = (blk - 1) * BLOCK + jnp.arange(2 * BLOCK)[None, None, :]
    rel = qpos - kpos
    valid = (rel >= 0) & (rel < WINDOW) & (kpos >= 0)
    scores = jnp.where(valid[None, :, None, None], scores, NEG_INF)
    sink = sinks.astype(jnp.float32).reshape(N_KV_HEADS, Q_PER_KV)[None, None, :, :, None, None]
    sink = jnp.broadcast_to(sink, scores.shape[:-1] + (1,))
    probs = jax.nn.softmax(jnp.concatenate([scores, sink], axis=-1), axis=-1)[..., :-1]
    out = jnp.einsum('bnhgqk,bnkhd->bnqhgd', probs.astype(v.dtype), vb)
    return out.reshape(b, s, N_Q_HEADS * HEAD_DIM)

def multiscale_pool(p, w_pool, pool_scale):
    b, s, _ = p.shape
    pf = p.astype(jnp.float32)
    cs = jnp.pad(jnp.cumsum(pf, axis=1), ((0, 0), (1, 0), (0, 0)))
    t = jnp.arange(s)
    means = []
    for g, w in enumerate(POOL_WINDOWS):
        sl = slice(g * POOL_GROUP_WIDTH, (g + 1) * POOL_GROUP_WIDTH)
        start = jnp.maximum(t + 1 - w, 0)
        window_sum = cs[:, t + 1, sl] - cs[:, start, sl]
        count = (t + 1 - start).astype(jnp.float32)
        means.append(window_sum / count[None, :, None])
    pooled = jnp.stack(means, axis=2)
    diff = (pooled - pf.reshape(b, s, N_POOL_GROUPS, POOL_GROUP_WIDTH)).astype(p.dtype)
    mixed = jnp.einsum('bsgc,gcd->bsgd', diff, w_pool).reshape(b, s, POOL_WIDTH)
    return mixed * pool_scale

def setup_inputs(seed: int = 0) -> dict:
    key = jax.random.key(seed)
    ks = jax.random.split(key, 24)
    L, D = DEPTH, D_MODEL

    def nrm(k, shape, scale):
        return jax.random.normal(k, shape, jnp.float32) * scale

    v_cols = jnp.ones((IN_PROJ_WIDTH,), jnp.float32).at[
        ATTN_WIDTH + KV_WIDTH:ATTN_WIDTH + 2 * KV_WIDTH].set(DEEPNORM_BETA)
    return {
        "x": nrm(ks[0], (BATCH, SEQ, D), 1.0),
        "c": nrm(ks[1], (BATCH, D), 1.0),
        "w_ada": nrm(ks[2], (L, D, ADA_WIDTH), 0.1 * D ** -0.5),
        "b_ada": nrm(ks[3], (L, ADA_WIDTH), 0.01),
        "ffn1_w1": nrm(ks[4], (L, D, D_FF), D ** -0.5),
        "ffn1_w3": nrm(ks[5], (L, D, D_FF), D ** -0.5),
        "ffn1_w2": nrm(ks[6], (L, D_FF, D), DEEPNORM_BETA * D_FF ** -0.5),
        "ln1_g": 1.0 + nrm(ks[7], (L, D), 0.05),
        "ln1_b": nrm(ks[8], (L, D), 0.05),
        "w_in": nrm(ks[9], (L, D, IN_PROJ_WIDTH), D ** -0.5) * v_cols,
        "b_in": nrm(ks[10], (L, IN_PROJ_WIDTH), 0.01),
        "attn_sinks": nrm(ks[11], (L, N_Q_HEADS), 0.5),
        "w_pool": nrm(ks[12], (L, N_POOL_GROUPS, POOL_GROUP_WIDTH, POOL_GROUP_WIDTH), POOL_GROUP_WIDTH ** -0.5),
        "pool_scale": 1.0 + nrm(ks[13], (L, POOL_WIDTH), 0.1),
        "w_out": nrm(ks[14], (L, MIX_WIDTH, D), DEEPNORM_BETA * MIX_WIDTH ** -0.5),
        "b_out": nrm(ks[15], (L, D), 0.01),
        "ln2_g": 1.0 + nrm(ks[16], (L, D), 0.05),
        "ln2_b": nrm(ks[17], (L, D), 0.05),
        "ffn2_w1": nrm(ks[18], (L, D, D_FF), D ** -0.5),
        "ffn2_w3": nrm(ks[19], (L, D, D_FF), D ** -0.5),
        "ffn2_w2": nrm(ks[20], (L, D_FF, D), DEEPNORM_BETA * D_FF ** -0.5),
        "ln3_g": 1.0 + nrm(ks[21], (L, D), 0.05),
        "ln3_b": nrm(ks[22], (L, D), 0.05),
    }

def reference(x, c, w_ada, b_ada, ffn1_w1, ffn1_w3, ffn1_w2, ln1_g, ln1_b,
              w_in, b_in, attn_sinks, w_pool, pool_scale, w_out, b_out, ln2_g, ln2_b,
              ffn2_w1, ffn2_w3, ffn2_w2, ln3_g, ln3_b):
    b, s, _ = x.shape
    h = x
    c_act = jax.nn.silu(c)
    for l in range(DEPTH):
        mods = (c_act @ w_ada[l] + b_ada[l]).astype(h.dtype)
        (sh1, sc1, gt1, sh2, sc2, gt2, sh3, sc3, gt3) = jnp.split(mods, 3 * N_SUBLAYERS, axis=-1)

        u = modulate(h, sh1, sc1)
        f = swiglu(u, ffn1_w1[l], ffn1_w3[l], ffn1_w2[l])
        h = layer_norm(DEEPNORM_ALPHA * h + FFN_RESIDUAL_WEIGHT * (1.0 + gt1[:, None, :]) * f,
                       ln1_g[l], ln1_b[l])

        u = modulate(h, sh2, sc2)
        z = u @ w_in[l] + b_in[l]
        q = z[..., :ATTN_WIDTH].reshape(b, s, N_Q_HEADS, HEAD_DIM)
        k = z[..., ATTN_WIDTH:ATTN_WIDTH + KV_WIDTH].reshape(b, s, N_KV_HEADS, HEAD_DIM)
        v = z[..., ATTN_WIDTH + KV_WIDTH:ATTN_WIDTH + 2 * KV_WIDTH].reshape(b, s, N_KV_HEADS, HEAD_DIM)
        p = z[..., ATTN_WIDTH + 2 * KV_WIDTH:]
        a = sliding_window_attention(partial_rope(q), partial_rope(k), v, attn_sinks[l])
        m = multiscale_pool(p, w_pool[l], pool_scale[l])
        y = jnp.concatenate([a, m], axis=-1) @ w_out[l] + b_out[l]
        h = layer_norm(DEEPNORM_ALPHA * h + (1.0 + gt2[:, None, :]) * y, ln2_g[l], ln2_b[l])

        u = modulate(h, sh3, sc3)
        f = swiglu(u, ffn2_w1[l], ffn2_w3[l], ffn2_w2[l])
        h = layer_norm(DEEPNORM_ALPHA * h + FFN_RESIDUAL_WEIGHT * (1.0 + gt3[:, None, :]) * f,
                       ln3_g[l], ln3_b[l])
    return h


_drawn_inputs = setup_inputs


def setup_inputs(seed=0):
    import zlib

    import numpy as np

    out = dict(_drawn_inputs(seed))
    spreads = {}
    factors = {'b_ada': 8.0, 'b_in': 21.408, 'attn_sinks': 30.059, 'b_out': 7.036}
    for name, (base, spread) in spreads.items():
        noise = np.random.default_rng([zlib.crc32(name.encode()), seed]).standard_normal(out[name].shape)
        drawn = base * np.exp(spread * noise) if base else spread * noise
        out[name] = __import__('jax').numpy.asarray(drawn.astype(out[name].dtype))
    for name, factor in factors.items():
        out[name] = (out[name] * factor).astype(out[name].dtype)
    return out
```

```python
import concourse.bass as bass
from concourse import mybir
from contextlib import ExitStack

P = 128
D = 1024
S = 1024
H = 512
KC = D // P
FF = 2816
ITER = FF // (2 * P)
HEAD = 64
NH = 8
WIN = (2, 4, 8, 16)
PAD = 16
ALPHA = 2.0 ** 0.25
EPS = 1e-5
NVEC = 9
IN_W = 1280
IN_PAIRS = 5
OUT_PAIRS = 4
PAIR0 = (0, 2 * ITER + 2 * IN_PAIRS + 2 * OUT_PAIRS)
MIX0 = 2 * ITER
ADA_EARLY = 2
ADA_UNITS = NVEC - ADA_EARLY

V_BADA, V_LN, V_BOUT, V_BIN, V_PS = 0, 72, 120, 128, 138
NV = 142
C_A, C_B, C_AG, C_AB, C_GATE, C_N = 0, 8, 16, 24, 32, 40

Q, K, V, PL = "q", "k", "v", "p"
Z_ORDER = ([(K, 0), (V, 0), (Q, 0), (Q, 1), (Q, 2), (Q, 3), (PL, 0), (PL, 1), (PL, 2), (PL, 3)],
           [(K, 0), (V, 0), (PL, 0), (PL, 1), (PL, 2), (PL, 3), (Q, 0), (Q, 1), (Q, 2), (Q, 3)])
Z_COL = {Q: 0, K: 4, V: 5, PL: 6}
Z_DMAS = {Q: 2, K: 1, V: 1, PL: 1}
NZ = 10
OUT0 = 2 * NZ
OUT_DMAS = 3


def pair_dmas(n):
    if n < MIX0 or n >= PAIR0[1]:
        return 2
    m = 2 * (n - MIX0)
    if m < OUT0:
        return sum(Z_DMAS[Z_ORDER[m // NZ][m % NZ + j][0]] for j in range(2))
    return 2 * OUT_DMAS


def raw_count(n):
    return 16 * sum(pair_dmas(x) for x in range(n % 2, n + 1, 2))


def above(eng, sem, n):
    if not isinstance(n, int) or n > 0:
        eng.wait_ge(sem, n)


def layer(nc, t, o_out):
    f32, f32r, u32 = mybir.dt.float32, mybir.dt.float32r, mybir.dt.uint32
    ALU, ACT, AX = mybir.AluOpType, mybir.ActivationFunctionType, mybir.AxisListType
    cur = [(nc.sbuf_base + 31) // 32 * 32]

    def at(name, shape, dtype, offset=None):
        size = 4
        for x in shape[1:]:
            size *= x
        if offset is None:
            offset = cur[0]
            cur[0] += (size + 31) // 32 * 32
        return nc.alloc_sbuf_tensor_at(name, shape, dtype, offset=offset)

    u_at = cur[0]
    u_hi = at("u_hi", [P, KC, S], f32r)
    u_lo = at("u_lo", [P, KC, S], f32r)
    acc = at("acc", [P, KC, S], f32)
    w_raw = [at(f"w_raw{s}", [P, 2, KC, P], f32) for s in range(2)]
    w_hi = [at(f"w_hi{s}", [P, 2, KC, P], f32r) for s in range(2)]
    w_lo = [at(f"w_lo{s}", [P, 2, KC, P], f32r) for s in range(2)]
    hid = at("hid", [P, 4, PAD + H], f32)
    scratch = at("scratch", [P, 3, D], f32)
    ident = at("ident", [P, P], f32)
    ones = at("ones", [P, P], f32)
    mean_w = at("mean_w", [P, P], f32)
    vec = at("vec", [P, NV], f32)
    mods = at("mods", [P, NVEC * KC], f32)
    coef = at("coef", [P, 4 * C_N], f32)
    c_act = at("c_act", [P, KC], f32)
    small = at("small", [P, 64], f32)
    half_pow = small[:, 0:4]
    var_eps = small[:, 4:8]
    rstd = small[:, 8:12]
    row_max, neg_max, sink_sh, sink_exp = (small[:, 12 + 4 * i:16 + 4 * i] for i in range(4))
    row_sum, denom, recip = (small[:, 28 + 4 * i:32 + 4 * i] for i in range(3))
    sinks, neg_sinks = small[:, 40:48], small[:, 48:56]
    over = cur[0]
    g_hi = at("g_hi", [P, 2, 2, H], f32r)
    g_lo = at("g_lo", [P, 2, 2, H], f32r)
    w2_hi = at("w2_hi", [P, 2, D], f32r)
    w2_lo = at("w2_lo", [P, 2, D], f32r)
    w2_raw = at("w2_raw", [P, 2, D], f32)
    assert cur[0] <= nc.sbuf_usable_end, (cur[0], nc.sbuf_usable_end)
    x_nat = at("x_nat", [P, S // P, D], f32, over)
    ada_sb = [at(f"ada{v}", [P, KC, D], f32, u_at + v * KC * S * 4) for v in range(ADA_EARLY)]
    x_u32 = at("x_u32", [P, 2, H], f32, over + 4096)
    vec_rows = [at(f"vec_rows{r}", [P, P], f32, cur[0] - 8192 + 512 * r) for r in range(2)]
    c_rows = at("c_rows", [KC, P], f32, cur[0] - 8192 + 1024)
    ffn_end = cur[0]
    cur[0] = over
    q_sb = at("q_sb", [P, 4, H], f32)
    k_sb = at("k_sb", [P, S], f32)
    v_sb = at("v_sb", [P, S // P, P], f32)
    v_tr = at("v_tr", [P, H], f32)
    rope = at("rope", [P, 2, H], f32)
    probs = at("probs", [P, 4, P], f32)
    pt = at("pt", [P, 2, 4, P], f32)
    pool_in = at("pool_in", [P, 4, PAD + H], f32)
    w_pool = at("w_pool", [P, 4, P], f32)
    own_mask = at("own_mask", [P, P], f32)
    own_t = at("own_t", [P, 2, P], f32)
    inv_cnt = at("inv_cnt", [P, 4, PAD], f32)
    assert cur[0] <= nc.sbuf_usable_end, (cur[0], nc.sbuf_usable_end)

    ctx = ExitStack()
    with ctx:
        ps = ctx.enter_context(nc.psum_tensor("ps", [P, 8, H], f32))

        def sem(name):
            return ctx.enter_context(nc.semaphore(name))

        c_in, c_tr, vec_in, x_in1 = sem("c_in"), sem("c_tr"), sem("vec_in"), sem("x_in1")
        x_in0 = [sem("x_in00"), sem("x_in01")]
        ada_in = [sem(f"ada_in{i}") for i in range(ADA_EARLY * KC)]
        early_acc = [sem(f"early_acc{v}") for v in range(ADA_EARLY)]
        const_ok, small_ok = sem("const_ok"), sem("small_ok")
        vec_t, vec_ok, cact_ok = sem("vec_t"), sem("vec_ok"), sem("cact_ok")
        mod0_ps, mod_ok, coef_ok = sem("mod0_ps"), sem("mod_ok"), sem("coef_ok")
        x_tr = sem("x_tr")
        raw_in = [sem("raw_in0"), sem("raw_in1")]
        wh_ok, wl_ok = sem("wh_ok"), sem("wl_ok")
        w2_in, w2h_ok, w2l_ok = sem("w2_in"), sem("w2h_ok"), sem("w2l_ok")
        ab_done, silu_ok, g_ok, gh_ok, gl_ok = (sem(n) for n in ("ab_done", "silu_ok", "g_ok", "gh_ok", "gl_ok"))
        f_done, f_used = sem("f_done"), sem("f_used")
        ada_tile = [sem("ada_tile0"), sem("ada_tile1")]
        ada_acc, ada_red = sem("ada_acc"), sem("ada_red")
        ln_sum, ln_mean, ln_cent, ln_sq, sq_used = (sem(n) for n in ("ln_sum", "ln_mean", "ln_cent", "ln_sq", "sq_used"))
        ln_var, ln_veps, ln_rstd, ln_diag, ln_bc, ln_t = (sem(n) for n in ("ln_var", "ln_veps", "ln_rstd", "ln_diag", "ln_bc", "ln_t"))
        u32_ok, uh_ok, ul_ok, acc_ok = (sem(n) for n in ("u32_ok", "uh_ok", "ul_ok", "acc_ok"))
        z_done, z_used, o_used = sem("z_done"), sem("z_used"), sem("o_used")
        sink_in, tab_in, rope_in, mask_ok, sink_ok = sem("sink_in"), sem("tab_in"), sem("rope_in"), sem("mask_ok"), sem("sink_ok")
        shuf_ok, rope_s, rope_c, rope_ok = sem("shuf_ok"), sem("rope_s"), sem("rope_c"), sem("rope_ok")
        v_t, v_ok = sem("v_t"), sem("v_ok")
        pad_ok, win_ok, diff_ok, carry_ok = sem("pad_ok"), sem("win_ok"), sem("diff_ok"), sem("carry_ok")
        pool_done, ph_ok, pl_ok = sem("pool_done"), sem("ph_ok"), sem("pl_ok")
        sc_done, prev_ok, sel_ok, max_ok, neg_ok, sd_ok = (sem(n) for n in ("sc_done", "prev_ok", "sel_ok", "max_ok", "neg_ok", "sd_ok"))
        exp_ok, den_ok, rec_ok, prob_ok = sem("exp_ok"), sem("den_ok"), sem("rec_ok"), sem("prob_ok")
        t_done, pt_ok, pv_done, yh_ok, yl_ok = (sem(n) for n in ("t_done", "pt_ok", "pv_done", "yh_ok", "yl_ok"))
        fin_ok, fin_t, fin_sb = sem("fin_ok"), sem("fin_t"), sem("fin_sb")
        stored = [sem(f"stored{i}") for i in range(4)]

        def tok(h):
            return slice(h * H, (h + 1) * H)

        def new_input(st, c):
            if st == 0:
                return acc[:, c, tok(1)]
            return x_u32[:, c % 2] if st == 1 else scratch[:, 1 + c % 2, 0:H]

        w1 = (t["ffn1_w1"], t["ffn2_w1"])
        w3 = (t["ffn1_w3"], t["ffn2_w3"])
        w2 = (t["ffn1_w2"], t["ffn2_w2"])

        def load_ffn_pair(sp, f, i, j):
            for a, w in enumerate((w1[f], w3[f])):
                src = w.rearrange("(k p) n -> p k n", p=P)[:, :, bass.ds(i * (2 * P) + j * P, P)]
                sp.dma_start(w_raw[j][:, a], src).then_inc(raw_in[j], 16)

        def load_w2(sp, f, i):
            src = w2[f].rearrange("(m j p) n -> m p j n", p=P, j=2)[bass.ds(i, 1)]
            sp.dma_start(w2_raw[:, :, :], src.rearrange("m p j n -> (m p) j n")).then_inc(w2_in, 16)

        def load_mix_pair(sp, n):
            for j in range(2):
                m = 2 * (n - MIX0) + j
                dst = w_raw[n % 2][:, j]
                if m < OUT0:
                    kind, c = Z_ORDER[m // NZ][m % NZ]
                    src = t["w_in"].rearrange("(k p) n -> p k n", p=P)
                    if kind == Q:
                        for a in range(2):
                            col = (4 * a + c) * HEAD
                            sp.dma_start(dst[:, :, a * HEAD:(a + 1) * HEAD], src[:, :, col:col + HEAD]).then_inc(raw_in[n % 2], 16)
                    else:
                        col = (Z_COL[kind] + c) * P
                        sp.dma_start(dst, src[:, :, col:col + P]).then_inc(raw_in[n % 2], 16)
                else:
                    col = (m - OUT0) % KC * P
                    wo = t["w_out"][:, col:col + P]
                    for a in range(2):
                        src = wo[a * 4 * HEAD:(a + 1) * 4 * HEAD].rearrange("(c d) n -> d c n", d=HEAD)
                        sp.dma_start(dst[a * HEAD:(a + 1) * HEAD, 0:4], src).then_inc(raw_in[n % 2], 16)
                    src = wo[NH * HEAD:].rearrange("(k p) n -> p k n", p=P)
                    sp.dma_start(dst[:, 4:8], src).then_inc(raw_in[n % 2], 16)

        block = ctx.enter_context(nc.Block())

        @block.sync
        def _(sp):
            for v in (1, 0):
                for k in range(KC):
                    sp.dma_start(ada_sb[v][:, k], t["w_ada"][k * P:(k + 1) * P, v * D:(v + 1) * D]).then_inc(ada_in[v * KC + k], 16)
            x_rows = t["x"].rearrange("(b p) n -> p b n", p=P)
            for half in range(2):
                cols = slice(half * H, (half + 1) * H)
                sp.dma_start(x_nat[:, 0:4, cols], x_rows[:, 0:4, cols]).then_inc(x_in0[half], 16)
            load_ffn_pair(sp, 0, 0, 0)
            sp.dma_start(x_nat[:, 4:8], x_rows[:, 4:8]).then_inc(x_in1, 16)
            load_ffn_pair(sp, 0, 0, 1)
            sp.wait_ge(vec_ok, 1)
            load_w2(sp, 0, 0)

            def prefetch(f, i, last=False):
                n = PAIR0[f] + 2 * i
                for j in range(2):
                    sp.wait_ge(wl_ok, n + 1 + j)
                    if not last:
                        load_ffn_pair(sp, f, i + 1, j)
                    elif f == 0:
                        load_mix_pair(sp, MIX0 + j)
                if not last:
                    sp.wait_ge(w2l_ok, (ITER * f + i + 1) * 2)
                    load_w2(sp, f, i + 1)

            with sp.Fori(0, ITER - 1) as i:
                prefetch(0, i)
            prefetch(0, ITER - 1, last=True)
            for n in range(MIX0 + 2, PAIR0[1]):
                sp.wait_ge(wl_ok, n - 1)
                load_mix_pair(sp, n)
            for j in range(2):
                sp.wait_ge(wl_ok, PAIR0[1] + j - 1)
                load_ffn_pair(sp, 1, 0, j)
            sp.wait_ge(yl_ok, 16)
            sp.wait_ge(pl_ok, 8)
            load_w2(sp, 1, 0)
            with sp.Fori(0, ITER - 1) as i:
                prefetch(1, i)
            for r in range(2 * KC):
                h, c = r // KC, r % KC
                sp.wait_ge(fin_sb, r + 1)
                dst = o_out[h * H:(h + 1) * H, c * P:(c + 1) * P].rearrange("(b p) n -> p b n", p=P)
                sp.dma_start(dst, w_raw[0][:, r % 4 // 2, 4 * (r % 2):4 * (r % 2) + 4]).then_inc(stored[r % 4], 16)
            for s in range(4):
                sp.wait_ge(stored[s], 16 * (2 * KC // 4))

        @block.gpsimd
        def _(pool):
            pool.memset(ident[:, :], 0.0).then_inc(small_ok, 1)
            pool.memset(ones[:, :], 1.0).then_inc(small_ok, 1)
            pool.memset(mean_w[:, :], 1.0 / D).then_inc(small_ok, 1)
            pool.memset(half_pow, -0.5).then_inc(small_ok, 1)
            pool.wait_ge(small_ok, 4)
            pool.affine_select(out=ident[:, :], in_=ident[:, :], compare_op=ALU.not_equal, fill=1.0,
                               base=0, pattern=[[-1, P]], channel_multiplier=1).then_inc(const_ok, 1)

            wa = t["w_ada"].rearrange("(k p) n -> p k n", p=P)

            def ada_tiles(i):
                for k in range(KC):
                    above(pool, ada_acc, i * KC + k - 1)
                    pool.dma_start(scratch[:, k % 2, :], wa[:, k, bass.ds(i * D + ADA_EARLY * D, D)]).then_inc(ada_tile[k % 2], 16)

            pool.wait_ge(x_in0[1], 16)
            ada_tiles(0)
            with pool.Fori(1, ADA_UNITS) as i:
                ada_tiles(i)

            def power(s):
                pool.wait_ge(ln_veps, s + 1)
                pool.tensor_tensor(rstd, var_eps, half_pow, ALU.pow).then_inc(ln_rstd, 1)

            def rope_tables(h):
                pool.dma_start(rope[:, 0], t["rope_cos"][:, tok(h)]).then_inc(rope_in, 16)
                pool.dma_start(rope[:, 1], t["rope_sin"][:, tok(h)]).then_inc(rope_in, 16)

            power(0)
            pool.wait_ge(f_done, ITER * 2 * KC)
            rope_tables(0)
            pool.dma_start(w_pool[:, :, :], t["w_pool"].rearrange("g c d -> c g d")).then_inc(tab_in, 16)
            pool.dma_start(inv_cnt[:, :, :], t["inv_count"]).then_inc(tab_in, 16)
            pool.memset(own_mask[:, :], 1.0).then_inc(mask_ok, 1)
            pool.memset(own_t[:, :, :], 1.0).then_inc(mask_ok, 1)
            pool.wait_ge(mask_ok, 2)
            pool.affine_select(out=own_mask[:, :], in_=own_mask[:, :], compare_op=ALU.is_ge, fill=0.0,
                               base=0, pattern=[[-1, P]], channel_multiplier=1).then_inc(mask_ok, 1)
            pool.affine_select(out=own_t[:, 0], in_=own_t[:, 0], compare_op=ALU.is_ge, fill=0.0,
                               base=0, pattern=[[1, P]], channel_multiplier=-1).then_inc(mask_ok, 1)
            pool.affine_select(out=own_t[:, 1], in_=own_t[:, 1], compare_op=ALU.is_gt, fill=0.0,
                               base=0, pattern=[[-1, P]], channel_multiplier=1).then_inc(mask_ok, 1)
            power(1)
            pool.wait_ge(rope_ok, 5)
            rope_tables(1)
            for s in range(2, 6):
                power(s)

        def split_product(pe, out, w_h, w_l, x_h, x_l, start, stop):
            pe.matmul(out, w_h, x_h, start=start, stop=False)
            pe.matmul(out, w_h, x_l, start=False, stop=False)
            return pe.matmul(out, w_l, x_h, start=False, stop=stop)

        @block.tensor
        def _(pe):
            def chunk_product(out, slot, a, h, stage=None):
                for k in range(KC):
                    if stage is not None:
                        pe.wait_ge(ul_ok, KC * stage + k + 1)
                    mm = split_product(pe, out, w_hi[slot][:, a, k], w_lo[slot][:, a, k],
                                       u_hi[:, k, tok(h)], u_lo[:, k, tok(h)], k == 0, k == KC - 1)
                return mm

            def up(f, i, j, h, stage=None, between=None):
                e = 4 * (ITER * f + i) + 2 * h + j
                pe.wait_ge(wl_ok, PAIR0[f] + 2 * i + j + 1)
                above(pe, g_ok, e - 1)
                chunk_product(ps[:, 2 * j], j, 0, h, stage).then_inc(ab_done, 1)
                if between:
                    between()
                chunk_product(ps[:, 2 * j + 1], j, 1, h).then_inc(ab_done, 1)

            def down(f, i, h, d0=0, d1=KC):
                if d0 == 0:
                    pe.wait_ge(gl_ok, 4 * (ITER * f + i) + 2 * h + 2)
                    pe.wait_ge(w2l_ok, 2 * (ITER * f + i) + 2)
                for d in range(d0, d1):
                    above(pe, f_used, 2 * KC * (ITER * f + i) + KC * h + d - 1)
                    out = ps[:, 4 + d % 2]
                    for j in range(2):
                        mm = split_product(pe, out, w2_hi[:, j, d * P:(d + 1) * P], w2_lo[:, j, d * P:(d + 1) * P],
                                           g_hi[:, h, j], g_lo[:, h, j], j == 0, j == 1)
                    mm.then_inc(f_done, 1)

            def ada_reduce(i):
                pe.wait_ge(ada_acc, KC * i + KC)
                for c in range(KC):
                    mm = pe.matmul(ps[:, 6, c:c + 1], scratch[:, 2, c * P:(c + 1) * P], ones[:, 0:1], start=True, stop=True)
                mm.then_inc(ada_red, 1)

            def mean(s):
                pe.wait_ge(ln_sum, s + 1)
                pe.matmul(ps[:, 6], mean_w[:, :], scratch[:, 0, 0:H], start=True, stop=True).then_inc(ln_mean, 1)

            def variance(s):
                pe.wait_ge(sq_used, KC * (s + 1))
                for b in range(4):
                    mm = pe.matmul(ps[:, 7, b:b + 1], scratch[:, 0, H + b * P:H + (b + 1) * P], mean_w[:, 0:1], start=True, stop=True)
                mm.then_inc(ln_var, 1)

            def spread(s):
                pe.wait_ge(ln_diag, s + 1)
                pe.matmul(ps[:, 7], ones[:, :], scratch[:, 1, 0:H], start=True, stop=True).then_inc(ln_bc, 1)

            pe.wait_ge(const_ok, 1)
            pe.wait_ge(c_in, 16)
            pe.transpose(ps[:, 3, 0:KC], c_rows[:, :], ident[0:KC, 0:KC]).then_inc(c_tr, 1)
            pe.wait_ge(vec_in, 16 * 12)
            pe.transpose(ps[:, 2, 0:P], vec_rows[0][:, :], ident[:, :]).then_inc(vec_t, 1)
            pe.transpose(ps[:, 2, P:NV], vec_rows[1][0:NV - P, :], ident[0:NV - P, 0:NV - P]).then_inc(vec_t, 1)
            def x_transpose(r):
                h, c = r // KC, r % KC
                above(pe, ul_ok, r - 3)
                for b in range(4):
                    mm = pe.transpose(ps[:, 4 + r % 4, b * P:(b + 1) * P], x_nat[:, 4 * h + b, c * P:(c + 1) * P], ident[:, :])
                mm.then_inc(x_tr, 1)
            for v in (1, 0):
                pe.wait_ge(early_acc[v], KC)
                for c in range(KC):
                    mm = pe.matmul(ps[:, 3, v * KC + c:v * KC + c + 1], acc[:, v, c * P:(c + 1) * P], ones[:, 0:1], start=True, stop=True)
            mm.then_inc(mod0_ps, 1)
            for r in range(KC):
                if r % 4 == 0:
                    pe.wait_ge(x_in0[r // 4], 16)
                x_transpose(r)

            def ffn(f):
                if f == 0:
                    def more_x(r0, r1):
                        pe.wait_ge(x_in1, 16)
                        for r in range(r0, r1):
                            x_transpose(r)
                    up(0, 0, 0, 0, stage=0, between=lambda: more_x(KC, KC + 4))
                    up(0, 0, 1, 0, between=lambda: more_x(KC + 4, KC + 6))
                    more_x(KC + 6, 2 * KC)
                    up(0, 0, 0, 1, stage=1)
                    up(0, 0, 1, 1)
                    ada_reduce(0)
                    down(0, 0, 0)
                else:
                    pe.wait_ge(o_used, 2 * KC)
                    up(1, 0, 0, 0, stage=4)
                    mean(3)
                    up(1, 0, 1, 0, between=lambda: variance(3))
                    spread(3)
                    down(1, 0, 0)
                    up(1, 0, 0, 1, stage=5)
                    up(1, 0, 1, 1)

                def steady(i, ada):
                    up(f, i, 0, 0)
                    up(f, i, 1, 0)
                    down(f, i - 1, 1)
                    up(f, i, 0, 1)
                    up(f, i, 1, 1)
                    down(f, i, 0)
                    if ada:
                        ada_reduce(i)

                if f == 0:
                    with pe.Fori(1, ADA_UNITS) as i:
                        steady(i, True)
                with pe.Fori(ADA_UNITS if f == 0 else 1, ITER - 1) as i:
                    steady(i, False)
                i, s = ITER - 1, 4 * f
                up(f, i, 0, 0)
                up(f, i, 1, 0)
                down(f, i - 1, 1)
                up(f, i, 0, 1)
                down(f, i, 0)
                up(f, i, 1, 1, between=lambda: mean(s))
                down(f, i, 1, 0, 2)
                variance(s)
                down(f, i, 1, 2, 5)
                spread(s)
                down(f, i, 1, 5, KC)

            ffn(0)

            def project(m, stage=None):
                if m < 2:
                    pe.wait_ge(g_ok, 4 * ITER)
                elif m - 2 < OUT0:
                    pe.wait_ge(z_used, m - 1)
                else:
                    pe.wait_ge(o_used, m - 1 - OUT0)
                if m % 2 == 0:
                    pe.wait_ge(wl_ok, MIX0 + m // 2 + 1)
                h = m // NZ if m < OUT0 else (m - OUT0) // KC
                chunk_product(ps[:, m % 2], m // 2 % 2, m % 2, h, stage).then_inc(z_done, 1)

            def v_transposes(h):
                pe.wait_ge(z_used, NZ * h + 2)
                for b in range(4):
                    mm = pe.transpose(ps[:, 4 + 2 * h, b * P:(b + 1) * P], v_tr[:, b * P:(b + 1) * P], ident[:, :])
                mm.then_inc(v_t, 1)

            def scores(n):
                b, kv = n // 2, n % 2
                pe.wait_ge(rope_ok, 5 if n < 8 else 10)
                above(pe, sel_ok, n)
                rows = slice(kv * HEAD, (kv + 1) * HEAD)
                q0 = b % 4 * P
                for c in range(4):
                    out = ps[:, 2 + c // 2, c % 2 * 2 * P:(c % 2 + 1) * 2 * P]
                    k0, out = (0, out[:, P:]) if b == 0 else ((b - 1) * P, out)
                    mm = pe.matmul(out, q_sb[rows, c, q0:q0 + P], k_sb[rows, k0:(b + 1) * P], start=True, stop=True)
                mm.then_inc(sc_done, 1)

            def transposes(n):
                pe.wait_ge(prob_ok, n + 1)
                for c in range(4):
                    mm = pe.transpose(ps[:, 4, c * P:(c + 1) * P], probs[:, c], ident[:, :])
                mm.then_inc(t_done, 1)

            def values(n):
                b = n // 2
                pe.wait_ge(pt_ok, 2 * n + 2)
                pe.wait_ge(v_ok, b // 4 + 1)
                above(pe, yl_ok, n)
                mm = pe.matmul(ps[:, 5], v_sb[:, b], pt[:, 0], start=True, stop=(b == 0))
                if b > 0:
                    mm = pe.matmul(ps[:, 5], v_sb[:, b - 1], pt[:, 1], start=False, stop=True)
                mm.then_inc(pv_done, 1)

            def pool_mix(r):
                pe.wait_ge(diff_ok, r + 1)
                pe.wait_ge(tab_in, 32)
                above(pe, pl_ok, r)
                pe.matmul(ps[:, 7], w_pool[:, r % 4], hid[:, 2 + r % 2, PAD:], start=True, stop=True).then_inc(pool_done, 1)

            project(0, stage=2)
            project(1)
            mean(1)
            for m in range(2, 5):
                project(m)
                if m == 3:
                    v_transposes(0)
            variance(1)
            project(5)
            spread(1)
            for m in range(6, NZ):
                project(m)
            for s in range(NZ):
                if 1 <= s <= 8:
                    transposes(s - 1)
                if s < 8:
                    scores(s)
                project(NZ + s, stage=3 if s == 0 else None)
                if s < 4:
                    pool_mix(s)
                if s == 3:
                    v_transposes(1)
                if 1 <= s <= 8:
                    values(s - 1)
            pe.wait_ge(yl_ok, 8)
            pe.wait_ge(pl_ok, 4)
            project(OUT0)
            for s in range(9):
                if s >= 1:
                    transposes(7 + s)
                if s < 8:
                    scores(8 + s)
                if s < 7:
                    project(OUT0 + 1 + s)
                if s >= 5:
                    pool_mix(s - 1)
                if s >= 1:
                    values(7 + s)
            pe.wait_ge(yl_ok, 16)
            pe.wait_ge(pl_ok, 8)
            for m in range(KC):
                project(OUT0 + KC + m)
                if m == 0:
                    mean(2)
                if m == 2:
                    variance(2)
                if m == 3:
                    spread(2)

            ffn(1)

            def finish(r):
                h, c = r // KC, r % KC
                pe.wait_ge(fin_ok, r + 1)
                above(pe, fin_sb, r - 1)
                for b in range(4):
                    mm = pe.transpose(ps[:, r % 2, b * P:(b + 1) * P], acc[:, c, h * H + b * P:h * H + (b + 1) * P], ident[:, :])
                mm.then_inc(fin_t, 1)
            for r in range(KC):
                finish(r)
            mean(5)
            variance(5)
            spread(5)
            for r in range(KC, 2 * KC):
                finish(r)

        @block.scalar
        def _(act):
            def w_split(n, slot, landed, used):
                if used is not None:
                    act.wait_ge(*used)
                act.wait_ge(raw_in[slot], landed)
                act.activation(w_hi[slot][:, :, :, :], w_raw[slot][:, :, :, :], ACT.Copy).then_inc(wh_ok, 1)

            def w2_split(f, i):
                above(act, f_done, 2 * KC * (ITER * f + i))
                act.wait_ge(w2_in, 16 * (ITER * f + i + 1))
                for j in range(2):
                    act.activation(w2_hi[:, j], w2_raw[:, j], ACT.Copy).then_inc(w2h_ok, 1)

            def silu(f, i, j, h):
                e = 4 * (ITER * f + i) + 2 * h + j
                act.wait_ge(ab_done, 2 * e + 1)
                act.activation(hid[:, j, 0:H], ps[:, 2 * j], ACT.Silu).then_inc(silu_ok, 1)

            def gate_hi(f, i, j, h):
                e = 4 * (ITER * f + i) + 2 * h + j
                act.wait_ge(g_ok, e + 1)
                above(act, f_done, 2 * KC * (ITER * f + i - 1) + KC * h + KC)
                act.activation(g_hi[:, h, j], hid[:, 2 + j, 0:H], ACT.Copy).then_inc(gh_ok, 1)

            def squares(s):
                h = s % 2
                for c in range(KC):
                    act.wait_ge(ln_cent, KC * s + c + 1)
                    if c >= 2:
                        act.wait_ge(sq_used, KC * s + c - 1)
                    act.activation(scratch[:, 1 + c % 2, H:], acc[:, c, tok(h)], ACT.Square).then_inc(ln_sq, 1)

            def input_hi(st, c):
                h, n, cf = st % 2, KC * st + c, C_N * (st // 2)
                act.wait_ge(u32_ok, n + 1)
                if st < 2:
                    act.activation(acc[:, c, tok(h)], ps[:, 4 + (KC * h + c) % 4], ACT.Copy, scale=ALPHA).then_inc(acc_ok, 1)
                else:
                    act.activation(acc[:, c, tok(h)], acc[:, c, tok(h)], ACT.Identity, bias=coef[:, cf + C_AB + c:cf + C_AB + c + 1],
                                   scale=coef[:, cf + C_AG + c:cf + C_AG + c + 1]).then_inc(acc_ok, 1)
                act.activation(u_hi[:, c, tok(h)], new_input(st, c), ACT.Copy).then_inc(uh_ok, 1)

            def finish(r):
                act.wait_ge(fin_t, r + 1)
                above(act, stored[r % 4], 16 * (r // 4))
                act.activation(w_raw[0][:, r % 4 // 2, 4 * (r % 2):4 * (r % 2) + 4], ps[:, r % 2].rearrange("p (b n) -> p b n", b=4),
                               ACT.Copy).then_inc(fin_sb, 1)

            act.dma_start(c_rows[:, :], t["c"].rearrange("a (n p) -> (a n) p", p=P)).then_inc(c_in, 16)
            rows = [(0, 0, t["b_ada"], 72), (0, 72, t["ln1_g"], 8), (0, 80, t["ln1_b"], 8), (0, 88, t["ln2_g"], 8),
                    (0, 96, t["ln2_b"], 8), (0, 104, t["ln3_g"], 8), (0, 112, t["ln3_b"], 8), (0, 120, t["b_out"], 8),
                    (1, 4, t["b_in"][:, 512:IN_W], 6), (1, 10, t["pool_scale"], 4)]
            for r, row, src, n in rows:
                act.dma_start(vec_rows[r][row:row + n, :], src.rearrange("a (n p) -> (a n) p", p=P)).then_inc(vec_in, 16)
            for a in range(2):
                src = t["b_in"][:, a * 256:(a + 1) * 256].rearrange("a (c d) -> (a c) d", d=HEAD)
                act.dma_start(vec_rows[1][0:4, a * HEAD:(a + 1) * HEAD], src).then_inc(vec_in, 16)
            act.dma_start(sinks, t["attn_sinks"].broadcast_to([P, NH])).then_inc(sink_in, 16)
            act.wait_ge(c_tr, 1)
            act.activation(c_act[:, :], ps[:, 3, 0:KC], ACT.Silu).then_inc(cact_ok, 1)
            w_split(0, 0, raw_count(0), None)

            def ffn(f):
                st, s = 4 * f, 4 * f - 1
                last = ITER - 1
                if f == 0:
                    for c in range(KC):
                        input_hi(0, c)
                    w_split(1, 1, raw_count(1), None)
                    for c in range(KC):
                        input_hi(1, c)
                        if c == 3:
                            silu(0, 0, 0, 0)
                            gate_hi(0, 0, 0, 0)
                    w2_split(0, 0)
                else:
                    silu(1, 0, 0, 0)
                    gate_hi(1, 0, 0, 0)
                    w2_split(1, 0)
                    squares(3)
                silu(f, 0, 1, 0)
                gate_hi(f, 0, 1, 0)
                if f == 1:
                    for c in range(KC):
                        input_hi(5, c)

                def half1(i):
                    for j in range(2):
                        silu(f, i, j, 1)
                        gate_hi(f, i, j, 1)
                        w_split(None, j, raw_count(PAIR0[f] + j) + 32 * (i + 1),
                                (ab_done, 8 * (ITER * f + i) + 6 + 2 * j))

                def steady(i):
                    for j in range(2):
                        silu(f, i, j, 0)
                        gate_hi(f, i, j, 0)
                    w2_split(f, i)
                    half1(i)

                half1(0)
                with act.Fori(1, last) as i:
                    steady(i)
                for j in range(2):
                    silu(f, last, j, 0)
                    gate_hi(f, last, j, 0)
                w2_split(f, last)
                silu(f, last, 0, 1)
                gate_hi(f, last, 0, 1)
                if f == 0:
                    w_split(MIX0, 0, raw_count(MIX0), (ab_done, 8 * last + 6))
                squares(4 * f)
                silu(f, last, 1, 1)
                gate_hi(f, last, 1, 1)
                if f == 0:
                    w_split(MIX0 + 1, 1, raw_count(MIX0 + 1), (ab_done, 8 * last + 8))

            ffn(0)

            def next_pair(m):
                n = MIX0 + m // 2 + 2
                w_split(n, n % 2, raw_count(n), (z_done, m + 1))

            def drain(m):
                h = m // NZ
                kind, c = Z_ORDER[h][m % NZ]
                act.wait_ge(z_done, m + 1)
                if kind == Q:
                    if h == 1:
                        act.wait_ge(sc_done, 8)
                    dst = q_sb[:, c]
                elif kind == K:
                    dst = k_sb[:, tok(h)]
                elif kind == V:
                    above(act, v_t, h)
                    dst = v_tr[:, :]
                else:
                    if h == 1:
                        act.wait_ge(carry_ok, c + 1)
                    dst = pool_in[:, c, PAD:]
                col = V_BIN + Z_COL[kind] + c
                act.activation(dst, ps[:, m % 2], ACT.Identity, bias=vec[:, col:col + 1]).then_inc(z_used, 1)

            def v_store(h):
                act.wait_ge(v_t, h + 1)
                act.activation(v_sb[:, 4 * h:4 * h + 4], ps[:, 4 + 2 * h].rearrange("p (b n) -> p b n", b=4), ACT.Copy).then_inc(v_ok, 1)

            def banded(block_of):
                return ps[:, 2:4].rearrange("p b (c k) -> p (b c) k", c=2)[:, :, block_of * P:(block_of + 1) * P]

            def before_scores(n):
                act.wait_ge(sc_done, n + 1)
                if n >= 2:
                    act.activation(probs[:, :, :], banded(0), ACT.Copy).then_inc(prev_ok, 1)

            def exps(n):
                act.wait_ge(sel_ok, n + 1)
                act.wait_ge(neg_ok, n + 1)
                for c in range(4):
                    act.activation(probs[:, c], probs[:, c], ACT.Exp, bias=neg_max[:, c:c + 1], scale=HEAD ** -0.5,
                                   accum_out=row_sum[:, c:c + 1]).then_inc(exp_ok, 1)
                act.wait_ge(sd_ok, n + 1)
                act.activation(sink_exp, sink_sh, ACT.Exp).then_inc(exp_ok, 1)

            def attn_hi(n):
                b, rows = n // 2, slice(n % 2 * HEAD, (n % 2 + 1) * HEAD)
                act.wait_ge(pv_done, n + 1)
                act.activation(u_hi[rows, 0:4, b * P:(b + 1) * P], ps[rows, 5].rearrange("p (c q) -> p c q", c=4), ACT.Copy).then_inc(yh_ok, 1)

            def pool_hi(r):
                h, g = r // 4, r % 4
                act.wait_ge(pool_done, r + 1)
                act.activation(u_hi[:, 4 + g, tok(h)], ps[:, 7], ACT.Copy, scale=vec[:, V_PS + g:V_PS + g + 1]).then_inc(ph_ok, 1)

            for c in range(KC):
                input_hi(2, c)
            drain(0)
            drain(1)
            next_pair(1)
            squares(1)
            drain(2)
            drain(3)
            next_pair(3)
            v_store(0)
            drain(4)
            drain(5)
            next_pair(5)
            drain(6)
            for c in range(KC):
                input_hi(3, c)
                if c == 3:
                    drain(7)
                    next_pair(7)
            drain(8)
            drain(9)
            next_pair(9)
            for s in range(NZ):
                if s < 8:
                    before_scores(s)
                    exps(s)
                drain(NZ + s)
                if s < 4:
                    pool_hi(s)
                if s == 3:
                    v_store(1)
                if 1 <= s <= 8:
                    attn_hi(s - 1)
                if s % 2 == 1:
                    next_pair(NZ + s)
            for s in range(9):
                if s < 8:
                    before_scores(8 + s)
                    exps(8 + s)
                if s < 7 and s % 2 == 0:
                    next_pair(OUT0 + 1 + s)
                if s >= 5:
                    pool_hi(s - 1)
                if s >= 1:
                    attn_hi(7 + s)
            squares(2)
            next_pair(OUT0 + KC + 1)
            next_pair(OUT0 + KC + 3)
            for c in range(KC):
                input_hi(4, c)
                if c == 3:
                    next_pair(OUT0 + KC + 5)
            next_pair(OUT0 + KC + 7)

            ffn(1)
            for r in range(KC):
                finish(r)
            squares(5)
            for r in range(KC, 2 * KC):
                finish(r)

        @block.vector
        def _(dve):
            f = f32

            def w_low(slot, n):
                dve.wait_ge(wh_ok, n + 1)
                dve.tensor_tensor(w_lo[slot][:, :, :, :], w_raw[slot][:, :, :, :], w_hi[slot][:, :, :, :].bitcast(f),
                                  ALU.subtract).then_inc(wl_ok, 1)

            def w2_low(f_, i):
                for j in range(2):
                    dve.wait_ge(w2h_ok, 2 * (ITER * f_ + i) + j + 1)
                    dve.tensor_tensor(w2_lo[:, j], w2_raw[:, j], w2_hi[:, j].bitcast(f), ALU.subtract).then_inc(w2l_ok, 1)

            def gated(f_, i, j, h):
                e = 4 * (ITER * f_ + i) + 2 * h + j
                dve.wait_ge(silu_ok, e + 1)
                dve.wait_ge(ab_done, 2 * e + 2)
                above(dve, gl_ok, e - 1)
                dve.tensor_tensor(hid[:, 2 + j, 0:H], hid[:, j, 0:H], ps[:, 2 * j + 1], ALU.mult).then_inc(g_ok, 1)
                dve.wait_ge(gh_ok, e + 1)
                dve.tensor_tensor(g_lo[:, h, j], hid[:, 2 + j, 0:H], g_hi[:, h, j].bitcast(f), ALU.subtract).then_inc(gl_ok, 1)

            def residual(f_, i, h, d0=0, d1=KC):
                cf = C_N * (0 if f_ == 0 else 2) + C_GATE
                for d in range(d0, d1):
                    q = 2 * KC * (ITER * f_ + i) + KC * h + d
                    dve.wait_ge(f_done, q + 1)
                    above(dve, f_used, q + 1 - KC)
                    dve.scalar_tensor_tensor(acc[:, d, tok(h)], ps[:, 4 + d % 2], coef[:, cf + d:cf + d + 1], acc[:, d, tok(h)],
                                             ALU.mult, ALU.add).then_inc(f_used, 1)

            def ada_step(i, k):
                dve.wait_ge(ada_tile[k % 2], 16 * (4 * i + k // 2 + 1))
                if k == 0:
                    above(dve, ada_red, i)
                    dve.tensor_scalar(scratch[:, 2], scratch[:, k % 2], c_act[:, k:k + 1], None, ALU.mult).then_inc(ada_acc, 1)
                else:
                    dve.wait_ge(ada_acc, KC * i + k)
                    dve.scalar_tensor_tensor(scratch[:, 2], scratch[:, k % 2], c_act[:, k:k + 1], scratch[:, 2],
                                             ALU.mult, ALU.add).then_inc(ada_acc, 1)

            def ada_store(i):
                dve.wait_ge(ada_red, i + 1)
                cols = bass.ds(i * KC + ADA_EARLY * KC, KC)
                dve.tensor_tensor(mods[:, cols], ps[:, 6, 0:KC], vec[:, cols], ALU.add).then_inc(mod_ok, 1)

            chain = [0]

            def coef_op(what, *args):
                what(*args).then_inc(coef_ok, 1)
                chain[0] += 1
                dve.wait_ge(coef_ok, chain[0])

            def coefs(st):
                cf = C_N * st
                sh, sc, gt = (mods[:, (3 * st + v) * KC:(3 * st + v + 1) * KC] for v in range(3))
                a, b, ag, ab, gate = (coef[:, cf + x:cf + x + KC] for x in (C_A, C_B, C_AG, C_AB, C_GATE))
                g, beta = (vec[:, V_LN + (2 * (st - 1) + v) * KC:V_LN + (2 * (st - 1) + v + 1) * KC] for v in range(2))
                coef_op(dve.tensor_scalar, a, sc, 1.0, None, ALU.add)
                coef_op(dve.tensor_tensor, b, beta, a, ALU.mult)
                coef_op(dve.tensor_tensor, b, b, sh, ALU.add)
                coef_op(dve.tensor_tensor, a, a, g, ALU.mult)
                coef_op(dve.tensor_scalar, gate, gt, 1.0, None, ALU.add)
                coef_op(dve.tensor_scalar, ag, g, ALPHA, None, ALU.mult)
                coef_op(dve.tensor_scalar, ab, beta, ALPHA, None, ALU.mult)
                if st == 1:
                    bias = vec[:, V_BOUT:V_BOUT + KC]
                    coef_op(dve.tensor_tensor, small[:, 56:64], gate, bias, ALU.mult)
                    coef_op(dve.tensor_tensor, ab, ab, small[:, 56:64], ALU.add)
                else:
                    coef_op(dve.tensor_scalar, gate, gate, 0.5, None, ALU.mult)

            def total(s):
                h = s % 2
                dve.tensor_reduce(scratch[:, 0, 0:H], acc[:, :, tok(h)].rearrange("p c n -> p n c"), AX.X, ALU.add).then_inc(ln_sum, 1)

            def centre(s):
                h = s % 2
                dve.wait_ge(ln_mean, s + 1)
                sq_sum = scratch[:, 0, H:]

                def add_square(c):
                    dve.wait_ge(ln_sq, KC * s + c + 1)
                    sq = scratch[:, 1 + c % 2, H:]
                    if c == 0:
                        dve.tensor_copy(sq_sum, sq).then_inc(sq_used, 1)
                    else:
                        dve.wait_ge(sq_used, KC * s + c)
                        dve.tensor_tensor(sq_sum, sq_sum, sq, ALU.add).then_inc(sq_used, 1)

                for c in range(KC):
                    dve.tensor_tensor(acc[:, c, tok(h)], acc[:, c, tok(h)], ps[:, 6], ALU.subtract).then_inc(ln_cent, 1)
                    if c >= 2:
                        add_square(c - 2)
                add_square(KC - 2)
                add_square(KC - 1)

            def deviation(s):
                dve.wait_ge(ln_var, s + 1)
                dve.tensor_scalar(var_eps, ps[:, 7, 0:4], EPS, None, ALU.add).then_inc(ln_veps, 1)

            def diagonal(s):
                dve.wait_ge(ln_rstd, s + 1)
                dve.tensor_tensor(scratch[:, 1, 0:H].rearrange("p (b n) -> p b n", b=4),
                                  ident[:, :].unsqueeze(1).broadcast_to([P, 4, P]),
                                  rstd.unsqueeze(2).broadcast_to([P, 4, P]), ALU.mult).then_inc(ln_diag, 1)

            def input_chunks(st, c0=0, c1=KC, tail=True):
                h, cf = st % 2, C_N * (st // 2)

                def low(c):
                    dve.wait_ge(uh_ok, KC * st + c + 1)
                    dve.tensor_tensor(u_lo[:, c, tok(h)], new_input(st, c), u_hi[:, c, tok(h)].bitcast(f),
                                      ALU.subtract).then_inc(ul_ok, 1)

                for c in range(c0, c1):
                    a, b = (coef[:, cf + x + c:cf + x + c + 1] for x in (C_A, C_B))
                    if st < 2:
                        dve.wait_ge(x_tr, KC * st + c + 1)
                        src = ps[:, 4 + (KC * h + c) % 4]
                    else:
                        s = st - 2
                        if c == 0:
                            dve.wait_ge(ln_bc, s + 1)
                        src = acc[:, c, tok(h)]
                        dve.tensor_tensor(src, src, ps[:, 7], ALU.mult).then_inc(ln_t, 1)
                        dve.wait_ge(ln_t, KC * s + c + 1)
                    above(dve, ul_ok, KC * st + c - 1)
                    dve.tensor_scalar(new_input(st, c), src, a, b, ALU.mult, ALU.add).then_inc(u32_ok, 1)
                    if c >= 1:
                        low(c - 1)
                if c1 == KC:
                    low(KC - 1)

            dve.wait_ge(cact_ok, 1)
            for v in (1, 0):
                for k in range(KC):
                    dve.wait_ge(ada_in[v * KC + k], 16)
                    if k == 0:
                        dve.tensor_scalar(acc[:, v], ada_sb[v][:, k], c_act[:, k:k + 1], None, ALU.mult).then_inc(early_acc[v], 1)
                    else:
                        dve.wait_ge(early_acc[v], k)
                        dve.scalar_tensor_tensor(acc[:, v], ada_sb[v][:, k], c_act[:, k:k + 1], acc[:, v],
                                                 ALU.mult, ALU.add).then_inc(early_acc[v], 1)
            dve.wait_ge(vec_t, 2)
            dve.tensor_copy(vec[:, :], ps[:, 2, 0:NV]).then_inc(vec_ok, 1)
            dve.wait_ge(sink_in, 16)
            dve.tensor_scalar(neg_sinks, sinks, -1.0, None, ALU.mult).then_inc(sink_ok, 1)
            dve.wait_ge(vec_ok, 1)
            dve.wait_ge(mod0_ps, 1)
            dve.tensor_tensor(mods[:, 0:2 * KC], ps[:, 3, 0:2 * KC], vec[:, 0:2 * KC], ALU.add).then_inc(mod_ok, 1)
            dve.wait_ge(mod_ok, 1)
            coef_op(dve.tensor_scalar, coef[:, C_A:C_A + KC], mods[:, KC:2 * KC], 1.0, None, ALU.add)
            coef_op(dve.tensor_copy, coef[:, C_B:C_B + KC], mods[:, 0:KC])

            def ffn(f_):
                last = ITER - 1
                if f_ == 0:
                    input_chunks(0, 0, 1)
                    w_low(0, 0)
                    input_chunks(0, 1, KC)
                    w_low(1, 1)
                    input_chunks(1, 0, 4)
                    gated(0, 0, 0, 0)
                    input_chunks(1, 4, KC)
                    gated(0, 0, 1, 0)
                    for k in range(4):
                        ada_step(0, k)
                    w2_low(0, 0)
                    gated(0, 0, 0, 1)
                    for k in range(4, 6):
                        ada_step(0, k)
                    w_low(0, 2)
                    for k in range(6, KC):
                        ada_step(0, k)
                    gated(0, 0, 1, 1)
                    ada_store(0)
                    dve.wait_ge(mod_ok, 2)
                    coef_op(dve.tensor_scalar, coef[:, C_GATE:C_GATE + KC], mods[:, 2 * KC:3 * KC], 1.0, None, ALU.add)
                    coef_op(dve.tensor_scalar, coef[:, C_GATE:C_GATE + KC], coef[:, C_GATE:C_GATE + KC], 0.5, None, ALU.mult)
                else:
                    total(3)
                    gated(1, 0, 0, 0)
                    w2_low(1, 0)
                    centre(3)
                    deviation(3)
                    diagonal(3)
                    gated(1, 0, 1, 0)
                    input_chunks(5)
                    residual(1, 0, 0)

                def half1(i, ada=False):
                    gated(f_, i, 0, 1)
                    w_low(0, PAIR0[f_] + 2 * i + 2)
                    if ada:
                        for k in range(6, KC):
                            ada_step(i, k)
                    gated(f_, i, 1, 1)
                    if f_ == 0 or not isinstance(i, int):
                        residual(f_, i, 0)
                    w_low(1, PAIR0[f_] + 2 * i + 3)

                if f_ == 0:
                    residual(0, 0, 0)
                    w_low(1, 3)
                else:
                    half1(0)

                def steady(i, ada):
                    gated(f_, i, 0, 0)
                    if ada:
                        for k in range(0, 3):
                            ada_step(i, k)
                    gated(f_, i, 1, 0)
                    residual(f_, i - 1, 1)
                    w2_low(f_, i)
                    if ada:
                        for k in range(3, 6):
                            ada_step(i, k)
                    half1(i, ada)
                    if ada:
                        ada_store(i)

                if f_ == 0:
                    with dve.Fori(1, ADA_UNITS) as i:
                        steady(i, True)
                    dve.wait_ge(mod_ok, 1 + ADA_UNITS)
                    coefs(1)
                    coefs(2)
                with dve.Fori(ADA_UNITS if f_ == 0 else 1, last) as i:
                    steady(i, False)
                s = 4 * f_
                gated(f_, last, 0, 0)
                gated(f_, last, 1, 0)
                residual(f_, last - 1, 1)
                w2_low(f_, last)
                gated(f_, last, 0, 1)
                if f_ == 0:
                    w_low(0, MIX0)
                residual(f_, last, 0)
                dve.wait_ge(f_used, 2 * KC * (ITER * f_ + last) + KC)
                total(s)
                centre(s)
                gated(f_, last, 1, 1)
                residual(f_, last, 1, 0, 2)
                deviation(s)
                diagonal(s)
                residual(f_, last, 1, 2, 5)
                if f_ == 0:
                    w_low(1, MIX0 + 1)
                    input_chunks(2, 0, 3)
                    residual(0, last, 1, 5, KC)
                    input_chunks(2, 3, KC)
                else:
                    last_chunks(0, 0, 3)
                    residual(1, last, 1, 5, KC)
                    last_chunks(0, 3, KC)

            def last_chunks(h, c0, c1):
                s = 4 + h
                for c in range(c0, c1):
                    if c == 0:
                        dve.wait_ge(ln_bc, s + 1)
                    g, b = (vec[:, V_LN + (4 + v) * KC + c:V_LN + (4 + v) * KC + c + 1] for v in range(2))
                    src = acc[:, c, tok(h)]
                    dve.tensor_tensor(src, src, ps[:, 7], ALU.mult).then_inc(ln_t, 1)
                    dve.wait_ge(ln_t, KC * s + c + 1)
                    dve.tensor_scalar(src, src, g, b, ALU.mult, ALU.add).then_inc(fin_ok, 1)

            ffn(0)

            def rotate(r, x):
                h = r // 5
                dve.wait_ge(rope_in, 32 * (h + 1))
                tmp = hid[:, r % 2, 0:H]
                above(dve, rope_ok, r - 1)
                half = HEAD // 8
                swap = [i + half for i in range(half)] + list(range(half)) + list(range(2 * half, 32))
                dve.stream_shuffle(in_=x, out=tmp, mask=swap).then_inc(shuf_ok, 1)
                dve.wait_ge(shuf_ok, r + 1)
                dve.tensor_tensor(tmp, tmp, rope[:, 1], ALU.mult).then_inc(rope_s, 1)
                dve.tensor_tensor(x, x, rope[:, 0], ALU.mult).then_inc(rope_c, 1)
                dve.wait_ge(rope_s, r + 1)
                dve.wait_ge(rope_c, r + 1)
                dve.tensor_tensor(x, x, tmp, ALU.add).then_inc(rope_ok, 1)

            def rotate_unit(m):
                h = m // NZ
                kind, c = Z_ORDER[h][m % NZ]
                dve.wait_ge(z_used, m + 1)
                rotate(5 * h + (0 if kind == K else 1 + c), k_sb[:, tok(h)] if kind == K else q_sb[:, c])

            wins = [0]

            def windows(r):
                h, g = r // 4, r % 4
                unit = NZ * h + Z_ORDER[h].index((PL, g))
                dve.wait_ge(z_used, unit + 1)
                x = pool_in[:, g]
                n, src = 1, x
                steps = g + 1
                order = [3 - r % 2 if (steps - 1 - q) % 2 == 0 else 2 + r % 2 for q in range(steps)]
                above(dve, pool_done, r)
                for q in range(steps):
                    dst = hid[:, order[q]]
                    lo = 2 * n - 1
                    dve.tensor_tensor(dst[:, lo:], src[:, lo:], src[:, lo - n:PAD + H - n], ALU.add).then_inc(win_ok, 1)
                    wins[0] += 1
                    dve.wait_ge(win_ok, wins[0])
                    src, n = dst, 2 * n
                out = hid[:, 2 + r % 2]
                first = PAD if h == 0 else 0
                if h == 0:
                    dve.wait_ge(tab_in, 32)
                    dve.tensor_tensor(out[:, PAD:2 * PAD], src[:, PAD:2 * PAD], inv_cnt[:, g], ALU.mult).then_inc(win_ok, 1)
                    wins[0] += 1
                    dve.wait_ge(win_ok, wins[0])
                    dve.tensor_tensor(out[:, PAD:2 * PAD], out[:, PAD:2 * PAD], x[:, PAD:2 * PAD], ALU.subtract).then_inc(win_ok, 1)
                    wins[0] += 1
                dve.scalar_tensor_tensor(out[:, PAD + first:], src[:, PAD + first:], 1.0 / WIN[g], x[:, PAD + first:],
                                         ALU.mult, ALU.subtract).then_inc(diff_ok, 1)
                if h == 0:
                    dve.wait_ge(diff_ok, r + 1)
                    dve.tensor_copy(x[:, 0:PAD], x[:, H:H + PAD]).then_inc(carry_ok, 1)

            def pool_low(r):
                h, g = r // 4, r % 4
                dve.wait_ge(ph_ok, r + 1)
                dve.scalar_tensor_tensor(u_lo[:, 4 + g, tok(h)], ps[:, 7], vec[:, V_PS + g:V_PS + g + 1],
                                         u_hi[:, 4 + g, tok(h)].bitcast(f), ALU.mult, ALU.subtract).then_inc(pl_ok, 1)

            def softmax(n):
                kv = n % 2
                own = ps[:, 2:4].rearrange("p b (c k) -> p (b c) k", c=2)[:, :, P:2 * P]
                dve.wait_ge(sc_done, n + 1)
                if n < 2:
                    dve.memset(probs[:, :, :], -1e30).then_inc(prev_ok, 1)
                dve.wait_ge(prev_ok, n + 1)
                dve.copy_predicated(out=probs[:, :, :], mask=own_mask[:, :].bitcast(u32).unsqueeze(1).broadcast_to([P, 4, P]),
                                    data=own).then_inc(sel_ok, 1)
                dve.wait_ge(sel_ok, n + 1)
                dve.tensor_reduce(row_max, probs[:, :, :], AX.X, ALU.max).then_inc(max_ok, 1)
                dve.wait_ge(max_ok, n + 1)
                dve.scalar_tensor_tensor(neg_max, row_max, -HEAD ** -0.5, neg_sinks[:, 4 * kv:4 * kv + 4],
                                         ALU.mult, ALU.min).then_inc(neg_ok, 1)
                dve.wait_ge(neg_ok, n + 1)
                dve.tensor_tensor(sink_sh, neg_max, sinks[:, 4 * kv:4 * kv + 4], ALU.add).then_inc(sd_ok, 1)

            def normalise(n):
                dve.wait_ge(exp_ok, 5 * (n + 1))
                dve.tensor_tensor(denom, row_sum, sink_exp, ALU.add).then_inc(den_ok, 1)
                dve.wait_ge(den_ok, n + 1)
                dve.reciprocal(recip, denom).then_inc(rec_ok, 1)
                dve.wait_ge(rec_ok, n + 1)
                dve.tensor_tensor(probs[:, :, :], probs[:, :, :], recip.unsqueeze(2).broadcast_to([P, 4, P]),
                                  ALU.mult).then_inc(prob_ok, 1)

            def masked_t(n):
                dve.wait_ge(t_done, n + 1)
                above(dve, pv_done, n)
                for a in range(2):
                    dve.tensor_tensor(pt[:, a], ps[:, 4].rearrange("p (c q) -> p c q", c=4),
                                      own_t[:, a].unsqueeze(1).broadcast_to([P, 4, P]), ALU.mult).then_inc(pt_ok, 1)

            def attn_low(n):
                b, rows = n // 2, slice(n % 2 * HEAD, (n % 2 + 1) * HEAD)
                dve.wait_ge(yh_ok, n + 1)
                dve.tensor_tensor(u_lo[rows, 0:4, b * P:(b + 1) * P], ps[rows, 5].rearrange("p (c q) -> p c q", c=4),
                                  u_hi[rows, 0:4, b * P:(b + 1) * P].bitcast(f), ALU.subtract).then_inc(yl_ok, 1)

            def out_residual(m):
                d, h = (m - OUT0) % KC, (m - OUT0) // KC
                dve.wait_ge(z_done, m + 1)
                dve.scalar_tensor_tensor(acc[:, d, tok(h)], ps[:, m % 2], coef[:, C_N + C_GATE + d:C_N + C_GATE + d + 1],
                                         acc[:, d, tok(h)], ALU.mult, ALU.add).then_inc(o_used, 1)

            def next_pair(m):
                n = MIX0 + m // 2 + 2
                w_low(n % 2, n)

            dve.wait_ge(f_used, 2 * KC * ITER)
            total(1)
            dve.memset(pool_in[:, :, 0:PAD], 0.0).then_inc(pad_ok, 1)
            next_pair(1)
            centre(1)
            next_pair(3)
            rotate_unit(0)
            deviation(1)
            rotate_unit(2)
            diagonal(1)
            rotate_unit(3)
            next_pair(5)
            input_chunks(3, 0, 4)
            rotate_unit(4)
            next_pair(7)
            input_chunks(3, 4, KC)
            rotate_unit(5)
            dve.wait_ge(sink_ok, 1)
            dve.wait_ge(mask_ok, 5)
            dve.wait_ge(pad_ok, 1)
            windows(0)
            next_pair(9)
            for s in range(NZ):
                if 1 <= s <= 8:
                    masked_t(s - 1)
                if s < 8:
                    softmax(s)
                    normalise(s)
                if s < 4:
                    pool_low(s)
                if s < 3:
                    windows(s + 1)
                if s == 1:
                    rotate_unit(NZ)
                if s >= 7:
                    rotate_unit(NZ + s - 1)
                if 1 <= s <= 8:
                    attn_low(s - 1)
                if s % 2 == 1:
                    next_pair(NZ + s)
            rotate_unit(2 * NZ - 1)
            for s in range(9):
                if s < 1:
                    windows(4)
                if s >= 1:
                    masked_t(7 + s)
                if s < 8:
                    softmax(8 + s)
                    normalise(8 + s)
                if s < 8:
                    out_residual(OUT0 + s)
                if s < 7 and s % 2 == 0:
                    next_pair(OUT0 + 1 + s)
                if s >= 5:
                    pool_low(s - 1)
                    if s < 8:
                        windows(s)
                if s >= 1:
                    attn_low(7 + s)
            dve.wait_ge(o_used, KC)
            total(2)
            out_residual(OUT0 + KC)
            centre(2)
            out_residual(OUT0 + KC + 1)
            next_pair(OUT0 + KC + 1)
            out_residual(OUT0 + KC + 2)
            deviation(2)
            diagonal(2)
            out_residual(OUT0 + KC + 3)
            next_pair(OUT0 + KC + 3)
            input_chunks(4, 0, 3)
            out_residual(OUT0 + KC + 4)
            input_chunks(4, 3, 6)
            out_residual(OUT0 + KC + 5)
            next_pair(OUT0 + KC + 5)
            input_chunks(4, 6, KC)
            out_residual(OUT0 + KC + 6)
            out_residual(OUT0 + KC + 7)
            next_pair(OUT0 + KC + 7)
            dve.wait_ge(o_used, 2 * KC)

            ffn(1)
            dve.wait_ge(f_used, 4 * KC * ITER)
            total(5)
            centre(5)
            deviation(5)
            diagonal(5)
            last_chunks(1, 0, KC)


_PARAMS = ["w_ada", "b_ada", "ffn1_w1", "ffn1_w3", "ffn1_w2", "ln1_g", "ln1_b", "w_in", "b_in", "attn_sinks", "w_pool",
           "pool_scale", "w_out", "b_out", "ln2_g", "ln2_b", "ffn2_w1", "ffn2_w3", "ffn2_w2", "ln3_g", "ln3_b"]


def _tables():
    import numpy as np
    rot = HEAD // 4
    freq = (500000.0 ** (-np.arange(0, rot, 2, dtype=np.float64) / rot)).astype(np.float32)
    ang = (np.arange(S, dtype=np.float32)[None, :] * freq[:, None]).astype(np.float64)
    cos, sin = np.ones((P, S), np.float32), np.zeros((P, S), np.float32)
    for base in (0, HEAD):
        for sign, at in ((-1.0, 0), (1.0, rot // 2)):
            cos[base + at:base + at + rot // 2] = np.cos(ang)
            sin[base + at:base + at + rot // 2] = sign * np.sin(ang)
    cnt = np.stack([1.0 / np.minimum(np.arange(PAD) + 1, w) for w in WIN])
    return {"rope_cos": cos, "rope_sin": sin,
            "inv_count": np.ascontiguousarray(np.broadcast_to(cnt[None], (P, 4, PAD))).astype(np.float32)}


def kernel(**inputs):
    import numpy as np
    import concourse.bacc as bacc
    from concourse.bass_utils import run_bass_kernel_spmd

    nc = bacc.Bacc("TRN2", target_bir_lowering=False, num_devices=1)
    arrays = {"x": np.ascontiguousarray(inputs["x"]).reshape(S, D), "c": np.ascontiguousarray(inputs["c"])}
    for name in _PARAMS:
        a = np.ascontiguousarray(inputs[name])
        arrays[name] = a if a.ndim == 2 else a.reshape(a.shape[1:])
    arrays.update(_tables())
    t = {name: nc.dram_tensor(name, a.shape, mybir.dt.from_np(a.dtype), kind="ExternalInput").ap() for name, a in arrays.items()}
    out = nc.dram_tensor("out", (S, D), mybir.dt.float32, kind="ExternalOutput").ap()
    layer(nc, t, out)
    r = run_bass_kernel_spmd(nc, [arrays], core_ids=[0])
    return r.results[0]["out"].reshape(1, S, D)
```

```python
import concourse.bass as bass
from concourse import mybir
from contextlib import ExitStack

P = 128
D = 1024
S = 1024
H = 512
KC = D // P
FF = 2816
ITER = FF // (2 * P)
HEAD = 64
NH = 8
WIN = (2, 4, 8, 16)
PAD = 16
ALPHA = 2.0 ** 0.25
EPS = 1e-5
NVEC = 9
IN_W = 1280
IN_PAIRS = 5
OUT_PAIRS = 4
PAIR0 = (0, 2 * ITER + 2 * IN_PAIRS + 2 * OUT_PAIRS)
MIX0 = 2 * ITER
ADA_EARLY = 2
ADA_UNITS = NVEC - ADA_EARLY

V_BADA, V_LN, V_BOUT, V_BIN, V_PS = 0, 72, 120, 128, 138
NV = 142
C_A, C_B, C_AG, C_AB, C_GATE, C_N = 0, 8, 16, 24, 32, 40

Q, K, V, PL = "q", "k", "v", "p"
Z_ORDER = ([(K, 0), (V, 0), (Q, 0), (Q, 1), (Q, 2), (Q, 3), (PL, 0), (PL, 1), (PL, 2), (PL, 3)],
           [(K, 0), (V, 0), (PL, 0), (PL, 1), (PL, 2), (PL, 3), (Q, 0), (Q, 1), (Q, 2), (Q, 3)])
Z_COL = {Q: 0, K: 4, V: 5, PL: 6}
Z_DMAS = {Q: 2, K: 1, V: 1, PL: 1}
NZ = 10
OUT0 = 2 * NZ
OUT_DMAS = 3


def pair_dmas(n):
    if n < MIX0 or n >= PAIR0[1]:
        return 2
    m = 2 * (n - MIX0)
    if m < OUT0:
        return sum(Z_DMAS[Z_ORDER[m // NZ][m % NZ + j][0]] for j in range(2))
    return 2 * OUT_DMAS


def raw_count(n):
    return 16 * sum(pair_dmas(x) for x in range(n % 2, n + 1, 2))


def win_count(r):
    return sum(q % 4 + 1 for q in range(r + 1))


POOL_SLOT = {1: 0, 2: 1, 3: 2, 4: 3, NZ + 1: 4, NZ + 3: 5, NZ + 5: 6, NZ + 7: 7}
OUT_SLOT = {NZ + x: m for m, x in enumerate((0, 1, 2, 3, 5, 6, 7, 8))}
SLOTS = NZ + 9
GROUP_SLOT = {x: x if x < 8 else x - 2 for x in list(range(8)) + list(range(NZ, NZ + 8))}


def sum_count(s):
    return (KC - 1) * (s + 1) if s < 1 else (KC - 1) * s + 1


def above(eng, sem, n):
    if not isinstance(n, int) or n > 0:
        eng.wait_ge(sem, n)


def layer(nc, t, o_out):
    f32, f32r, u32 = mybir.dt.float32, mybir.dt.float32r, mybir.dt.uint32
    ALU, ACT, AX = mybir.AluOpType, mybir.ActivationFunctionType, mybir.AxisListType
    cur = [(nc.sbuf_base + 31) // 32 * 32]

    def at(name, shape, dtype, offset=None):
        size = 4
        for x in shape[1:]:
            size *= x
        if offset is None:
            offset = cur[0]
            cur[0] += (size + 31) // 32 * 32
        return nc.alloc_sbuf_tensor_at(name, shape, dtype, offset=offset)

    u_at = cur[0]
    u_hi = at("u_hi", [P, KC, S], f32r)
    u_lo = at("u_lo", [P, KC, S], f32r)
    acc = at("acc", [P, KC, S], f32)
    w_raw = [at(f"w_raw{s}", [P, 2, KC, P], f32) for s in range(2)]
    w_hi = [at(f"w_hi{s}", [P, 2, KC, P], f32r) for s in range(2)]
    w_lo = [at(f"w_lo{s}", [P, 2, KC, P], f32r) for s in range(2)]
    hid = at("hid", [P, 4, PAD + H], f32)
    scratch = at("scratch", [P, 3, D], f32)
    ident = at("ident", [P, P], f32)
    ones = at("ones", [P, P], f32)
    mean_w = at("mean_w", [P, P], f32)
    vec = at("vec", [P, NV], f32)
    mods = at("mods", [P, NVEC * KC], f32)
    coef = at("coef", [P, 4 * C_N], f32)
    c_act = at("c_act", [P, KC], f32)
    small = at("small", [P, 64], f32)
    half_pow = small[:, 0:4]
    var_eps = small[:, 4:8]
    rstd = small[:, 8:12]
    row_max, neg_max, sink_sh, sink_exp = (small[:, 12 + 4 * i:16 + 4 * i] for i in range(4))
    row_sum, denom, recip = (small[:, 28 + 4 * i:32 + 4 * i] for i in range(3))
    sinks, neg_sinks = small[:, 40:48], small[:, 48:56]
    over = cur[0]
    g_hi = at("g_hi", [P, 2, 2, H], f32r)
    g_lo = at("g_lo", [P, 2, 2, H], f32r)
    w2_hi = at("w2_hi", [P, 2, D], f32r)
    w2_lo = at("w2_lo", [P, 2, D], f32r)
    w2_raw = at("w2_raw", [P, 2, D], f32)
    assert cur[0] <= nc.sbuf_usable_end, (cur[0], nc.sbuf_usable_end)
    x_nat = at("x_nat", [P, S // P, D], f32, over)
    ada_sb = [at(f"ada{v}", [P, KC, D], f32, u_at + v * KC * S * 4) for v in range(ADA_EARLY)]
    x_u32 = at("x_u32", [P, 2, H], f32, over + 4096)
    vec_rows = [at(f"vec_rows{r}", [P, P], f32, cur[0] - 8192 + 512 * r) for r in range(2)]
    c_rows = at("c_rows", [KC, P], f32, cur[0] - 8192 + 1024)
    ffn_end = cur[0]
    cur[0] = over
    q_sb = at("q_sb", [P, 4, H], f32)
    k_sb = at("k_sb", [P, S], f32)
    v_sb = at("v_sb", [P, S // P, P], f32)
    v_tr = hid[:, 1, 0:H]
    rope = at("rope", [P, 2, H], f32)
    probs = at("probs", [P, 2, 4, P], f32)
    pt = at("pt", [P, 2, 4, P], f32)
    pool_in = at("pool_in", [P, 4, PAD + H], f32)
    w_pool = at("w_pool", [P, 4, P], f32)
    own_mask = at("own_mask", [P, P], f32)
    own_t = at("own_t", [P, 2, P], f32)
    inv_cnt = at("inv_cnt", [P, 4, PAD], f32)
    assert cur[0] <= nc.sbuf_usable_end, (cur[0], nc.sbuf_usable_end)

    ctx = ExitStack()
    with ctx:
        ps = ctx.enter_context(nc.psum_tensor("ps", [P, 8, H], f32))

        def sem(name):
            return ctx.enter_context(nc.semaphore(name))

        c_in, c_tr, vec_in, x_in1 = sem("c_in"), sem("c_tr"), sem("vec_in"), sem("x_in1")
        x_in0 = [sem("x_in00"), sem("x_in01")]
        ada_in = [sem(f"ada_in{i}") for i in range(ADA_EARLY * KC)]
        early_acc = [sem(f"early_acc{v}") for v in range(ADA_EARLY)]
        const_ok, small_ok = sem("const_ok"), sem("small_ok")
        vec_t, vec_ok, cact_ok = sem("vec_t"), sem("vec_ok"), sem("cact_ok")
        mod0_ps, mod_ok, coef_ok = sem("mod0_ps"), sem("mod_ok"), sem("coef_ok")
        x_tr = sem("x_tr")
        raw_in = [sem("raw_in0"), sem("raw_in1")]
        wh_ok, wl_ok = sem("wh_ok"), sem("wl_ok")
        w2_in, w2h_ok, w2l_ok = sem("w2_in"), sem("w2h_ok"), sem("w2l_ok")
        ab_done, silu_ok, g_ok, gh_ok, gl_ok = (sem(n) for n in ("ab_done", "silu_ok", "g_ok", "gh_ok", "gl_ok"))
        f_done, f_used = sem("f_done"), sem("f_used")
        ada_tile = [sem("ada_tile0"), sem("ada_tile1")]
        ada_acc, ada_red = sem("ada_acc"), sem("ada_red")
        ln_sum, ln_mean, ln_cent, ln_sq, sq_used = (sem(n) for n in ("ln_sum", "ln_mean", "ln_cent", "ln_sq", "sq_used"))
        ln_var, ln_veps, ln_rstd, ln_diag, ln_bc, ln_t = (sem(n) for n in ("ln_var", "ln_veps", "ln_rstd", "ln_diag", "ln_bc", "ln_t"))
        u32_ok, uh_ok, ul_ok, acc_ok = (sem(n) for n in ("u32_ok", "uh_ok", "ul_ok", "acc_ok"))
        z_done, z_used, o_used = sem("z_done"), sem("z_used"), sem("o_used")
        sink_in, tab_in, rope_in, mask_ok, sink_ok = sem("sink_in"), sem("tab_in"), sem("rope_in"), sem("mask_ok"), sem("sink_ok")
        shuf_ok, rope_s, rope_c, rope_ok = sem("shuf_ok"), sem("rope_s"), sem("rope_c"), sem("rope_ok")
        v_t, v_ok = sem("v_t"), sem("v_ok")
        win_ok, short_ok, diff_ok, carry_ok = sem("win_ok"), sem("short_ok"), sem("diff_ok"), sem("carry_ok")
        pool_done, ph_ok, pl_ok = sem("pool_done"), sem("ph_ok"), sem("pl_ok")
        sc_done, prev_ok, sel_ok, max_ok, neg_ok, sd_ok = (sem(n) for n in ("sc_done", "prev_ok", "sel_ok", "max_ok", "neg_ok", "sd_ok"))
        exp_ok, den_ok, rec_ok, prob_ok = sem("exp_ok"), sem("den_ok"), sem("rec_ok"), sem("prob_ok")
        t_done, pt_ok, pv_done, yh_ok, yl_ok = (sem(n) for n in ("t_done", "pt_ok", "pv_done", "yh_ok", "yl_ok"))
        fin_ok, fin_t = sem("fin_ok"), sem("fin_t")
        fin_sb = [sem("fin_sb0"), sem("fin_sb1")]
        stored = [sem(f"stored{i}") for i in range(4)]

        def tok(h):
            return slice(h * H, (h + 1) * H)

        def new_input(st, c):
            if st == 0:
                return acc[:, c, tok(1)]
            return x_u32[:, c % 2] if st == 1 else scratch[:, 1 + c % 2, 0:H]

        w1 = (t["ffn1_w1"], t["ffn2_w1"])
        w3 = (t["ffn1_w3"], t["ffn2_w3"])
        w2 = (t["ffn1_w2"], t["ffn2_w2"])

        def load_ffn_pair(sp, f, i, j):
            for a, w in enumerate((w1[f], w3[f])):
                src = w.rearrange("(k p) n -> p k n", p=P)[:, :, bass.ds(i * (2 * P) + j * P, P)]
                sp.dma_start(w_raw[j][:, a], src).then_inc(raw_in[j], 16)

        def load_w2(sp, f, i):
            src = w2[f].rearrange("(m j p) n -> m p j n", p=P, j=2)[bass.ds(i, 1)]
            sp.dma_start(w2_raw[:, :, :], src.rearrange("m p j n -> (m p) j n")).then_inc(w2_in, 16)

        def load_mix_pair(sp, n):
            for j in range(2):
                m = 2 * (n - MIX0) + j
                dst = w_raw[n % 2][:, j]
                if m < OUT0:
                    kind, c = Z_ORDER[m // NZ][m % NZ]
                    src = t["w_in"].rearrange("(k p) n -> p k n", p=P)
                    if kind == Q:
                        for a in range(2):
                            col = (4 * a + c) * HEAD
                            sp.dma_start(dst[:, :, a * HEAD:(a + 1) * HEAD], src[:, :, col:col + HEAD]).then_inc(raw_in[n % 2], 16)
                    else:
                        col = (Z_COL[kind] + c) * P
                        sp.dma_start(dst, src[:, :, col:col + P]).then_inc(raw_in[n % 2], 16)
                else:
                    col = (m - OUT0) % KC * P
                    wo = t["w_out"][:, col:col + P]
                    for a in range(2):
                        src = wo[a * 4 * HEAD:(a + 1) * 4 * HEAD].rearrange("(c d) n -> d c n", d=HEAD)
                        sp.dma_start(dst[a * HEAD:(a + 1) * HEAD, 0:4], src).then_inc(raw_in[n % 2], 16)
                    src = wo[NH * HEAD:].rearrange("(k p) n -> p k n", p=P)
                    sp.dma_start(dst[:, 4:8], src).then_inc(raw_in[n % 2], 16)

        block = ctx.enter_context(nc.Block())

        @block.sync
        def _(sp):
            load_ffn_pair(sp, 0, 0, 0)
            for v in (1, 0):
                for k in range(KC):
                    sp.dma_start(ada_sb[v][:, k], t["w_ada"][k * P:(k + 1) * P, v * D:(v + 1) * D]).then_inc(ada_in[v * KC + k], 16)
            x_rows = t["x"].rearrange("(b p) n -> p b n", p=P)
            for half in range(2):
                cols = slice(half * H, (half + 1) * H)
                sp.dma_start(x_nat[:, 0:4, cols], x_rows[:, 0:4, cols]).then_inc(x_in0[half], 16)
            sp.dma_start(x_nat[:, 4:8], x_rows[:, 4:8]).then_inc(x_in1, 16)
            load_ffn_pair(sp, 0, 0, 1)
            sp.wait_ge(vec_ok, 1)
            load_w2(sp, 0, 0)

            def prefetch(f, i, last=False):
                n = PAIR0[f] + 2 * i
                for j in range(2):
                    sp.wait_ge(wl_ok, n + 1 + j)
                    if not last:
                        load_ffn_pair(sp, f, i + 1, j)
                    elif f == 0:
                        load_mix_pair(sp, MIX0 + j)
                if not last:
                    sp.wait_ge(w2l_ok, (ITER * f + i + 1) * 2)
                    load_w2(sp, f, i + 1)

            with sp.Fori(0, ITER - 1) as i:
                prefetch(0, i)
            prefetch(0, ITER - 1, last=True)
            for n in range(MIX0 + 2, PAIR0[1]):
                sp.wait_ge(wl_ok, n - 1)
                load_mix_pair(sp, n)
            for j in range(2):
                sp.wait_ge(wl_ok, PAIR0[1] + j - 1)
                load_ffn_pair(sp, 1, 0, j)
            sp.wait_ge(yl_ok, 16)
            sp.wait_ge(pl_ok, 8)
            load_w2(sp, 1, 0)
            with sp.Fori(0, ITER - 1) as i:
                prefetch(1, i)
            for r in range(2 * KC):
                h, c = r // KC, r % KC
                sp.wait_ge(fin_sb[r % 2], r // 2 + 1)
                dst = o_out[h * H:(h + 1) * H, c * P:(c + 1) * P].rearrange("(b p) n -> p b n", p=P)
                sp.dma_start(dst, w_raw[0][:, r % 4 // 2, 4 * (r % 2):4 * (r % 2) + 4]).then_inc(stored[r % 4], 16)
            for s in range(4):
                sp.wait_ge(stored[s], 16 * (2 * KC // 4))

        @block.gpsimd
        def _(pool):
            pool.memset(ident[:, :], 0.0).then_inc(small_ok, 1)
            pool.memset(ones[:, :], 1.0).then_inc(small_ok, 1)
            pool.memset(mean_w[:, :], 1.0 / D).then_inc(small_ok, 1)
            pool.memset(half_pow, -0.5).then_inc(small_ok, 1)
            pool.wait_ge(small_ok, 4)
            pool.affine_select(out=ident[:, :], in_=ident[:, :], compare_op=ALU.not_equal, fill=1.0,
                               base=0, pattern=[[-1, P]], channel_multiplier=1).then_inc(const_ok, 1)

            wa = t["w_ada"].rearrange("(k p) n -> p k n", p=P)

            def ada_tiles(i):
                for k in range(KC):
                    above(pool, ada_acc, i * KC + k - 1)
                    pool.dma_start(scratch[:, k % 2, :], wa[:, k, bass.ds(i * D + ADA_EARLY * D, D)]).then_inc(ada_tile[k % 2], 16)

            pool.wait_ge(x_in0[1], 16)
            ada_tiles(0)
            with pool.Fori(1, ADA_UNITS) as i:
                ada_tiles(i)

            def power(s):
                pool.wait_ge(ln_veps, s + 1)
                pool.tensor_tensor(rstd, var_eps, half_pow, ALU.pow).then_inc(ln_rstd, 1)

            def rope_tables(h):
                pool.dma_start(rope[:, 0], t["rope_cos"][:, tok(h)]).then_inc(rope_in, 16)
                pool.dma_start(rope[:, 1], t["rope_sin"][:, tok(h)]).then_inc(rope_in, 16)

            def w_low(n):
                slot = n % 2
                pool.wait_ge(wh_ok, n + 1)
                pool.wait_ge(wl_ok, n)
                pool.tensor_tensor(w_lo[slot][:, :, :, :], w_raw[slot][:, :, :, :], w_hi[slot][:, :, :, :].bitcast(f32),
                                   ALU.subtract).then_inc(wl_ok, 1)

            def windows(r):
                h, g = r // 4, r % 4
                pool.wait_ge(z_used, NZ * h + Z_ORDER[h].index((PL, g)) + 1)
                above(pool, pool_done, r)
                src, n = pool_in[:, g], 1
                for q in range(g + 1):
                    dst = hid[:, 3 - r % 2 if (g - q) % 2 == 0 else 2 + r % 2]
                    lo = 2 * n - 1
                    if q:
                        pool.wait_ge(win_ok, win_count(r) - g - 1 + q)
                    pool.tensor_tensor(dst[:, lo:], src[:, lo:], src[:, lo - n:PAD + H - n], ALU.add).then_inc(win_ok, 1)
                    src, n = dst, 2 * n

            w_low(MIX0)
            power(0)
            w_low(MIX0 + 1)
            pool.wait_ge(f_done, ITER * 2 * KC)
            rope_tables(0)
            pool.dma_start(w_pool[:, :, :], t["w_pool"].rearrange("g c d -> c g d")).then_inc(tab_in, 16)
            pool.dma_start(inv_cnt[:, :, :], t["inv_count"]).then_inc(tab_in, 16)
            pool.memset(own_mask[:, :], 1.0).then_inc(mask_ok, 1)
            pool.memset(own_t[:, :, :], 1.0).then_inc(mask_ok, 1)
            pool.memset(pool_in[:, :, 0:PAD], 0.0).then_inc(mask_ok, 1)
            pool.wait_ge(mask_ok, 3)
            pool.affine_select(out=own_mask[:, :], in_=own_mask[:, :], compare_op=ALU.is_ge, fill=0.0,
                               base=0, pattern=[[-1, P]], channel_multiplier=1).then_inc(mask_ok, 1)
            pool.affine_select(out=own_t[:, 0], in_=own_t[:, 0], compare_op=ALU.is_ge, fill=0.0,
                               base=0, pattern=[[1, P]], channel_multiplier=-1).then_inc(mask_ok, 1)
            pool.affine_select(out=own_t[:, 1], in_=own_t[:, 1], compare_op=ALU.is_gt, fill=0.0,
                               base=0, pattern=[[-1, P]], channel_multiplier=1).then_inc(mask_ok, 1)
            w_low(MIX0 + 2)
            w_low(MIX0 + 3)
            power(1)
            w_low(MIX0 + 4)
            windows(0)
            w_low(MIX0 + 5)
            pool.wait_ge(rope_ok, 5)
            rope_tables(1)
            w_low(MIX0 + 6)
            windows(1)
            w_low(MIX0 + 7)
            windows(2)
            windows(3)
            w_low(MIX0 + 8)
            windows(4)
            w_low(MIX0 + 9)
            w_low(MIX0 + 10)
            w_low(MIX0 + 11)
            windows(5)
            w_low(MIX0 + 12)
            windows(6)
            w_low(MIX0 + 13)
            windows(7)
            for n in range(MIX0 + 14, MIX0 + 17):
                w_low(n)
            power(2)
            for n in range(MIX0 + 17, MIX0 + 20):
                w_low(n)
            for s in range(3, 6):
                power(s)

        def split_product(pe, out, w_h, w_l, x_h, x_l, start, stop):
            pe.matmul(out, w_h, x_h, start=start, stop=False)
            pe.matmul(out, w_h, x_l, start=False, stop=False)
            return pe.matmul(out, w_l, x_h, start=False, stop=stop)

        @block.tensor
        def _(pe):
            def chunk_product(out, slot, a, h, inside=None, order=range(KC)):
                for x, k in enumerate(order):
                    mm = split_product(pe, out, w_hi[slot][:, a, k], w_lo[slot][:, a, k],
                                       u_hi[:, k, tok(h)], u_lo[:, k, tok(h)], x == 0, x == KC - 1)
                    if inside and k in inside:
                        inside[k]()
                return mm

            def staged_product(out, slot, h, stage, done, inside=None):
                for k in range(KC):
                    pe.wait_ge(ul_ok, KC * stage + k + 1)
                    for a in range(2):
                        mm = split_product(pe, ps[:, out + a], w_hi[slot][:, a, k], w_lo[slot][:, a, k],
                                           u_hi[:, k, tok(h)], u_lo[:, k, tok(h)], k == 0, k == KC - 1)
                        if k == KC - 1:
                            mm.then_inc(done, 1)
                    if inside and k in inside:
                        inside[k]()

            def up(f, i, j, h, stage=None, between=None, inside=None):
                e = 4 * (ITER * f + i) + 2 * h + j
                pe.wait_ge(wl_ok, PAIR0[f] + 2 * i + j + 1)
                above(pe, g_ok, e - 1)
                if stage is not None:
                    staged_product(2 * j, j, h, stage, ab_done, inside)
                    return
                chunk_product(ps[:, 2 * j], j, 0, h).then_inc(ab_done, 1)
                if between:
                    between()
                chunk_product(ps[:, 2 * j + 1], j, 1, h, inside).then_inc(ab_done, 1)

            def down(f, i, h, d0=0, d1=KC):
                if d0 == 0:
                    pe.wait_ge(gl_ok, 4 * (ITER * f + i) + 2 * h + 2)
                    pe.wait_ge(w2l_ok, 2 * (ITER * f + i) + 2)
                for d in range(d0, d1):
                    above(pe, f_used, 2 * KC * (ITER * f + i) + KC * h + d - 1)
                    out = ps[:, 4 + d % 2]
                    for j in range(2):
                        mm = split_product(pe, out, w2_hi[:, j, d * P:(d + 1) * P], w2_lo[:, j, d * P:(d + 1) * P],
                                           g_hi[:, h, j], g_lo[:, h, j], j == 0, j == 1)
                    mm.then_inc(f_done, 1)

            def ada_reduce(i):
                pe.wait_ge(ada_acc, KC * i + KC)
                for c in range(KC):
                    mm = pe.matmul(ps[:, 6, c:c + 1], scratch[:, 2, c * P:(c + 1) * P], ones[:, 0:1], start=True, stop=True)
                mm.then_inc(ada_red, 1)

            def mean(s):
                pe.wait_ge(ln_sum, sum_count(s))
                pe.matmul(ps[:, 6], mean_w[:, :], scratch[:, 0, 0:H], start=True, stop=True).then_inc(ln_mean, 1)

            def variance(s):
                pe.wait_ge(sq_used, KC * (s + 1))
                for b in range(4):
                    mm = pe.matmul(ps[:, 7, b:b + 1], scratch[:, 0, H + b * P:H + (b + 1) * P], mean_w[:, 0:1], start=True, stop=True)
                mm.then_inc(ln_var, 1)

            def spread(s):
                pe.wait_ge(ln_diag, s + 1)
                pe.matmul(ps[:, 7], ones[:, :], scratch[:, 1, 0:H], start=True, stop=True).then_inc(ln_bc, 1)

            pe.wait_ge(const_ok, 1)
            pe.wait_ge(c_in, 16)
            pe.transpose(ps[:, 3, 0:KC], c_rows[:, :], ident[0:KC, 0:KC]).then_inc(c_tr, 1)
            def x_transpose(r):
                h, c = r // KC, r % KC
                above(pe, ul_ok, r - 3)
                for b in range(4):
                    mm = pe.transpose(ps[:, 4 + r % 4, b * P:(b + 1) * P], x_nat[:, 4 * h + b, c * P:(c + 1) * P], ident[:, :])
                mm.then_inc(x_tr, 1)
            for v in (1, 0):
                if v == 0:
                    pe.wait_ge(vec_in, 16 * 12)
                    pe.transpose(ps[:, 2, 0:P], vec_rows[0][:, :], ident[:, :]).then_inc(vec_t, 1)
                    pe.transpose(ps[:, 2, P:NV], vec_rows[1][0:NV - P, :], ident[0:NV - P, 0:NV - P]).then_inc(vec_t, 1)
                pe.wait_ge(early_acc[v], KC)
                for c in range(KC):
                    mm = pe.matmul(ps[:, 3, v * KC + c:v * KC + c + 1], acc[:, v, c * P:(c + 1) * P], ones[:, 0:1], start=True, stop=True)
            mm.then_inc(mod0_ps, 1)
            for r in range(KC):
                if r % 4 == 0:
                    pe.wait_ge(x_in0[r // 4], 16)
                x_transpose(r)

            def ffn(f):
                if f == 0:
                    def more_x(r0, r1):
                        pe.wait_ge(x_in1, 16)
                        for r in range(r0, r1):
                            x_transpose(r)
                    up(0, 0, 0, 0, stage=0)
                    more_x(KC, KC + 4)
                    up(0, 0, 1, 0, between=lambda: more_x(KC + 4, KC + 6))
                    more_x(KC + 6, 2 * KC)
                    up(0, 0, 0, 1, stage=1)
                    up(0, 0, 1, 1)
                    ada_reduce(0)
                    down(0, 0, 0)
                else:
                    pe.wait_ge(o_used, 2 * KC)
                    up(1, 0, 0, 0, stage=4, inside={0: lambda: mean(3)})
                    up(1, 0, 1, 0, between=lambda: variance(3))
                    spread(3)
                    down(1, 0, 0)
                    up(1, 0, 0, 1, stage=5)
                    up(1, 0, 1, 1)

                def steady(i, ada):
                    up(f, i, 0, 0)
                    up(f, i, 1, 0)
                    down(f, i - 1, 1)
                    up(f, i, 0, 1)
                    up(f, i, 1, 1)
                    down(f, i, 0)
                    if ada:
                        ada_reduce(i)

                if f == 0:
                    with pe.Fori(1, ADA_UNITS) as i:
                        steady(i, True)
                with pe.Fori(ADA_UNITS if f == 0 else 1, ITER - 1) as i:
                    steady(i, False)
                i, s = ITER - 1, 4 * f
                up(f, i, 0, 0)
                up(f, i, 1, 0)
                down(f, i - 1, 1)
                up(f, i, 0, 1, between=lambda: down(f, i, 0), inside={2: lambda: mean(s)})
                up(f, i, 1, 1)
                variance(s)
                down(f, i, 1, 0, 2)
                spread(s)
                if f == 0:
                    down(f, i, 1, 2, KC)
                else:
                    down(f, i, 1, 2, 5)
                    pe.wait_ge(g_ok, 8 * ITER)
                    for d in range(5, KC):
                        down(f, i, 1, d, d + 1)
                        finish(d - 5)

            def finish(r):
                h, c = r // KC, r % KC
                pe.wait_ge(fin_ok, r + 1)
                above(pe, fin_sb[r % 2], r // 2)
                for b in range(4):
                    mm = pe.transpose(ps[:, r % 2, b * P:(b + 1) * P], acc[:, c, h * H + b * P:h * H + (b + 1) * P], ident[:, :])
                mm.then_inc(fin_t, 1)

            ffn(0)

            def project(m, stage=None, inside=None):
                if m < 2:
                    pe.wait_ge(g_ok, 4 * ITER)
                elif m - 2 < OUT0:
                    pe.wait_ge(z_used, m - 1 + (stage is not None))
                else:
                    pe.wait_ge(o_used, m - 1 - OUT0)
                if m % 2 == 0:
                    pe.wait_ge(wl_ok, MIX0 + m // 2 + 1)
                h = m // NZ if m < OUT0 else (m - OUT0) // KC
                if stage is not None:
                    staged_product(0, m // 2 % 2, h, stage, z_done)
                elif m < OUT0:
                    chunk_product(ps[:, m % 2], m // 2 % 2, m % 2, h, inside).then_inc(z_done, 1)
                else:
                    inside = dict(inside or {})
                    pe.wait_ge(pl_ok, 4 * (h + 1))
                    then = inside.get(KC - 1)

                    def attention_ready():
                        if then:
                            then()
                        pe.wait_ge(yl_ok, 8 * (h + 1))
                    inside[KC - 1] = attention_ready
                    chunk_product(ps[:, m % 2], m // 2 % 2, m % 2, h, inside, list(range(4, KC)) + list(range(4))).then_inc(z_done, 1)

            def v_transposes(h):
                pe.wait_ge(z_used, NZ * h + 2)
                for b in range(4):
                    mm = pe.transpose(ps[:, 4 + 2 * h, b * P:(b + 1) * P], v_tr[:, b * P:(b + 1) * P], ident[:, :])
                mm.then_inc(v_t, 1)

            def scores(n):
                b, kv = n // 2, n % 2
                pe.wait_ge(rope_ok, 5 if n < 8 else 10)
                above(pe, sel_ok, n)
                rows = slice(kv * HEAD, (kv + 1) * HEAD)
                q0 = b % 4 * P
                for c in range(4):
                    out = ps[:, 2 + c // 2, c % 2 * 2 * P:(c % 2 + 1) * 2 * P]
                    k0, out = (0, out[:, P:]) if b == 0 else ((b - 1) * P, out)
                    mm = pe.matmul(out, q_sb[rows, c, q0:q0 + P], k_sb[rows, k0:(b + 1) * P], start=True, stop=True)
                mm.then_inc(sc_done, 1)

            def transposes(n):
                pe.wait_ge(prob_ok, n + 1)
                for c in range(4):
                    mm = pe.transpose(ps[:, 4, c * P:(c + 1) * P], probs[:, n % 2, c], ident[:, :])
                mm.then_inc(t_done, 1)

            def values(n):
                b = n // 2
                pe.wait_ge(pt_ok, 2 * n + 2)
                pe.wait_ge(v_ok, b // 4 + 1)
                above(pe, yl_ok, n)
                mm = pe.matmul(ps[:, 5], v_sb[:, b], pt[:, 0], start=True, stop=(b == 0))
                if b > 0:
                    mm = pe.matmul(ps[:, 5], v_sb[:, b - 1], pt[:, 1], start=False, stop=True)
                mm.then_inc(pv_done, 1)

            def pool_mix(r):
                pe.wait_ge(diff_ok, r + 1)
                pe.wait_ge(tab_in, 32)
                above(pe, pl_ok, r)
                pe.matmul(ps[:, 7], w_pool[:, r % 4], hid[:, 2 + r % 2, PAD:], start=True, stop=True).then_inc(pool_done, 1)

            project(0, stage=2)
            project(2)
            project(3, inside={1: lambda: mean(1)})
            v_transposes(0)
            project(4)
            project(5, inside={3: lambda: variance(1)})
            project(6, inside={0: lambda: spread(1)})
            for m in range(7, NZ):
                project(m)
            for x in range(SLOTS):
                if x in GROUP_SLOT and x != NZ:
                    scores(GROUP_SLOT[x])
                if x == 0:
                    project(NZ, stage=3)
                elif 1 < x < NZ - 1:
                    project(NZ + x)
                elif x == NZ - 1:
                    project(NZ + x, inside={4: lambda: values(7)})
                elif x in OUT_SLOT:
                    project(OUT0 + OUT_SLOT[x])
                if x == NZ:
                    scores(8)
                if x in POOL_SLOT:
                    pool_mix(POOL_SLOT[x])
                if x == 3:
                    v_transposes(1)
                if x != NZ - 1 and x - 2 in GROUP_SLOT:
                    values(GROUP_SLOT[x - 2])
                if x - 1 in GROUP_SLOT:
                    transposes(GROUP_SLOT[x - 1])
            for m in range(KC):
                inside = {0: {5: lambda: values(15), 2: lambda: mean(2)}, 3: {1: lambda: variance(2)}, 4: {4: lambda: spread(2)}}
                project(OUT0 + KC + m, inside=inside.get(m))

            ffn(1)

            finish(3)
            mean(5)
            for c in range(KC):
                pe.wait_ge(ln_sq, KC * 5 + c + 1)
                for b in range(4):
                    mm = pe.matmul(ps[:, 2 + b, 0:1], scratch[:, 1 + c % 2, H + b * P:H + (b + 1) * P], mean_w[:, 0:1],
                                   start=(c == 0), stop=(c == KC - 1))
                mm.then_inc(sq_used, 1)
            finish(4)
            finish(5)
            spread(5)
            for r in range(6, 2 * KC):
                finish(r)

        @block.scalar
        def _(act):
            def w_split(n, slot, landed, used):
                if used is not None:
                    act.wait_ge(*used)
                act.wait_ge(raw_in[slot], landed)
                act.activation(w_hi[slot][:, :, :, :], w_raw[slot][:, :, :, :], ACT.Copy).then_inc(wh_ok, 1)

            def w2_split(f, i):
                above(act, f_done, 2 * KC * (ITER * f + i))
                act.wait_ge(w2_in, 16 * (ITER * f + i + 1))
                for j in range(2):
                    act.activation(w2_hi[:, j], w2_raw[:, j], ACT.Copy).then_inc(w2h_ok, 1)

            def silu(f, i, j, h):
                e = 4 * (ITER * f + i) + 2 * h + j
                act.wait_ge(ab_done, 2 * e + 1)
                act.activation(hid[:, j, 0:H], ps[:, 2 * j], ACT.Silu).then_inc(silu_ok, 1)

            def gate_hi(f, i, j, h):
                e = 4 * (ITER * f + i) + 2 * h + j
                act.wait_ge(g_ok, e + 1)
                above(act, f_done, 2 * KC * (ITER * f + i - 1) + KC * h + KC)
                act.activation(g_hi[:, h, j], hid[:, 2 + j, 0:H], ACT.Copy).then_inc(gh_ok, 1)

            def squares(s, c0=0, c1=KC):
                h = s % 2
                for c in range(c0, c1):
                    act.wait_ge(ln_cent, KC * s + c + 1)
                    if c >= 2:
                        act.wait_ge(sq_used, KC * s + c - 1)
                    act.activation(scratch[:, 1 + c % 2, H:], acc[:, c, tok(h)], ACT.Square).then_inc(ln_sq, 1)

            def input_hi(st, c):
                h, n, cf = st % 2, KC * st + c, C_N * (st // 2)
                if st < 2:
                    act.wait_ge(u32_ok, n + 1)
                    act.activation(acc[:, c, tok(h)], ps[:, 4 + (KC * h + c) % 4], ACT.Copy, scale=ALPHA).then_inc(acc_ok, 1)
                    act.activation(u_hi[:, c, tok(h)], new_input(st, c), ACT.Copy).then_inc(uh_ok, 1)
                    return
                a, b = (coef[:, cf + x + c:cf + x + c + 1] for x in (C_A, C_B))
                act.wait_ge(ln_t, n - 2 * KC + 1)
                act.wait_ge(ul_ok, n - 1)
                act.activation(new_input(st, c), acc[:, c, tok(h)], ACT.Identity, bias=b, scale=a).then_inc(u32_ok, 1)
                act.activation(u_hi[:, c, tok(h)], acc[:, c, tok(h)], ACT.Identity, bias=b, scale=a).then_inc(uh_ok, 1)

            def keep(st, c0=0, c1=KC):
                h, cf = st % 2, C_N * (st // 2)
                for c in range(c0, c1):
                    act.wait_ge(uh_ok, KC * st + c + 1)
                    act.activation(acc[:, c, tok(h)], acc[:, c, tok(h)], ACT.Identity, bias=coef[:, cf + C_AB + c:cf + C_AB + c + 1],
                                   scale=coef[:, cf + C_AG + c:cf + C_AG + c + 1]).then_inc(acc_ok, 1)

            def affine(h, c):
                s = 4 + h
                g, b = (vec[:, V_LN + (4 + v) * KC + c:V_LN + (4 + v) * KC + c + 1] for v in range(2))
                act.wait_ge(ln_t, KC * s + c + 1)
                act.activation(acc[:, c, tok(h)], acc[:, c, tok(h)], ACT.Identity, bias=b, scale=g).then_inc(fin_ok, 1)

            def finish(r):
                act.wait_ge(fin_t, r + 1)
                above(act, stored[r % 4], 16 * (r // 4))
                act.activation(w_raw[0][:, r % 4 // 2, 4 * (r % 2):4 * (r % 2) + 4], ps[:, r % 2].rearrange("p (b n) -> p b n", b=4),
                               ACT.Copy).then_inc(fin_sb[r % 2], 1)

            act.dma_start(c_rows[:, :], t["c"].rearrange("a (n p) -> (a n) p", p=P)).then_inc(c_in, 16)
            rows = [(0, 0, t["b_ada"], 72), (0, 72, t["ln1_g"], 8), (0, 80, t["ln1_b"], 8), (0, 88, t["ln2_g"], 8),
                    (0, 96, t["ln2_b"], 8), (0, 104, t["ln3_g"], 8), (0, 112, t["ln3_b"], 8), (0, 120, t["b_out"], 8),
                    (1, 4, t["b_in"][:, 512:IN_W], 6), (1, 10, t["pool_scale"], 4)]
            for x, (r, row, src, n) in enumerate(rows):
                act.dma_start(vec_rows[r][row:row + n, :], src.rearrange("a (n p) -> (a n) p", p=P)).then_inc(vec_in, 16)
                if x == 4:
                    act.wait_ge(c_tr, 1)
                    act.activation(c_act[:, :], ps[:, 3, 0:KC], ACT.Silu).then_inc(cact_ok, 1)
                    w_split(0, 0, raw_count(0), None)
            for a in range(2):
                src = t["b_in"][:, a * 256:(a + 1) * 256].rearrange("a (c d) -> (a c) d", d=HEAD)
                act.dma_start(vec_rows[1][0:4, a * HEAD:(a + 1) * HEAD], src).then_inc(vec_in, 16)
            act.dma_start(sinks, t["attn_sinks"].broadcast_to([P, NH])).then_inc(sink_in, 16)

            def ffn(f):
                st, s = 4 * f, 4 * f - 1
                last = ITER - 1
                if f == 0:
                    for c in range(KC):
                        input_hi(0, c)
                    w_split(1, 1, raw_count(1), None)
                    for c in range(KC):
                        input_hi(1, c)
                        if c == 3:
                            silu(0, 0, 0, 0)
                            gate_hi(0, 0, 0, 0)
                    w2_split(0, 0)
                else:
                    squares(3)
                    silu(1, 0, 0, 0)
                    gate_hi(1, 0, 0, 0)
                    w2_split(1, 0)
                silu(f, 0, 1, 0)
                gate_hi(f, 0, 1, 0)
                if f == 1:
                    for c in range(KC):
                        input_hi(5, c)
                    keep(5)

                def half1(i):
                    for j in range(2):
                        silu(f, i, j, 1)
                        gate_hi(f, i, j, 1)
                        w_split(None, j, raw_count(PAIR0[f] + j) + 32 * (i + 1),
                                (ab_done, 8 * (ITER * f + i) + 6 + 2 * j))

                def steady(i):
                    for j in range(2):
                        silu(f, i, j, 0)
                        gate_hi(f, i, j, 0)
                    w2_split(f, i)
                    half1(i)

                half1(0)
                with act.Fori(1, last) as i:
                    steady(i)
                for j in range(2):
                    silu(f, last, j, 0)
                    gate_hi(f, last, j, 0)
                w2_split(f, last)
                squares(4 * f, 0, 4)
                silu(f, last, 0, 1)
                gate_hi(f, last, 0, 1)
                if f == 0:
                    w_split(MIX0, 0, raw_count(MIX0), (ab_done, 8 * last + 6))
                squares(4 * f, 4, KC)
                silu(f, last, 1, 1)
                gate_hi(f, last, 1, 1)
                if f == 0:
                    w_split(MIX0 + 1, 1, raw_count(MIX0 + 1), (ab_done, 8 * last + 8))

            ffn(0)

            def next_pair(m):
                n = MIX0 + m // 2 + 2
                w_split(n, n % 2, raw_count(n), (z_done, m + 1))

            def drain(m):
                h = m // NZ
                kind, c = Z_ORDER[h][m % NZ]
                act.wait_ge(z_done, m + 1)
                if kind == Q:
                    if h == 1:
                        act.wait_ge(sc_done, 8)
                    dst = q_sb[:, c]
                elif kind == K:
                    dst = k_sb[:, tok(h)]
                elif kind == V:
                    above(act, v_t, h)
                    dst = v_tr
                else:
                    if h == 1:
                        act.wait_ge(carry_ok, c + 1)
                    dst = pool_in[:, c, PAD:]
                col = V_BIN + Z_COL[kind] + c
                act.activation(dst, ps[:, m % 2], ACT.Identity, bias=vec[:, col:col + 1]).then_inc(z_used, 1)

            def v_store(h):
                act.wait_ge(v_t, h + 1)
                act.activation(v_sb[:, 4 * h:4 * h + 4], ps[:, 4 + 2 * h].rearrange("p (b n) -> p b n", b=4), ACT.Copy).then_inc(v_ok, 1)

            def banded(block_of):
                return ps[:, 2:4].rearrange("p b (c k) -> p (b c) k", c=2)[:, :, block_of * P:(block_of + 1) * P]

            def before_scores(n):
                if n >= 2:
                    act.wait_ge(sc_done, n + 1)
                    act.wait_ge(t_done, n - 1)
                    act.activation(probs[:, n % 2], banded(0), ACT.Copy).then_inc(prev_ok, 1)

            def exps(n):
                act.wait_ge(sel_ok, n + 1)
                act.wait_ge(neg_ok, n + 1)
                for c in range(4):
                    act.activation(probs[:, n % 2, c], probs[:, n % 2, c], ACT.Exp, bias=neg_max[:, c:c + 1], scale=HEAD ** -0.5,
                                   accum_out=row_sum[:, c:c + 1]).then_inc(exp_ok, 1)
                act.wait_ge(sd_ok, n + 1)
                act.activation(sink_exp, sink_sh, ACT.Exp).then_inc(exp_ok, 1)

            def attn_hi(n):
                b, rows = n // 2, slice(n % 2 * HEAD, (n % 2 + 1) * HEAD)
                act.wait_ge(pv_done, n + 1)
                act.activation(u_hi[rows, 0:4, b * P:(b + 1) * P], ps[rows, 5].rearrange("p (c q) -> p c q", c=4), ACT.Copy).then_inc(yh_ok, 1)

            def pool_hi(r):
                h, g = r // 4, r % 4
                act.wait_ge(pool_done, r + 1)
                act.activation(u_hi[:, 4 + g, tok(h)], ps[:, 7], ACT.Copy, scale=vec[:, V_PS + g:V_PS + g + 1]).then_inc(ph_ok, 1)

            for c in range(KC):
                input_hi(2, c)
            drain(0)
            drain(1)
            next_pair(1)
            drain(2)
            squares(1, 0, 4)
            drain(3)
            next_pair(3)
            squares(1, 4, KC)
            v_store(0)
            drain(4)
            drain(5)
            next_pair(5)
            input_hi(3, 0)
            drain(6)
            for c in range(1, KC):
                input_hi(3, c)
                if c == 3:
                    drain(7)
                if c == 5:
                    next_pair(7)
            drain(8)
            drain(9)
            next_pair(9)
            for x in range(SLOTS):
                if x in GROUP_SLOT:
                    before_scores(GROUP_SLOT[x])
                    exps(GROUP_SLOT[x])
                if x == 0:
                    drain(NZ)
                    drain(NZ + 1)
                elif 1 < x < NZ and x != 6:
                    if x == 7:
                        drain(NZ + 6)
                    drain(NZ + x)
                if x in POOL_SLOT:
                    pool_hi(POOL_SLOT[x])
                if x == 3:
                    v_store(1)
                if x < KC:
                    keep(2, x, x + 1)
                    keep(3, x, x + 1)
                if x - 2 in GROUP_SLOT:
                    attn_hi(GROUP_SLOT[x - 2])
                if x < NZ and x % 2 == 1:
                    next_pair(NZ + x if x > 1 else NZ + 1)
                if x in OUT_SLOT and OUT_SLOT[x] % 2 == 1:
                    next_pair(OUT0 + OUT_SLOT[x])
            attn_hi(15)
            squares(2)
            next_pair(OUT0 + KC + 1)
            next_pair(OUT0 + KC + 3)
            for c in range(KC):
                input_hi(4, c)
                if c == 5:
                    next_pair(OUT0 + KC + 5)
            keep(4)
            next_pair(OUT0 + KC + 7)

            ffn(1)
            for c in range(4):
                affine(0, c)
                if c >= 2:
                    finish(2 * c - 4)
            for c in range(KC):
                act.wait_ge(ln_cent, KC * 5 + c + 1)
                act.wait_ge(sq_used, KC * 5 + c - 1)
                act.activation(scratch[:, 1 + c % 2, H:], acc[:, c, tok(1)], ACT.Square).then_inc(ln_sq, 1)
            for c in range(4, KC):
                affine(0, c)
            finish(4)
            affine(1, 0)
            finish(6)
            for c in range(1, KC):
                affine(1, c)
                if c % 2 == 1:
                    finish(KC + c - 1)

        @block.vector
        def _(dve):
            f = f32

            def w_low(slot, n):
                dve.wait_ge(wh_ok, n + 1)
                dve.tensor_tensor(w_lo[slot][:, :, :, :], w_raw[slot][:, :, :, :], w_hi[slot][:, :, :, :].bitcast(f),
                                  ALU.subtract).then_inc(wl_ok, 1)

            def w2_low(f_, i):
                for j in range(2):
                    dve.wait_ge(w2h_ok, 2 * (ITER * f_ + i) + j + 1)
                    dve.tensor_tensor(w2_lo[:, j], w2_raw[:, j], w2_hi[:, j].bitcast(f), ALU.subtract).then_inc(w2l_ok, 1)

            def gated(f_, i, j, h, between=None):
                e = 4 * (ITER * f_ + i) + 2 * h + j
                dve.wait_ge(silu_ok, e + 1)
                dve.wait_ge(ab_done, 2 * e + 2)
                above(dve, gl_ok, e - 1)
                dve.tensor_tensor(hid[:, 2 + j, 0:H], hid[:, j, 0:H], ps[:, 2 * j + 1], ALU.mult).then_inc(g_ok, 1)
                if between:
                    between()
                dve.wait_ge(gh_ok, e + 1)
                dve.tensor_tensor(g_lo[:, h, j], hid[:, 2 + j, 0:H], g_hi[:, h, j].bitcast(f), ALU.subtract).then_inc(gl_ok, 1)

            def add_total(s, d, used):
                if d == 0:
                    return
                dve.wait_ge(*used)
                own = sum_count(s - 1) if s else 0
                first = scratch[:, 0, 0:H] if d > 1 else acc[:, 0, tok(s % 2)]
                above(dve, ln_mean, s)
                above(dve, ln_sum, own + d - 1)
                dve.tensor_tensor(scratch[:, 0, 0:H], first, acc[:, d, tok(s % 2)], ALU.add).then_inc(ln_sum, 1)

            def residual(f_, i, h, d0=0, d1=KC, s=None):
                cf = C_N * (0 if f_ == 0 else 2) + C_GATE
                for d in range(d0, d1):
                    q = 2 * KC * (ITER * f_ + i) + KC * h + d
                    dve.wait_ge(f_done, q + 1)
                    above(dve, f_used, q + 1 - KC)
                    dve.scalar_tensor_tensor(acc[:, d, tok(h)], ps[:, 4 + d % 2], coef[:, cf + d:cf + d + 1], acc[:, d, tok(h)],
                                             ALU.mult, ALU.add).then_inc(f_used, 1)
                    if s is not None:
                        add_total(s, d, (f_used, q + 1))

            def ada_step(i, k):
                dve.wait_ge(ada_tile[k % 2], 16 * (4 * i + k // 2 + 1))
                if k == 0:
                    above(dve, ada_red, i)
                    dve.tensor_scalar(scratch[:, 2], scratch[:, k % 2], c_act[:, k:k + 1], None, ALU.mult).then_inc(ada_acc, 1)
                else:
                    dve.wait_ge(ada_acc, KC * i + k)
                    dve.scalar_tensor_tensor(scratch[:, 2], scratch[:, k % 2], c_act[:, k:k + 1], scratch[:, 2],
                                             ALU.mult, ALU.add).then_inc(ada_acc, 1)

            def ada_store(i):
                dve.wait_ge(ada_red, i + 1)
                cols = bass.ds(i * KC + ADA_EARLY * KC, KC)
                dve.tensor_tensor(mods[:, cols], ps[:, 6, 0:KC], vec[:, cols], ALU.add).then_inc(mod_ok, 1)

            chain = [0]

            def coef_op(what, *args):
                what(*args).then_inc(coef_ok, 1)
                chain[0] += 1
                dve.wait_ge(coef_ok, chain[0])

            def coefs(st):
                cf = C_N * st
                sh, sc, gt = (mods[:, (3 * st + v) * KC:(3 * st + v + 1) * KC] for v in range(3))
                a, b, ag, ab, gate = (coef[:, cf + x:cf + x + KC] for x in (C_A, C_B, C_AG, C_AB, C_GATE))
                g, beta = (vec[:, V_LN + (2 * (st - 1) + v) * KC:V_LN + (2 * (st - 1) + v + 1) * KC] for v in range(2))
                coef_op(dve.tensor_scalar, a, sc, 1.0, None, ALU.add)
                coef_op(dve.tensor_tensor, b, beta, a, ALU.mult)
                coef_op(dve.tensor_tensor, b, b, sh, ALU.add)
                coef_op(dve.tensor_tensor, a, a, g, ALU.mult)
                coef_op(dve.tensor_scalar, gate, gt, 1.0, None, ALU.add)
                coef_op(dve.tensor_scalar, ag, g, ALPHA, None, ALU.mult)
                coef_op(dve.tensor_scalar, ab, beta, ALPHA, None, ALU.mult)
                if st == 1:
                    bias = vec[:, V_BOUT:V_BOUT + KC]
                    coef_op(dve.tensor_tensor, small[:, 56:64], gate, bias, ALU.mult)
                    coef_op(dve.tensor_tensor, ab, ab, small[:, 56:64], ALU.add)
                else:
                    coef_op(dve.tensor_scalar, gate, gate, 0.5, None, ALU.mult)

            def total(s):
                h = s % 2
                dve.tensor_reduce(scratch[:, 0, 0:H], acc[:, :, tok(h)].rearrange("p c n -> p n c"), AX.X, ALU.add).then_inc(ln_sum, 1)

            def add_square(s, c):
                sq, sq_sum = scratch[:, 1 + c % 2, H:], scratch[:, 0, H:]
                dve.wait_ge(ln_sq, KC * s + c + 1)
                if c == 0:
                    dve.tensor_copy(sq_sum, sq).then_inc(sq_used, 1)
                else:
                    dve.wait_ge(sq_used, KC * s + c)
                    dve.tensor_tensor(sq_sum, sq_sum, sq, ALU.add).then_inc(sq_used, 1)

            def centre(s, c0=0, c1=KC, sums=True):
                h = s % 2
                dve.wait_ge(ln_mean, s + 1)
                for c in range(c0, c1):
                    dve.tensor_tensor(acc[:, c, tok(h)], acc[:, c, tok(h)], ps[:, 6], ALU.subtract).then_inc(ln_cent, 1)
                    if c >= 2 and sums:
                        add_square(s, c - 2)
                if c1 == KC and sums:
                    add_square(s, KC - 2)
                    add_square(s, KC - 1)

            def deviation(s):
                if s < 5:
                    dve.wait_ge(ln_var, s + 1)
                else:
                    dve.wait_ge(sq_used, KC * 6)
                var = ps[:, 7, 0:4] if s < 5 else ps[:, 2:6, 0]
                dve.tensor_scalar(var_eps, var, EPS, None, ALU.add).then_inc(ln_veps, 1)

            def diagonal(s):
                dve.wait_ge(ln_rstd, s + 1)
                dve.tensor_tensor(scratch[:, 1, 0:H].rearrange("p (b n) -> p b n", b=4),
                                  ident[:, :].unsqueeze(1).broadcast_to([P, 4, P]),
                                  rstd.unsqueeze(2).broadcast_to([P, 4, P]), ALU.mult).then_inc(ln_diag, 1)

            def normal(s, c):
                if c == 0:
                    dve.wait_ge(ln_bc, s + 1)
                src = acc[:, c, tok(s % 2)]
                dve.tensor_tensor(src, src, ps[:, 7], ALU.mult).then_inc(ln_t, 1)

            def input_chunks(st, c0=0, c1=KC):
                h, cf = st % 2, C_N * (st // 2)

                def low(c):
                    dve.wait_ge(uh_ok, KC * st + c + 1)
                    dve.wait_ge(u32_ok, KC * st + c + 1)
                    dve.tensor_tensor(u_lo[:, c, tok(h)], new_input(st, c), u_hi[:, c, tok(h)].bitcast(f),
                                      ALU.subtract).then_inc(ul_ok, 1)

                for c in range(c0, c1):
                    if st < 2:
                        a, b = (coef[:, cf + x + c:cf + x + c + 1] for x in (C_A, C_B))
                        dve.wait_ge(x_tr, KC * st + c + 1)
                        above(dve, ul_ok, KC * st + c - 1)
                        dve.tensor_scalar(new_input(st, c), ps[:, 4 + (KC * h + c) % 4], a, b, ALU.mult, ALU.add).then_inc(u32_ok, 1)
                    else:
                        normal(st - 2, c)
                    if c >= 1:
                        low(c - 1)
                if c1 == KC:
                    low(KC - 1)

            def finish(r):
                dve.wait_ge(fin_t, r + 1)
                above(dve, stored[r % 4], 16 * (r // 4))
                dve.tensor_copy(w_raw[0][:, r % 4 // 2, 4 * (r % 2):4 * (r % 2) + 4],
                                ps[:, r % 2].rearrange("p (b n) -> p b n", b=4)).then_inc(fin_sb[r % 2], 1)

            dve.wait_ge(cact_ok, 1)
            for v in (1, 0):
                for k in range(KC):
                    if v == 1 and k == 2:
                        w_low(0, 0)
                    dve.wait_ge(ada_in[v * KC + k], 16)
                    if k == 0:
                        dve.tensor_scalar(acc[:, v], ada_sb[v][:, k], c_act[:, k:k + 1], None, ALU.mult).then_inc(early_acc[v], 1)
                    else:
                        dve.wait_ge(early_acc[v], k)
                        dve.scalar_tensor_tensor(acc[:, v], ada_sb[v][:, k], c_act[:, k:k + 1], acc[:, v],
                                                 ALU.mult, ALU.add).then_inc(early_acc[v], 1)
            dve.wait_ge(vec_t, 2)
            dve.tensor_copy(vec[:, :], ps[:, 2, 0:NV]).then_inc(vec_ok, 1)
            dve.wait_ge(sink_in, 16)
            dve.tensor_scalar(neg_sinks, sinks, -1.0, None, ALU.mult).then_inc(sink_ok, 1)
            dve.wait_ge(vec_ok, 1)
            dve.wait_ge(mod0_ps, 1)
            dve.tensor_tensor(mods[:, 0:2 * KC], ps[:, 3, 0:2 * KC], vec[:, 0:2 * KC], ALU.add).then_inc(mod_ok, 1)
            dve.wait_ge(mod_ok, 1)
            coef_op(dve.tensor_scalar, coef[:, C_A:C_A + KC], mods[:, KC:2 * KC], 1.0, None, ALU.add)
            coef_op(dve.tensor_copy, coef[:, C_B:C_B + KC], mods[:, 0:KC])

            def ffn(f_):
                last = ITER - 1
                if f_ == 0:
                    input_chunks(0)
                    w_low(1, 1)
                    for k in range(2):
                        ada_step(0, k)
                    input_chunks(1, 0, 4)
                    ada_step(0, 2)
                    gated(0, 0, 0, 0)
                    ada_step(0, 3)
                    input_chunks(1, 4, KC)
                    ada_step(0, 4)
                    gated(0, 0, 1, 0)
                    w2_low(0, 0)
                    for k in range(5, 7):
                        ada_step(0, k)
                    gated(0, 0, 0, 1)
                    ada_step(0, 7)
                    w_low(0, 2)
                    gated(0, 0, 1, 1)
                    ada_store(0)
                    dve.wait_ge(mod_ok, 2)
                    coef_op(dve.tensor_scalar, coef[:, C_GATE:C_GATE + KC], mods[:, 2 * KC:3 * KC], 1.0, None, ALU.add)
                    coef_op(dve.tensor_scalar, coef[:, C_GATE:C_GATE + KC], coef[:, C_GATE:C_GATE + KC], 0.5, None, ALU.mult)
                else:
                    centre(3)
                    gated(1, 0, 0, 0)
                    w2_low(1, 0)
                    deviation(3)
                    diagonal(3)
                    gated(1, 0, 1, 0)
                    input_chunks(5, 0, 2)
                    dve.wait_ge(acc_ok, KC * 5)
                    for c in range(KC):
                        residual(1, 0, 0, c, c + 1)
                        if c % 2 == 1 and c < 6:
                            input_chunks(5, c // 2 + 2, c // 2 + 3)
                    input_chunks(5, 5, KC)
                    dve.wait_ge(acc_ok, KC * 6)

                def half1(i, ada=False):
                    gated(f_, i, 0, 1)
                    w_low(0, PAIR0[f_] + 2 * i + 2)
                    if ada:
                        for k in range(6, KC):
                            ada_step(i, k)
                    if isinstance(i, int):
                        gated(f_, i, 1, 1)
                    else:
                        gated(f_, i, 1, 1, between=lambda: residual(f_, i, 0, 0, 1))
                        residual(f_, i, 0, 1, KC)
                    w_low(1, PAIR0[f_] + 2 * i + 3)

                if f_ == 0:
                    residual(0, 0, 0)
                    w_low(1, 3)
                else:
                    half1(0)

                def steady(i, ada):
                    gated(f_, i, 0, 0)
                    if ada:
                        for k in range(0, 3):
                            ada_step(i, k)
                    gated(f_, i, 1, 0, between=lambda: residual(f_, i - 1, 1, 0, 1))
                    residual(f_, i - 1, 1, 1, KC)
                    w2_low(f_, i)
                    if ada:
                        for k in range(3, 6):
                            ada_step(i, k)
                    half1(i, ada)
                    if ada:
                        ada_store(i)

                if f_ == 0:
                    with dve.Fori(1, ADA_UNITS) as i:
                        steady(i, True)
                    dve.wait_ge(mod_ok, 1 + ADA_UNITS)
                    coefs(1)
                    coefs(2)
                with dve.Fori(ADA_UNITS if f_ == 0 else 1, last) as i:
                    steady(i, False)
                s = 4 * f_
                gated(f_, last, 0, 0)
                gated(f_, last, 1, 0, between=lambda: residual(f_, last - 1, 1, 0, 1))
                residual(f_, last - 1, 1, 1, KC)
                w2_low(f_, last)
                residual(f_, last, 0, s=s)
                centre(s, 0, 4)
                gated(f_, last, 0, 1)
                centre(s, 4, KC)
                gated(f_, last, 1, 1)
                residual(f_, last, 1, 0, 1)
                deviation(s)
                diagonal(s)
                if f_ == 0:
                    residual(0, last, 1, 1, 4)
                    for c in range(4, KC):
                        residual(0, last, 1, c, c + 1)
                        input_chunks(2, c - 4, c - 3)
                    input_chunks(2, 4, KC)
                else:
                    residual(1, last, 1, 1, 3, s=5)
                    for c in range(3, KC):
                        residual(1, last, 1, c, c + 1, s=5)
                        if c < 7:
                            normal(4, c - 3)
                        if c == 6:
                            finish(1)

            ffn(0)

            def rotate(r, x):
                h = r // 5
                dve.wait_ge(rope_in, 32 * (h + 1))
                tmp = hid[:, 0, 0:H]
                above(dve, rope_ok, r)
                half = HEAD // 8
                swap = [i + half for i in range(half)] + list(range(half)) + list(range(2 * half, 32))
                dve.stream_shuffle(in_=x, out=tmp, mask=swap).then_inc(shuf_ok, 1)
                dve.wait_ge(shuf_ok, r + 1)
                dve.tensor_tensor(tmp, tmp, rope[:, 1], ALU.mult).then_inc(rope_s, 1)
                dve.tensor_tensor(x, x, rope[:, 0], ALU.mult).then_inc(rope_c, 1)
                dve.wait_ge(rope_s, r + 1)
                dve.wait_ge(rope_c, r + 1)
                dve.tensor_tensor(x, x, tmp, ALU.add).then_inc(rope_ok, 1)

            def rotate_unit(m):
                h = m // NZ
                kind, c = Z_ORDER[h][m % NZ]
                dve.wait_ge(z_used, m + 1)
                rotate(5 * h + (0 if kind == K else 1 + c), k_sb[:, tok(h)] if kind == K else q_sb[:, c])

            shorts = [0]

            def differences(r):
                h, g = r // 4, r % 4
                x, src, out = pool_in[:, g], hid[:, 3 - r % 2], hid[:, 2 + r % 2]
                dve.wait_ge(win_ok, win_count(r))
                first = PAD if h == 0 else 0
                if h == 0:
                    dve.wait_ge(tab_in, 32)
                    dve.tensor_tensor(out[:, PAD:2 * PAD], src[:, PAD:2 * PAD], inv_cnt[:, g], ALU.mult).then_inc(short_ok, 1)
                    shorts[0] += 1
                    dve.wait_ge(short_ok, shorts[0])
                    dve.tensor_tensor(out[:, PAD:2 * PAD], out[:, PAD:2 * PAD], x[:, PAD:2 * PAD], ALU.subtract).then_inc(short_ok, 1)
                    shorts[0] += 1
                dve.scalar_tensor_tensor(out[:, PAD + first:], src[:, PAD + first:], 1.0 / WIN[g], x[:, PAD + first:],
                                         ALU.mult, ALU.subtract).then_inc(diff_ok, 1)
                if h == 0:
                    dve.wait_ge(diff_ok, r + 1)
                    dve.tensor_copy(x[:, 0:PAD], x[:, H:H + PAD]).then_inc(carry_ok, 1)

            def pool_low(r):
                h, g = r // 4, r % 4
                dve.wait_ge(ph_ok, r + 1)
                dve.scalar_tensor_tensor(u_lo[:, 4 + g, tok(h)], ps[:, 7], vec[:, V_PS + g:V_PS + g + 1],
                                         u_hi[:, 4 + g, tok(h)].bitcast(f), ALU.mult, ALU.subtract).then_inc(pl_ok, 1)

            def softmax(n):
                kv = n % 2
                own = ps[:, 2:4].rearrange("p b (c k) -> p (b c) k", c=2)[:, :, P:2 * P]
                dve.wait_ge(sc_done, n + 1)
                if n < 2:
                    dve.memset(probs[:, n % 2], -1e30).then_inc(prev_ok, 1)
                dve.wait_ge(prev_ok, n + 1)
                dve.copy_predicated(out=probs[:, n % 2], mask=own_mask[:, :].bitcast(u32).unsqueeze(1).broadcast_to([P, 4, P]),
                                    data=own).then_inc(sel_ok, 1)
                dve.wait_ge(sel_ok, n + 1)
                dve.tensor_reduce(row_max, probs[:, n % 2], AX.X, ALU.max).then_inc(max_ok, 1)
                dve.wait_ge(max_ok, n + 1)
                dve.scalar_tensor_tensor(neg_max, row_max, -HEAD ** -0.5, neg_sinks[:, 4 * kv:4 * kv + 4],
                                         ALU.mult, ALU.min).then_inc(neg_ok, 1)
                dve.wait_ge(neg_ok, n + 1)
                dve.tensor_tensor(sink_sh, neg_max, sinks[:, 4 * kv:4 * kv + 4], ALU.add).then_inc(sd_ok, 1)

            def normalise(n):
                dve.wait_ge(exp_ok, 5 * (n + 1))
                dve.tensor_tensor(denom, row_sum, sink_exp, ALU.add).then_inc(den_ok, 1)
                dve.wait_ge(den_ok, n + 1)
                dve.reciprocal(recip, denom).then_inc(rec_ok, 1)
                dve.wait_ge(rec_ok, n + 1)
                dve.tensor_tensor(probs[:, n % 2], probs[:, n % 2], recip.unsqueeze(2).broadcast_to([P, 4, P]),
                                  ALU.mult).then_inc(prob_ok, 1)

            def masked_t(n):
                dve.wait_ge(t_done, n + 1)
                above(dve, pv_done, n)
                for a in range(2):
                    dve.tensor_tensor(pt[:, a], ps[:, 4].rearrange("p (c q) -> p c q", c=4),
                                      own_t[:, a].unsqueeze(1).broadcast_to([P, 4, P]), ALU.mult).then_inc(pt_ok, 1)

            def attn_low(n):
                b, rows = n // 2, slice(n % 2 * HEAD, (n % 2 + 1) * HEAD)
                dve.wait_ge(yh_ok, n + 1)
                dve.tensor_tensor(u_lo[rows, 0:4, b * P:(b + 1) * P], ps[rows, 5].rearrange("p (c q) -> p c q", c=4),
                                  u_hi[rows, 0:4, b * P:(b + 1) * P].bitcast(f), ALU.subtract).then_inc(yl_ok, 1)

            def out_residual(m):
                d, h = (m - OUT0) % KC, (m - OUT0) // KC
                dve.wait_ge(z_done, m + 1)
                dve.wait_ge(acc_ok, KC * 4)
                dve.scalar_tensor_tensor(acc[:, d, tok(h)], ps[:, m % 2], coef[:, C_N + C_GATE + d:C_N + C_GATE + d + 1],
                                         acc[:, d, tok(h)], ALU.mult, ALU.add).then_inc(o_used, 1)
                add_total(2 + h, d, (o_used, m - OUT0 + 1))

            total(1)
            rotate_unit(0)
            centre(1, 0, 4)
            centre(1, 4, KC)
            deviation(1)
            diagonal(1)
            for m in range(2, 5):
                rotate_unit(m)
            input_chunks(3, 0, 4)
            rotate_unit(5)
            input_chunks(3, 4, KC)
            dve.wait_ge(sink_ok, 1)
            dve.wait_ge(mask_ok, 6)
            for x in range(SLOTS):
                if x in GROUP_SLOT:
                    softmax(GROUP_SLOT[x])
                if x == 1:
                    rotate_unit(NZ)
                if x in GROUP_SLOT:
                    normalise(GROUP_SLOT[x])
                if x in (8, 9):
                    rotate_unit(NZ + x - 2)
                if x == 9:
                    rotate_unit(2 * NZ - 2)
                if x in OUT_SLOT:
                    out_residual(OUT0 + OUT_SLOT[x])
                if x in POOL_SLOT:
                    pool_low(POOL_SLOT[x])
                if x - 2 in GROUP_SLOT:
                    attn_low(GROUP_SLOT[x - 2])
                if x - 1 in GROUP_SLOT:
                    masked_t(GROUP_SLOT[x - 1])
                if x + 1 in POOL_SLOT:
                    differences(POOL_SLOT[x + 1])
                if x == 9:
                    rotate_unit(2 * NZ - 1)
            attn_low(15)
            centre(2, 0, 4)
            out_residual(OUT0 + KC)
            centre(2, 4, KC)
            out_residual(OUT0 + KC + 1)
            out_residual(OUT0 + KC + 2)
            deviation(2)
            diagonal(2)
            out_residual(OUT0 + KC + 3)
            input_chunks(4, 0, 3)
            out_residual(OUT0 + KC + 4)
            input_chunks(4, 3, 6)
            out_residual(OUT0 + KC + 5)
            input_chunks(4, 6, KC)
            out_residual(OUT0 + KC + 6)
            out_residual(OUT0 + KC + 7)

            ffn(1)
            centre(5, 0, 4, sums=False)
            finish(3)
            centre(5, 4, KC, sums=False)
            for c in range(4, KC):
                normal(4, c)
            deviation(5)
            diagonal(5)
            finish(5)
            for c in range(KC):
                normal(5, c)
                if c == 1:
                    finish(7)
                if c >= 3 and c % 2 == 1:
                    finish(KC + c - 2)
            finish(2 * KC - 1)


_PARAMS = ["w_ada", "b_ada", "ffn1_w1", "ffn1_w3", "ffn1_w2", "ln1_g", "ln1_b", "w_in", "b_in", "attn_sinks", "w_pool",
           "pool_scale", "w_out", "b_out", "ln2_g", "ln2_b", "ffn2_w1", "ffn2_w3", "ffn2_w2", "ln3_g", "ln3_b"]


def _tables():
    import numpy as np
    rot = HEAD // 4
    freq = (500000.0 ** (-np.arange(0, rot, 2, dtype=np.float64) / rot)).astype(np.float32)
    ang = (np.arange(S, dtype=np.float32)[None, :] * freq[:, None]).astype(np.float64)
    cos, sin = np.ones((P, S), np.float32), np.zeros((P, S), np.float32)
    for base in (0, HEAD):
        for sign, at in ((-1.0, 0), (1.0, rot // 2)):
            cos[base + at:base + at + rot // 2] = np.cos(ang)
            sin[base + at:base + at + rot // 2] = sign * np.sin(ang)
    cnt = np.stack([1.0 / np.minimum(np.arange(PAD) + 1, w) for w in WIN])
    return {"rope_cos": cos, "rope_sin": sin,
            "inv_count": np.ascontiguousarray(np.broadcast_to(cnt[None], (P, 4, PAD))).astype(np.float32)}


def kernel(**inputs):
    import numpy as np
    import concourse.bacc as bacc
    from concourse.bass_utils import run_bass_kernel_spmd

    nc = bacc.Bacc("TRN2", target_bir_lowering=False, num_devices=1)
    arrays = {"x": np.ascontiguousarray(inputs["x"]).reshape(S, D), "c": np.ascontiguousarray(inputs["c"])}
    for name in _PARAMS:
        a = np.ascontiguousarray(inputs[name])
        arrays[name] = a if a.ndim == 2 else a.reshape(a.shape[1:])
    arrays.update(_tables())
    t = {name: nc.dram_tensor(name, a.shape, mybir.dt.from_np(a.dtype), kind="ExternalInput").ap() for name, a in arrays.items()}
    out = nc.dram_tensor("out", (S, D), mybir.dt.float32, kind="ExternalOutput").ap()
    layer(nc, t, out)
    r = run_bass_kernel_spmd(nc, [arrays], core_ids=[0])
    return r.results[0]["out"].reshape(1, S, D)
```

```python
import concourse.bass as bass
from concourse import mybir
from contextlib import ExitStack

P = 128
D = 1024
S = 1024
H = 512
KC = D // P
FF = 2816
ITER = FF // (2 * P)
HEAD = 64
NH = 8
WIN = (2, 4, 8, 16)
PAD = 16
ALPHA = 2.0 ** 0.25
EPS = 1e-5
NVEC = 9
IN_W = 1280
IN_PAIRS = 5
OUT_PAIRS = 4
PAIR0 = (0, 2 * ITER + 2 * IN_PAIRS + 2 * OUT_PAIRS)
MIX0 = 2 * ITER
ADA_EARLY = 2
QW = D // 4
ADA_UNITS = NVEC - ADA_EARLY

V_BADA, V_LN, V_BOUT, V_BIN, V_PS = 0, 72, 120, 128, 138
NV = 142
C_A, C_B, C_AG, C_AB, C_GATE, C_N = 0, 8, 16, 24, 32, 40

Q, K, V, PL = "q", "k", "v", "p"
Z_ORDER = ([(K, 0), (V, 0), (Q, 0), (Q, 1), (Q, 2), (Q, 3), (PL, 0), (PL, 1), (PL, 2), (PL, 3)],
           [(K, 0), (V, 0), (PL, 0), (PL, 1), (PL, 2), (PL, 3), (Q, 0), (Q, 1), (Q, 2), (Q, 3)])
Z_COL = {Q: 0, K: 4, V: 5, PL: 6}
Z_DMAS = {Q: 2, K: 1, V: 1, PL: 1}
NZ = 10
OUT0 = 2 * NZ
OUT_DMAS = 3


def pair_dmas(n):
    if n < MIX0 or n >= PAIR0[1]:
        return 2
    m = 2 * (n - MIX0)
    if m < OUT0:
        return sum(Z_DMAS[Z_ORDER[m // NZ][m % NZ + j][0]] for j in range(2))
    return 2 * OUT_DMAS


def raw_count(n):
    return 16 * sum(pair_dmas(x) for x in range(n % 2, n + 1, 2))


def win_count(r):
    return sum(q % 4 + 1 for q in range(r + 1))


POOL_SLOT = {1: 0, 2: 1, 3: 2, 4: 3, NZ + 1: 4, NZ + 3: 5, NZ + 5: 6, NZ + 7: 7}
OUT_SLOT = {NZ + x: m for m, x in enumerate((0, 1, 2, 3, 5, 6, 7, 8))}
SLOTS = NZ + 9
GROUP_SLOT = {x: x if x < 8 else x - 2 for x in list(range(8)) + list(range(NZ, NZ + 8))}


def sum_count(s):
    return (KC - 1) * (s + 1) if s < 1 else (KC - 1) * s + 1


def above(eng, sem, n):
    if not isinstance(n, int) or n > 0:
        eng.wait_ge(sem, n)


def layer(nc, t, o_out):
    f32, f32r, u32 = mybir.dt.float32, mybir.dt.float32r, mybir.dt.uint32
    ALU, ACT, AX = mybir.AluOpType, mybir.ActivationFunctionType, mybir.AxisListType
    cur = [(nc.sbuf_base + 31) // 32 * 32]

    def at(name, shape, dtype, offset=None):
        size = 4
        for x in shape[1:]:
            size *= x
        if offset is None:
            offset = cur[0]
            cur[0] += (size + 31) // 32 * 32
        return nc.alloc_sbuf_tensor_at(name, shape, dtype, offset=offset)

    u_at = cur[0]
    u_hi = at("u_hi", [P, KC, S], f32r)
    u_lo = at("u_lo", [P, KC, S], f32r)
    acc = at("acc", [P, KC, S], f32)
    w_raw = [at(f"w_raw{s}", [P, 2, KC, P], f32) for s in range(2)]
    w_hi = [at(f"w_hi{s}", [P, 2, KC, P], f32r) for s in range(2)]
    w_lo = [at(f"w_lo{s}", [P, 2, KC, P], f32r) for s in range(2)]
    hid = at("hid", [P, 4, PAD + H], f32)
    scratch = at("scratch", [P, 3, D], f32)
    ident = at("ident", [P, P], f32)
    ones = at("ones", [P, P], f32)
    mean_w = at("mean_w", [P, P], f32)
    vec = at("vec", [P, NV], f32)
    mods = at("mods", [P, NVEC * KC], f32)
    coef = at("coef", [P, 4 * C_N], f32)
    c_act = at("c_act", [P, KC], f32)
    small = at("small", [P, 64], f32)
    half_pow = small[:, 0:4]
    var_eps = small[:, 4:8]
    rstd = small[:, 8:12]
    row_max, neg_max, sink_sh, sink_exp = (small[:, 12 + 4 * i:16 + 4 * i] for i in range(4))
    row_sum, denom, recip = (small[:, 28 + 4 * i:32 + 4 * i] for i in range(3))
    sinks, neg_sinks = small[:, 40:48], small[:, 48:56]
    over = cur[0]
    g_hi = at("g_hi", [P, 2, 2, H], f32r)
    g_lo = at("g_lo", [P, 2, 2, H], f32r)
    w2_hi = at("w2_hi", [P, 2, D], f32r)
    w2_lo = at("w2_lo", [P, 2, D], f32r)
    w2_raw = at("w2_raw", [P, 2, D], f32)
    assert cur[0] <= nc.sbuf_usable_end, (cur[0], nc.sbuf_usable_end)
    x_nat = at("x_nat", [P, S // P, D], f32, over)
    early_sb = [at(f"early{v}", [P, KC, S], f32, u_at + v * KC * S * 4) for v in range(ADA_EARLY)]
    x_u32 = at("x_u32", [P, 2, H], f32, over + 4096)
    vec_rows = [at(f"vec_rows{r}", [P, P], f32, cur[0] - 8192 + 512 * r) for r in range(2)]
    c_rows = at("c_rows", [KC, P], f32, cur[0] - 8192 + 1024)
    ffn_end = cur[0]
    cur[0] = over
    q_sb = at("q_sb", [P, 4, H], f32)
    k_sb = at("k_sb", [P, S], f32)
    v_sb = at("v_sb", [P, S // P, P], f32)
    v_tr = hid[:, 1, 0:H]
    rope = at("rope", [P, 2, H], f32)
    probs = at("probs", [P, 2, 4, P], f32)
    pt = at("pt", [P, 2, 4, P], f32)
    pool_in = at("pool_in", [P, 4, PAD + H], f32)
    w_pool = at("w_pool", [P, 4, P], f32)
    own_mask = at("own_mask", [P, P], f32)
    own_t = at("own_t", [P, 2, P], f32)
    inv_cnt = at("inv_cnt", [P, 4, PAD], f32)
    assert cur[0] <= nc.sbuf_usable_end, (cur[0], nc.sbuf_usable_end)

    ctx = ExitStack()
    with ctx:
        ps = ctx.enter_context(nc.psum_tensor("ps", [P, 8, H], f32))

        def sem(name):
            return ctx.enter_context(nc.semaphore(name))

        c_in, c_tr, vec_in, x_in1 = sem("c_in"), sem("c_tr"), sem("vec_in"), sem("x_in1")
        x_in0 = [sem("x_in00"), sem("x_in01")]
        ada_in = [sem(f"ada_in{i}") for i in range(16)]
        early_acc, early_ps, early_ok = sem("early_acc"), sem("early_ps"), sem("early_ok")
        bada_in = sem("bada_in")
        const_ok, small_ok = sem("const_ok"), sem("small_ok")
        vec_t, vec_ok, cact_ok = sem("vec_t"), sem("vec_ok"), sem("cact_ok")
        mod_ok, coef_ok = sem("mod_ok"), sem("coef_ok")
        x_tr = sem("x_tr")
        raw_in = [sem("raw_in0"), sem("raw_in1")]
        wh_ok, wl_ok = sem("wh_ok"), sem("wl_ok")
        w2_in, w2h_ok, w2l_ok = sem("w2_in"), sem("w2h_ok"), sem("w2l_ok")
        ab_done, silu_ok, g_ok, gh_ok, gl_ok = (sem(n) for n in ("ab_done", "silu_ok", "g_ok", "gh_ok", "gl_ok"))
        f_done, f_used = sem("f_done"), sem("f_used")
        ada_tile = [sem("ada_tile0"), sem("ada_tile1")]
        ada_acc, ada_red = sem("ada_acc"), sem("ada_red")
        even_sum, odd_sum = sem("even_sum"), sem("odd_sum")
        ln_sum, ln_mean, ln_cent, ln_sq, sq_used = (sem(n) for n in ("ln_sum", "ln_mean", "ln_cent", "ln_sq", "sq_used"))
        ln_var, ln_veps, ln_rstd, ln_diag, ln_bc, ln_t = (sem(n) for n in ("ln_var", "ln_veps", "ln_rstd", "ln_diag", "ln_bc", "ln_t"))
        u32_ok, uh_ok, ul_ok, acc_ok = (sem(n) for n in ("u32_ok", "uh_ok", "ul_ok", "acc_ok"))
        z_done, z_used, o_used = sem("z_done"), sem("z_used"), sem("o_used")
        sink_in, tab_in, rope_in, mask_ok, sink_ok = sem("sink_in"), sem("tab_in"), sem("rope_in"), sem("mask_ok"), sem("sink_ok")
        shuf_ok, rope_s, rope_c, rope_ok = sem("shuf_ok"), sem("rope_s"), sem("rope_c"), sem("rope_ok")
        v_t, v_ok = sem("v_t"), sem("v_ok")
        win_ok, short_ok, diff_ok, carry_ok = sem("win_ok"), sem("short_ok"), sem("diff_ok"), sem("carry_ok")
        pool_done, ph_ok, pl_ok = sem("pool_done"), sem("ph_ok"), sem("pl_ok")
        sc_done, prev_ok, sel_ok, max_ok, neg_ok, sd_ok = (sem(n) for n in ("sc_done", "prev_ok", "sel_ok", "max_ok", "neg_ok", "sd_ok"))
        exp_ok, den_ok, rec_ok, prob_ok = sem("exp_ok"), sem("den_ok"), sem("rec_ok"), sem("prob_ok")
        t_done, pt_ok, pv_done, yh_ok, yl_ok = (sem(n) for n in ("t_done", "pt_ok", "pv_done", "yh_ok", "yl_ok"))
        fin_ok, fin_t = sem("fin_ok"), sem("fin_t")
        fin_sb = [sem("fin_sb0"), sem("fin_sb1")]
        stored = [sem(f"stored{i}") for i in range(4)]

        def tok(h):
            return slice(h * H, (h + 1) * H)

        def early_part(v, q):
            return early_sb[v][:, :, H + q % 2 * QW:H + (q % 2 + 1) * QW]

        def new_input(st, c):
            if st == 0:
                return acc[:, c, tok(1)]
            return x_u32[:, c % 2] if st == 1 else scratch[:, 1 + c % 2, 0:H]

        w1 = (t["ffn1_w1"], t["ffn2_w1"])
        w3 = (t["ffn1_w3"], t["ffn2_w3"])
        w2 = (t["ffn1_w2"], t["ffn2_w2"])

        def load_ffn_pair(sp, f, i, j):
            for a, w in enumerate((w1[f], w3[f])):
                src = w.rearrange("(k p) n -> p k n", p=P)[:, :, bass.ds(i * (2 * P) + j * P, P)]
                sp.dma_start(w_raw[j][:, a], src).then_inc(raw_in[j], 16)

        def load_w2(sp, f, i):
            src = w2[f].rearrange("(m j p) n -> m p j n", p=P, j=2)[bass.ds(i, 1)]
            sp.dma_start(w2_raw[:, :, :], src.rearrange("m p j n -> (m p) j n")).then_inc(w2_in, 16)

        def load_mix_pair(sp, n):
            for j in range(2):
                m = 2 * (n - MIX0) + j
                dst = w_raw[n % 2][:, j]
                if m < OUT0:
                    kind, c = Z_ORDER[m // NZ][m % NZ]
                    src = t["w_in"].rearrange("(k p) n -> p k n", p=P)
                    if kind == Q:
                        for a in range(2):
                            col = (4 * a + c) * HEAD
                            sp.dma_start(dst[:, :, a * HEAD:(a + 1) * HEAD], src[:, :, col:col + HEAD]).then_inc(raw_in[n % 2], 16)
                    else:
                        col = (Z_COL[kind] + c) * P
                        sp.dma_start(dst, src[:, :, col:col + P]).then_inc(raw_in[n % 2], 16)
                else:
                    col = (m - OUT0) % KC * P
                    wo = t["w_out"][:, col:col + P]
                    for a in range(2):
                        src = wo[a * 4 * HEAD:(a + 1) * 4 * HEAD].rearrange("(c d) n -> d c n", d=HEAD)
                        sp.dma_start(dst[a * HEAD:(a + 1) * HEAD, 0:4], src).then_inc(raw_in[n % 2], 16)
                    src = wo[NH * HEAD:].rearrange("(k p) n -> p k n", p=P)
                    sp.dma_start(dst[:, 4:8], src).then_inc(raw_in[n % 2], 16)

        block = ctx.enter_context(nc.Block())

        @block.sync
        def _(sp):
            x_rows = t["x"].rearrange("(b p) n -> p b n", p=P)
            for j in range(2):
                load_ffn_pair(sp, 0, 0, j)
            for q in range(4):
                if q < 2:
                    cols = slice(q * H, (q + 1) * H)
                    sp.dma_start(x_nat[:, 0:4, cols], x_rows[:, 0:4, cols]).then_inc(x_in0[q], 16)
                if q >= 2:
                    sp.wait_ge(early_ps, q - 1)
                for half in range(2):
                    for v in range(2):
                        src = t["w_ada"][half * 4 * P:(half + 1) * 4 * P, v * D + q * QW:v * D + (q + 1) * QW]
                        sp.dma_start(early_part(v, q)[:, 4 * half:4 * half + 4], src.rearrange("(k p) n -> p k n", p=P)) \
                          .then_inc(ada_in[4 * q + 2 * half + v], 16)
            sp.dma_start(x_nat[:, 4:8], x_rows[:, 4:8]).then_inc(x_in1, 16)
            sp.wait_ge(vec_ok, 2)
            load_w2(sp, 0, 0)

            def prefetch(f, i, last=False):
                n = PAIR0[f] + 2 * i
                for j in range(2):
                    sp.wait_ge(wl_ok, n + 1 + j)
                    if not last:
                        load_ffn_pair(sp, f, i + 1, j)
                    elif f == 0:
                        load_mix_pair(sp, MIX0 + j)
                if not last:
                    sp.wait_ge(w2l_ok, (ITER * f + i + 1) * 2)
                    load_w2(sp, f, i + 1)

            with sp.Fori(0, ITER - 1) as i:
                prefetch(0, i)
            prefetch(0, ITER - 1, last=True)
            for n in range(MIX0 + 2, PAIR0[1]):
                sp.wait_ge(wl_ok, n - 1)
                load_mix_pair(sp, n)
            for j in range(2):
                sp.wait_ge(wl_ok, PAIR0[1] + j - 1)
                load_ffn_pair(sp, 1, 0, j)
            sp.wait_ge(yl_ok, 16)
            sp.wait_ge(pl_ok, 8)
            load_w2(sp, 1, 0)
            with sp.Fori(0, ITER - 1) as i:
                prefetch(1, i)
            for r in range(2 * KC):
                h, c = r // KC, r % KC
                sp.wait_ge(fin_sb[r % 2], r // 2 + 1)
                dst = o_out[h * H:(h + 1) * H, c * P:(c + 1) * P].rearrange("(b p) n -> p b n", p=P)
                sp.dma_start(dst, w_raw[0][:, r % 4 // 2, 4 * (r % 2):4 * (r % 2) + 4]).then_inc(stored[r % 4], 16)
            for s in range(4):
                sp.wait_ge(stored[s], 16 * (2 * KC // 4))

        @block.gpsimd
        def _(pool):
            pool.memset(ident[:, :], 0.0).then_inc(small_ok, 1)
            pool.memset(ones[:, :], 1.0).then_inc(small_ok, 1)
            pool.memset(mean_w[:, :], 1.0 / D).then_inc(small_ok, 1)
            pool.memset(half_pow, -0.5).then_inc(small_ok, 1)
            pool.wait_ge(small_ok, 4)
            pool.affine_select(out=ident[:, :], in_=ident[:, :], compare_op=ALU.not_equal, fill=1.0,
                               base=0, pattern=[[-1, P]], channel_multiplier=1).then_inc(const_ok, 1)

            wa = t["w_ada"].rearrange("(k p) n -> p k n", p=P)

            def ada_tiles(i):
                for k in range(KC):
                    above(pool, ada_acc, i * KC + k - 1)
                    pool.dma_start(scratch[:, k % 2, :], wa[:, k, bass.ds(i * D + ADA_EARLY * D, D)]).then_inc(ada_tile[k % 2], 16)

            def w_low(n):
                slot = n % 2
                pool.wait_ge(wh_ok, n + 1)
                above(pool, wl_ok, n)
                pool.tensor_tensor(w_lo[slot][:, :, :, :], w_raw[slot][:, :, :, :], w_hi[slot][:, :, :, :].bitcast(f32),
                                   ALU.subtract).then_inc(wl_ok, 1)

            pool.wait_ge(early_ps, 3)
            ada_tiles(0)
            with pool.Fori(1, ADA_UNITS) as i:
                ada_tiles(i)

            def power(s):
                pool.wait_ge(ln_veps, s + 1)
                pool.tensor_tensor(rstd, var_eps, half_pow, ALU.pow).then_inc(ln_rstd, 1)

            def rope_tables(h):
                pool.dma_start(rope[:, 0], t["rope_cos"][:, tok(h)]).then_inc(rope_in, 16)
                pool.dma_start(rope[:, 1], t["rope_sin"][:, tok(h)]).then_inc(rope_in, 16)

            def windows(r):
                h, g = r // 4, r % 4
                pool.wait_ge(z_used, NZ * h + Z_ORDER[h].index((PL, g)) + 1)
                above(pool, pool_done, r)
                src, n = pool_in[:, g], 1
                for q in range(g + 1):
                    dst = hid[:, 3 - r % 2 if (g - q) % 2 == 0 else 2 + r % 2]
                    lo = 2 * n - 1
                    if q:
                        pool.wait_ge(win_ok, win_count(r) - g - 1 + q)
                    pool.tensor_tensor(dst[:, lo:], src[:, lo:], src[:, lo - n:PAD + H - n], ALU.add).then_inc(win_ok, 1)
                    src, n = dst, 2 * n

            w_low(MIX0)
            power(0)
            w_low(MIX0 + 1)
            pool.wait_ge(f_done, ITER * 2 * KC)
            rope_tables(0)
            pool.dma_start(w_pool[:, :, :], t["w_pool"].rearrange("g c d -> c g d")).then_inc(tab_in, 16)
            pool.dma_start(inv_cnt[:, :, :], t["inv_count"]).then_inc(tab_in, 16)
            pool.memset(own_mask[:, :], 1.0).then_inc(mask_ok, 1)
            pool.memset(own_t[:, :, :], 1.0).then_inc(mask_ok, 1)
            pool.memset(pool_in[:, :, 0:PAD], 0.0).then_inc(mask_ok, 1)
            pool.wait_ge(mask_ok, 3)
            pool.affine_select(out=own_mask[:, :], in_=own_mask[:, :], compare_op=ALU.is_ge, fill=0.0,
                               base=0, pattern=[[-1, P]], channel_multiplier=1).then_inc(mask_ok, 1)
            pool.affine_select(out=own_t[:, 0], in_=own_t[:, 0], compare_op=ALU.is_ge, fill=0.0,
                               base=0, pattern=[[1, P]], channel_multiplier=-1).then_inc(mask_ok, 1)
            pool.affine_select(out=own_t[:, 1], in_=own_t[:, 1], compare_op=ALU.is_gt, fill=0.0,
                               base=0, pattern=[[-1, P]], channel_multiplier=1).then_inc(mask_ok, 1)
            w_low(MIX0 + 2)
            w_low(MIX0 + 3)
            power(1)
            w_low(MIX0 + 4)
            windows(0)
            w_low(MIX0 + 5)
            pool.wait_ge(rope_ok, 5)
            rope_tables(1)
            w_low(MIX0 + 6)
            windows(1)
            w_low(MIX0 + 7)
            windows(2)
            windows(3)
            w_low(MIX0 + 8)
            windows(4)
            w_low(MIX0 + 9)
            w_low(MIX0 + 10)
            w_low(MIX0 + 11)
            windows(5)
            w_low(MIX0 + 12)
            windows(6)
            w_low(MIX0 + 13)
            windows(7)
            for n in range(MIX0 + 14, MIX0 + 17):
                w_low(n)
            power(2)
            for n in range(MIX0 + 17, MIX0 + 20):
                w_low(n)
            power(3)
            power(4)
            total_5 = scratch[:, 0, 0:H]
            for d in range(1, KC):
                pool.wait_ge(f_used, 2 * KC * (2 * ITER - 1) + KC + d + 1)
                if d == 1:
                    pool.wait_ge(ln_mean, 5)
                else:
                    pool.wait_ge(ln_sum, sum_count(4) + d - 1)
                pool.tensor_tensor(total_5, total_5 if d > 1 else acc[:, 0, tok(1)], acc[:, d, tok(1)], ALU.add).then_inc(ln_sum, 1)
            odd = scratch[:, 2, 0:H]
            for c in range(3, KC, 2):
                pool.wait_ge(ln_sq, KC * 5 + c + 1)
                if c > 3:
                    pool.wait_ge(odd_sum, c // 2 - 1)
                pool.tensor_tensor(odd, odd if c > 3 else hid[:, 1, 0:H], hid[:, c % 4, 0:H], ALU.add).then_inc(odd_sum, 1)
            power(5)

        def split_product(pe, out, w_h, w_l, x_h, x_l, start, stop):
            pe.matmul(out, w_h, x_h, start=start, stop=False)
            pe.matmul(out, w_h, x_l, start=False, stop=False)
            return pe.matmul(out, w_l, x_h, start=False, stop=stop)

        @block.tensor
        def _(pe):
            def chunk_product(out, slot, a, h, inside=None, order=range(KC)):
                for x, k in enumerate(order):
                    mm = split_product(pe, out, w_hi[slot][:, a, k], w_lo[slot][:, a, k],
                                       u_hi[:, k, tok(h)], u_lo[:, k, tok(h)], x == 0, x == KC - 1)
                    if inside and k in inside:
                        inside[k]()
                return mm

            def staged_product(out, slot, h, stage, done, inside=None):
                for k in range(KC):
                    pe.wait_ge(ul_ok, KC * stage + k + 1)
                    for a in range(2):
                        mm = split_product(pe, ps[:, out + a], w_hi[slot][:, a, k], w_lo[slot][:, a, k],
                                           u_hi[:, k, tok(h)], u_lo[:, k, tok(h)], k == 0, k == KC - 1)
                        if k == KC - 1:
                            mm.then_inc(done, 1)
                    if inside and k in inside:
                        inside[k]()

            def up(f, i, j, h, stage=None, between=None, inside=None):
                e = 4 * (ITER * f + i) + 2 * h + j
                pe.wait_ge(wl_ok, PAIR0[f] + 2 * i + j + 1)
                above(pe, g_ok, e - 1)
                if stage is not None:
                    staged_product(2 * j, j, h, stage, ab_done, inside)
                    return
                chunk_product(ps[:, 2 * j], j, 0, h).then_inc(ab_done, 1)
                if between:
                    between()
                chunk_product(ps[:, 2 * j + 1], j, 1, h, inside).then_inc(ab_done, 1)

            def down(f, i, h, d0=0, d1=KC, early=False):
                def half_product(d, j):
                    if j == 0:
                        above(pe, f_used, 2 * KC * (ITER * f + i) + KC * h + d - 1)
                    return split_product(pe, ps[:, 4 + d % 2], w2_hi[:, j, d * P:(d + 1) * P], w2_lo[:, j, d * P:(d + 1) * P],
                                         g_hi[:, h, j], g_lo[:, h, j], j == 0, j == 1)

                if d0 == 0:
                    pe.wait_ge(gl_ok, 4 * (ITER * f + i) + 2 * h + (1 if early else 2))
                    pe.wait_ge(w2l_ok, 2 * (ITER * f + i) + 2)
                if early:
                    for d in range(2):
                        half_product(d, 0)
                    pe.wait_ge(gl_ok, 4 * (ITER * f + i) + 2 * h + 2)
                    for d in range(2):
                        half_product(d, 1).then_inc(f_done, 1)
                    d0 = 2
                for d in range(d0, d1):
                    half_product(d, 0)
                    half_product(d, 1).then_inc(f_done, 1)

            def ada_reduce(i):
                pe.wait_ge(ada_acc, KC * i + KC)
                for c in range(KC):
                    mm = pe.matmul(ps[:, 6, c:c + 1], scratch[:, 2, c * P:(c + 1) * P], ones[:, 0:1], start=True, stop=True)
                mm.then_inc(ada_red, 1)

            def mean(s):
                pe.wait_ge(ln_sum, sum_count(s))
                pe.matmul(ps[:, 6], mean_w[:, :], scratch[:, 0, 0:H], start=True, stop=True).then_inc(ln_mean, 1)

            def variance(s):
                if s < 5:
                    pe.wait_ge(sq_used, KC * (s + 1))
                else:
                    pe.wait_ge(even_sum, 4)
                for b in range(4):
                    mm = pe.matmul(ps[:, 7, b:b + 1], scratch[:, 0, H + b * P:H + (b + 1) * P], mean_w[:, 0:1], start=True, stop=True)
                mm.then_inc(ln_var, 1)

            def spread(s):
                pe.wait_ge(ln_diag, s + 1)
                pe.matmul(ps[:, 7], ones[:, :], scratch[:, 1, 0:H], start=True, stop=True).then_inc(ln_bc, 1)

            pe.wait_ge(const_ok, 1)
            pe.wait_ge(c_in, 16)
            pe.transpose(ps[:, 7, 0:KC], c_rows[:, :], ident[0:KC, 0:KC]).then_inc(c_tr, 1)
            pe.wait_ge(cact_ok, 1)
            pe.wait_ge(bada_in, 16)
            pe.transpose(ps[:, 7, 0:V_LN], vec_rows[0][0:V_LN, :], ident[0:V_LN, 0:V_LN]).then_inc(vec_t, 1)

            def x_transpose(r):
                h, c = r // KC, r % KC
                if r in (0, 4):
                    pe.wait_ge(x_in0[r // 4], 16)
                if r == KC:
                    pe.wait_ge(x_in1, 16)
                above(pe, ul_ok, r - 2)
                for b in range(4):
                    mm = pe.transpose(ps[:, 4 + r % 3, b * P:(b + 1) * P], x_nat[:, 4 * h + b, c * P:(c + 1) * P], ident[:, :])
                mm.then_inc(x_tr, 1)

            for r in range(3):
                x_transpose(r)
            def early_columns(q):
                pe.wait_ge(vec_ok, 2 if q == 3 else 1)
                above(pe, early_ok, 2 * q)
                pe.wait_ge(early_acc, 2 * KC * (q + 1))
                for c in (2 * q, 2 * q + 1):
                    for v in range(2):
                        out = ps[:, 7, v * KC + c:v * KC + c + 1]
                        col = q % 2 * H + v * QW + c % 2 * P
                        mm = pe.matmul(out, scratch[:, 2, col:col + P], ones[:, 0:1], start=True, stop=True)
                mm.then_inc(early_ps, 1)

            def four_products(k):
                if k == 0:
                    pe.wait_ge(wl_ok, 2)
                pe.wait_ge(ul_ok, k + 1)
                x_transpose(k + 3)
                for out in range(4):
                    mm = split_product(pe, ps[:, out], w_hi[out // 2][:, out % 2, k], w_lo[out // 2][:, out % 2, k],
                                       u_hi[:, k, tok(0)], u_lo[:, k, tok(0)], k == 0, k == KC - 1)
                    if k == KC - 1:
                        mm.then_inc(ab_done, 1)

            early_columns(0)
            four_products(0)
            early_columns(1)
            four_products(1)
            four_products(2)
            early_columns(2)
            pe.wait_ge(early_ok, 6)
            pe.wait_ge(vec_in, 16 * 11)
            pe.transpose(ps[:, 7, 2 * P:2 * P + NV - V_LN], vec_rows[1][0:NV - V_LN, :], ident[0:NV - V_LN, 0:NV - V_LN]).then_inc(vec_t, 1)
            four_products(3)
            four_products(4)
            early_columns(3)
            for k in range(5, KC):
                four_products(k)

            def ffn(f):
                if f == 0:
                    x_transpose(KC + 3)
                    up(0, 0, 0, 1, stage=1, inside={k: lambda r=KC + 4 + k: x_transpose(r) for k in range(4)})
                    up(0, 0, 1, 1)
                    ada_reduce(0)
                    down(0, 0, 0)
                else:
                    pe.wait_ge(o_used, 2 * KC)
                    up(1, 0, 0, 0, stage=4, inside={0: lambda: mean(3)})
                    up(1, 0, 1, 0, between=lambda: variance(3))
                    spread(3)
                    down(1, 0, 0, early=True)
                    up(1, 0, 0, 1, stage=5)
                    up(1, 0, 1, 1)

                def steady(i, ada):
                    up(f, i, 0, 0)
                    up(f, i, 1, 0)
                    down(f, i - 1, 1)
                    up(f, i, 0, 1)
                    up(f, i, 1, 1)
                    down(f, i, 0)
                    if ada:
                        ada_reduce(i)

                if f == 0:
                    with pe.Fori(1, ADA_UNITS) as i:
                        steady(i, True)
                with pe.Fori(ADA_UNITS if f == 0 else 1, ITER - 1) as i:
                    steady(i, False)
                i, s = ITER - 1, 4 * f
                up(f, i, 0, 0)
                up(f, i, 1, 0)
                down(f, i - 1, 1)
                up(f, i, 0, 1, between=lambda: down(f, i, 0), inside={2: lambda: mean(s)})
                up(f, i, 1, 1)
                variance(s)
                down(f, i, 1, 0, 3, early=True)
                spread(s)
                down(f, i, 1, 3, KC)

            def finish(r):
                h, c = r // KC, r % KC
                pe.wait_ge(fin_ok, r + 1)
                above(pe, fin_sb[r % 2], r // 2 - 1)
                for b in range(4):
                    mm = pe.transpose(ps[:, r % 4, b * P:(b + 1) * P], acc[:, c, h * H + b * P:h * H + (b + 1) * P], ident[:, :])
                mm.then_inc(fin_t, 1)

            ffn(0)

            def project(m, stage=None, inside=None):
                if m < 2:
                    pe.wait_ge(g_ok, 4 * ITER)
                elif m - 2 < OUT0:
                    pe.wait_ge(z_used, m - 1 + (stage is not None))
                else:
                    pe.wait_ge(o_used, m - 1 - OUT0)
                if m % 2 == 0:
                    pe.wait_ge(wl_ok, MIX0 + m // 2 + 1)
                h = m // NZ if m < OUT0 else (m - OUT0) // KC
                if stage is not None:
                    staged_product(0, m // 2 % 2, h, stage, z_done)
                elif m < OUT0:
                    chunk_product(ps[:, m % 2], m // 2 % 2, m % 2, h, inside).then_inc(z_done, 1)
                else:
                    inside = dict(inside or {})
                    pe.wait_ge(pl_ok, 4 * (h + 1))
                    then = inside.get(KC - 1)

                    def attention_ready():
                        if then:
                            then()
                        pe.wait_ge(yl_ok, 8 * (h + 1))
                    inside[KC - 1] = attention_ready
                    chunk_product(ps[:, m % 2], m // 2 % 2, m % 2, h, inside, list(range(4, KC)) + list(range(4))).then_inc(z_done, 1)

            def v_transposes(h):
                pe.wait_ge(z_used, NZ * h + 2)
                for b in range(4):
                    mm = pe.transpose(ps[:, 4 + 2 * h, b * P:(b + 1) * P], v_tr[:, b * P:(b + 1) * P], ident[:, :])
                mm.then_inc(v_t, 1)

            def scores(n):
                b, kv = n // 2, n % 2
                pe.wait_ge(rope_ok, 5 if n < 8 else 10)
                above(pe, sel_ok, n)
                rows = slice(kv * HEAD, (kv + 1) * HEAD)
                q0 = b % 4 * P
                for c in range(4):
                    out = ps[:, 2 + c // 2, c % 2 * 2 * P:(c % 2 + 1) * 2 * P]
                    k0, out = (0, out[:, P:]) if b == 0 else ((b - 1) * P, out)
                    mm = pe.matmul(out, q_sb[rows, c, q0:q0 + P], k_sb[rows, k0:(b + 1) * P], start=True, stop=True)
                mm.then_inc(sc_done, 1)

            def transposes(n):
                pe.wait_ge(prob_ok, n + 1)
                for c in range(4):
                    mm = pe.transpose(ps[:, 4, c * P:(c + 1) * P], probs[:, n % 2, c], ident[:, :])
                mm.then_inc(t_done, 1)

            def values(n):
                b = n // 2
                pe.wait_ge(pt_ok, 2 * n + 2)
                pe.wait_ge(v_ok, b // 4 + 1)
                above(pe, yl_ok, n)
                mm = pe.matmul(ps[:, 5], v_sb[:, b], pt[:, 0], start=True, stop=(b == 0))
                if b > 0:
                    mm = pe.matmul(ps[:, 5], v_sb[:, b - 1], pt[:, 1], start=False, stop=True)
                mm.then_inc(pv_done, 1)

            def pool_mix(r):
                pe.wait_ge(diff_ok, r + 1)
                pe.wait_ge(tab_in, 32)
                above(pe, pl_ok, r)
                pe.matmul(ps[:, 7], w_pool[:, r % 4], hid[:, 2 + r % 2, PAD:], start=True, stop=True).then_inc(pool_done, 1)

            project(0, stage=2)
            project(2, inside={5: lambda: mean(1)})
            project(3)
            v_transposes(0)
            project(4)
            project(5, inside={0: lambda: variance(1), 6: lambda: spread(1)})
            project(6)
            for m in range(7, NZ):
                project(m)
            for x in range(SLOTS):
                if x in GROUP_SLOT and x != NZ:
                    scores(GROUP_SLOT[x])
                if x == 0:
                    project(NZ, stage=3)
                elif 1 < x < NZ - 1:
                    project(NZ + x)
                elif x == NZ - 1:
                    project(NZ + x, inside={4: lambda: values(7)})
                elif x in OUT_SLOT:
                    project(OUT0 + OUT_SLOT[x])
                if x == NZ:
                    scores(8)
                if x in POOL_SLOT:
                    pool_mix(POOL_SLOT[x])
                if x == 3:
                    v_transposes(1)
                if x != NZ - 1 and x - 2 in GROUP_SLOT:
                    values(GROUP_SLOT[x - 2])
                if x - 1 in GROUP_SLOT:
                    transposes(GROUP_SLOT[x - 1])
            for m in range(KC):
                inside = {0: {5: lambda: values(15), 2: lambda: mean(2)}, 3: {1: lambda: variance(2)}, 4: {4: lambda: spread(2)}}
                project(OUT0 + KC + m, inside=inside.get(m))

            ffn(1)

            pe.wait_ge(g_ok, 8 * ITER)
            mean(5)
            for r in range(5):
                finish(r)
            variance(5)
            for r in range(5, KC):
                finish(r)
            spread(5)
            for r in range(KC, 2 * KC):
                finish(r)

        @block.scalar
        def _(act):
            def w_split(n, slot, landed, used):
                if used is not None:
                    act.wait_ge(*used)
                act.wait_ge(raw_in[slot], landed)
                act.activation(w_hi[slot][:, :, :, :], w_raw[slot][:, :, :, :], ACT.Copy).then_inc(wh_ok, 1)

            def w2_split(f, i):
                above(act, f_done, 2 * KC * (ITER * f + i))
                act.wait_ge(w2_in, 16 * (ITER * f + i + 1))
                for j in range(2):
                    act.activation(w2_hi[:, j], w2_raw[:, j], ACT.Copy).then_inc(w2h_ok, 1)

            def silu(f, i, j, h):
                e = 4 * (ITER * f + i) + 2 * h + j
                act.wait_ge(ab_done, 2 * e + 1)
                act.activation(hid[:, j, 0:H], ps[:, 2 * j], ACT.Silu).then_inc(silu_ok, 1)

            def gate_hi(f, i, j, h):
                e = 4 * (ITER * f + i) + 2 * h + j
                act.wait_ge(g_ok, e + 1)
                above(act, f_done, 2 * KC * (ITER * f + i - 1) + KC * h + KC)
                act.activation(g_hi[:, h, j], hid[:, 2 + j, 0:H], ACT.Copy).then_inc(gh_ok, 1)

            def squares(s, c0=0, c1=KC):
                h = s % 2
                for c in range(c0, c1):
                    act.wait_ge(ln_cent, KC * s + c + 1)
                    if c >= 2:
                        act.wait_ge(sq_used, KC * s + c - 1)
                    act.activation(scratch[:, 1 + c % 2, H:], acc[:, c, tok(h)], ACT.Square).then_inc(ln_sq, 1)

            def input_hi(st, c):
                h, n, cf = st % 2, KC * st + c, C_N * (st // 2)
                a, b = (coef[:, cf + x + c:cf + x + c + 1] for x in (C_A, C_B))
                if st == 0:
                    act.wait_ge(early_ok, 2 * (c // 2) + 2)
                if st < 2:
                    act.wait_ge(x_tr, n + 1)
                    src = ps[:, 4 + n % 3]
                else:
                    act.wait_ge(ln_t, n - 2 * KC + 1)
                    src = acc[:, c, tok(h)]
                above(act, ul_ok, n - 1)
                if st < 2:
                    act.activation(acc[:, c, tok(h)], src, ACT.Copy, scale=ALPHA).then_inc(acc_ok, 1)
                act.activation(new_input(st, c), src, ACT.Identity, bias=b, scale=a).then_inc(u32_ok, 1)
                act.activation(u_hi[:, c, tok(h)], src, ACT.Identity, bias=b, scale=a).then_inc(uh_ok, 1)

            def keep(st, c0=0, c1=KC):
                h, cf = st % 2, C_N * (st // 2)
                for c in range(c0, c1):
                    act.wait_ge(uh_ok, KC * st + c + 1)
                    act.activation(acc[:, c, tok(h)], acc[:, c, tok(h)], ACT.Identity, bias=coef[:, cf + C_AB + c:cf + C_AB + c + 1],
                                   scale=coef[:, cf + C_AG + c:cf + C_AG + c + 1]).then_inc(acc_ok, 1)

            def affine(h, c):
                s = 4 + h
                g, b = (vec[:, V_LN + (4 + v) * KC + c:V_LN + (4 + v) * KC + c + 1] for v in range(2))
                act.wait_ge(ln_t, KC * s + c + 1)
                act.activation(acc[:, c, tok(h)], acc[:, c, tok(h)], ACT.Identity, bias=b, scale=g).then_inc(fin_ok, 1)

            def finish(r):
                act.wait_ge(fin_t, r + 1)
                above(act, stored[r % 4], 16 * (r // 4))
                act.activation(w_raw[0][:, r % 4 // 2, 4 * (r % 2):4 * (r % 2) + 4], ps[:, r % 4].rearrange("p (b n) -> p b n", b=4),
                               ACT.Copy).then_inc(fin_sb[r % 2], 1)

            act.dma_start(c_rows[:, :], t["c"].rearrange("a (n p) -> (a n) p", p=P)).then_inc(c_in, 16)
            act.dma_start(vec_rows[0][0:V_LN, :], t["b_ada"].rearrange("a (n p) -> (a n) p", p=P)).then_inc(bada_in, 16)
            act.wait_ge(c_tr, 1)
            act.activation(c_act[:, :], ps[:, 7, 0:KC], ACT.Silu).then_inc(cact_ok, 1)
            for j in range(2):
                w_split(j, j, raw_count(j), None)
            rows = [(0, t["ln1_g"], 8), (8, t["ln1_b"], 8), (16, t["ln2_g"], 8), (24, t["ln2_b"], 8), (32, t["ln3_g"], 8),
                    (40, t["ln3_b"], 8), (V_BOUT - V_LN, t["b_out"], 8), (V_BIN - V_LN + 4, t["b_in"][:, 512:IN_W], 6),
                    (V_PS - V_LN, t["pool_scale"], 4)]
            for row, src, n in rows:
                act.dma_start(vec_rows[1][row:row + n, :], src.rearrange("a (n p) -> (a n) p", p=P)).then_inc(vec_in, 16)
            for a in range(2):
                src = t["b_in"][:, a * 256:(a + 1) * 256].rearrange("a (c d) -> (a c) d", d=HEAD)
                row = V_BIN - V_LN
                act.dma_start(vec_rows[1][row:row + 4, a * HEAD:(a + 1) * HEAD], src).then_inc(vec_in, 16)
            act.dma_start(sinks, t["attn_sinks"].broadcast_to([P, NH])).then_inc(sink_in, 16)

            def ffn(f):
                st, s = 4 * f, 4 * f - 1
                last = ITER - 1
                if f == 0:
                    for c in range(KC):
                        input_hi(0, c)
                    for c in range(3):
                        input_hi(1, c)
                    for j in range(2):
                        silu(0, 0, j, 0)
                        gate_hi(0, 0, j, 0)
                    for c in range(3, KC):
                        input_hi(1, c)
                    w2_split(0, 0)
                else:
                    squares(3)
                    silu(1, 0, 0, 0)
                    gate_hi(1, 0, 0, 0)
                    w2_split(1, 0)
                if f == 1:
                    silu(f, 0, 1, 0)
                    gate_hi(f, 0, 1, 0)
                    for c in range(KC):
                        input_hi(5, c)
                    keep(5)

                def half1(i):
                    for j in range(2):
                        silu(f, i, j, 1)
                        gate_hi(f, i, j, 1)
                        w_split(None, j, raw_count(PAIR0[f] + j) + 32 * (i + 1),
                                (ab_done, 8 * (ITER * f + i) + 6 + 2 * j))

                def steady(i):
                    for j in range(2):
                        silu(f, i, j, 0)
                        gate_hi(f, i, j, 0)
                    w2_split(f, i)
                    half1(i)

                half1(0)
                with act.Fori(1, last) as i:
                    steady(i)
                for j in range(2):
                    silu(f, last, j, 0)
                    gate_hi(f, last, j, 0)
                w2_split(f, last)
                squares(4 * f, 0, 4)
                silu(f, last, 0, 1)
                gate_hi(f, last, 0, 1)
                if f == 0:
                    w_split(MIX0, 0, raw_count(MIX0), (ab_done, 8 * last + 6))
                squares(4 * f, 4, KC)
                silu(f, last, 1, 1)
                gate_hi(f, last, 1, 1)
                if f == 0:
                    w_split(MIX0 + 1, 1, raw_count(MIX0 + 1), (ab_done, 8 * last + 8))

            ffn(0)

            def next_pair(m):
                n = MIX0 + m // 2 + 2
                w_split(n, n % 2, raw_count(n), (z_done, m + 1))

            def drain(m):
                h = m // NZ
                kind, c = Z_ORDER[h][m % NZ]
                act.wait_ge(z_done, m + 1)
                if kind == Q:
                    if h == 1:
                        act.wait_ge(sc_done, 8)
                    dst = q_sb[:, c]
                elif kind == K:
                    dst = k_sb[:, tok(h)]
                elif kind == V:
                    above(act, v_t, h)
                    dst = v_tr
                else:
                    if h == 1:
                        act.wait_ge(carry_ok, c + 1)
                    dst = pool_in[:, c, PAD:]
                col = V_BIN + Z_COL[kind] + c
                act.activation(dst, ps[:, m % 2], ACT.Identity, bias=vec[:, col:col + 1]).then_inc(z_used, 1)

            def v_store(h):
                act.wait_ge(v_t, h + 1)
                act.activation(v_sb[:, 4 * h:4 * h + 4], ps[:, 4 + 2 * h].rearrange("p (b n) -> p b n", b=4), ACT.Copy).then_inc(v_ok, 1)

            def banded(block_of):
                return ps[:, 2:4].rearrange("p b (c k) -> p (b c) k", c=2)[:, :, block_of * P:(block_of + 1) * P]

            def before_scores(n):
                if n >= 2:
                    act.wait_ge(sc_done, n + 1)
                    act.wait_ge(t_done, n - 1)
                    act.activation(probs[:, n % 2], banded(0), ACT.Copy).then_inc(prev_ok, 1)

            def exps(n):
                act.wait_ge(sel_ok, n + 1)
                act.wait_ge(neg_ok, n + 1)
                for c in range(4):
                    act.activation(probs[:, n % 2, c], probs[:, n % 2, c], ACT.Exp, bias=neg_max[:, c:c + 1], scale=HEAD ** -0.5,
                                   accum_out=row_sum[:, c:c + 1]).then_inc(exp_ok, 1)
                act.wait_ge(sd_ok, n + 1)
                act.activation(sink_exp, sink_sh, ACT.Exp).then_inc(exp_ok, 1)

            def attn_hi(n):
                b, rows = n // 2, slice(n % 2 * HEAD, (n % 2 + 1) * HEAD)
                act.wait_ge(pv_done, n + 1)
                act.activation(u_hi[rows, 0:4, b * P:(b + 1) * P], ps[rows, 5].rearrange("p (c q) -> p c q", c=4), ACT.Copy).then_inc(yh_ok, 1)

            def pool_hi(r):
                h, g = r // 4, r % 4
                act.wait_ge(pool_done, r + 1)
                act.activation(u_hi[:, 4 + g, tok(h)], ps[:, 7], ACT.Copy, scale=vec[:, V_PS + g:V_PS + g + 1]).then_inc(ph_ok, 1)

            for c in range(KC):
                input_hi(2, c)
            drain(0)
            drain(1)
            next_pair(1)
            drain(2)
            squares(1, 0, 4)
            drain(3)
            next_pair(3)
            squares(1, 4, KC)
            v_store(0)
            drain(4)
            drain(5)
            next_pair(5)
            input_hi(3, 0)
            drain(6)
            for c in range(1, KC):
                input_hi(3, c)
                if c == 3:
                    drain(7)
                if c == 5:
                    next_pair(7)
            drain(8)
            drain(9)
            next_pair(9)
            for x in range(SLOTS):
                if x in GROUP_SLOT:
                    before_scores(GROUP_SLOT[x])
                    exps(GROUP_SLOT[x])
                if x == 0:
                    drain(NZ)
                    drain(NZ + 1)
                elif 1 < x < NZ and x != 6:
                    if x == 7:
                        drain(NZ + 6)
                    drain(NZ + x)
                if x in POOL_SLOT:
                    pool_hi(POOL_SLOT[x])
                if x == 3:
                    v_store(1)
                if x < KC:
                    keep(2, x, x + 1)
                    keep(3, x, x + 1)
                if x - 2 in GROUP_SLOT:
                    attn_hi(GROUP_SLOT[x - 2])
                if x < NZ and x % 2 == 1:
                    next_pair(NZ + x if x > 1 else NZ + 1)
                if x in OUT_SLOT and OUT_SLOT[x] % 2 == 1:
                    next_pair(OUT0 + OUT_SLOT[x])
            attn_hi(15)
            squares(2)
            next_pair(OUT0 + KC + 1)
            next_pair(OUT0 + KC + 3)
            for c in range(KC):
                input_hi(4, c)
                if c == 5:
                    next_pair(OUT0 + KC + 5)
            keep(4)
            next_pair(OUT0 + KC + 7)

            ffn(1)
            for c in range(KC):
                affine(0, c)
            for c in range(KC):
                act.wait_ge(ln_cent, KC * 5 + c + 1)
                if c >= 4:
                    act.wait_ge(odd_sum if c % 2 else even_sum, 1)
                act.activation(hid[:, c % 4, 0:H], acc[:, c, tok(1)], ACT.Square).then_inc(ln_sq, 1)
                if c % 2 == 1:
                    finish(c // 2)
            for r in range(4, KC):
                finish(r)
            affine(1, 0)
            for c in range(1, KC):
                affine(1, c)
                if c % 2 == 1:
                    finish(KC + c - 1)

        @block.vector
        def _(dve):
            f = f32

            def w_low(slot, n):
                dve.wait_ge(wh_ok, n + 1)
                dve.tensor_tensor(w_lo[slot][:, :, :, :], w_raw[slot][:, :, :, :], w_hi[slot][:, :, :, :].bitcast(f),
                                  ALU.subtract).then_inc(wl_ok, 1)

            def w2_low(f_, i):
                for j in range(2):
                    dve.wait_ge(w2h_ok, 2 * (ITER * f_ + i) + j + 1)
                    dve.tensor_tensor(w2_lo[:, j], w2_raw[:, j], w2_hi[:, j].bitcast(f), ALU.subtract).then_inc(w2l_ok, 1)

            def gated(f_, i, j, h, between=None):
                e = 4 * (ITER * f_ + i) + 2 * h + j
                dve.wait_ge(silu_ok, e + 1)
                dve.wait_ge(ab_done, 2 * e + 2)
                above(dve, gl_ok, e - 1)
                dve.tensor_tensor(hid[:, 2 + j, 0:H], hid[:, j, 0:H], ps[:, 2 * j + 1], ALU.mult).then_inc(g_ok, 1)
                if between:
                    between()
                dve.wait_ge(gh_ok, e + 1)
                dve.tensor_tensor(g_lo[:, h, j], hid[:, 2 + j, 0:H], g_hi[:, h, j].bitcast(f), ALU.subtract).then_inc(gl_ok, 1)

            def add_total(s, d, used):
                if d == 0:
                    return
                dve.wait_ge(*used)
                own = sum_count(s - 1) if s else 0
                first = scratch[:, 0, 0:H] if d > 1 else acc[:, 0, tok(s % 2)]
                above(dve, ln_mean, s)
                above(dve, ln_sum, own + d - 1)
                dve.tensor_tensor(scratch[:, 0, 0:H], first, acc[:, d, tok(s % 2)], ALU.add).then_inc(ln_sum, 1)

            def residual(f_, i, h, d0=0, d1=KC, s=None):
                cf = C_N * (0 if f_ == 0 else 2) + C_GATE
                for d in range(d0, d1):
                    q = 2 * KC * (ITER * f_ + i) + KC * h + d
                    dve.wait_ge(f_done, q + 1)
                    above(dve, f_used, q + 1 - KC)
                    dve.scalar_tensor_tensor(acc[:, d, tok(h)], ps[:, 4 + d % 2], coef[:, cf + d:cf + d + 1], acc[:, d, tok(h)],
                                             ALU.mult, ALU.add).then_inc(f_used, 1)
                    if s is not None:
                        add_total(s, d, (f_used, q + 1))

            def ada_step(i, k):
                dve.wait_ge(ada_tile[k % 2], 16 * (4 * i + k // 2 + 1))
                if k == 0:
                    above(dve, ada_red, i)
                    dve.tensor_scalar(scratch[:, 2], scratch[:, k % 2], c_act[:, k:k + 1], None, ALU.mult).then_inc(ada_acc, 1)
                else:
                    dve.wait_ge(ada_acc, KC * i + k)
                    dve.scalar_tensor_tensor(scratch[:, 2], scratch[:, k % 2], c_act[:, k:k + 1], scratch[:, 2],
                                             ALU.mult, ALU.add).then_inc(ada_acc, 1)

            def ada_store(i):
                dve.wait_ge(ada_red, i + 1)
                cols = bass.ds(i * KC + ADA_EARLY * KC, KC)
                dve.tensor_tensor(mods[:, cols], ps[:, 6, 0:KC], vec[:, cols], ALU.add).then_inc(mod_ok, 1)

            chain = [0]

            def coef_op(what, *args):
                what(*args).then_inc(coef_ok, 1)
                chain[0] += 1
                dve.wait_ge(coef_ok, chain[0])

            def coefs(st):
                cf = C_N * st
                sh, sc, gt = (mods[:, (3 * st + v) * KC:(3 * st + v + 1) * KC] for v in range(3))
                a, b, ag, ab, gate = (coef[:, cf + x:cf + x + KC] for x in (C_A, C_B, C_AG, C_AB, C_GATE))
                g, beta = (vec[:, V_LN + (2 * (st - 1) + v) * KC:V_LN + (2 * (st - 1) + v + 1) * KC] for v in range(2))
                coef_op(dve.tensor_scalar, a, sc, 1.0, None, ALU.add)
                coef_op(dve.tensor_tensor, b, beta, a, ALU.mult)
                coef_op(dve.tensor_tensor, b, b, sh, ALU.add)
                coef_op(dve.tensor_tensor, a, a, g, ALU.mult)
                coef_op(dve.tensor_scalar, gate, gt, 1.0, None, ALU.add)
                coef_op(dve.tensor_scalar, ag, g, ALPHA, None, ALU.mult)
                coef_op(dve.tensor_scalar, ab, beta, ALPHA, None, ALU.mult)
                if st == 1:
                    bias = vec[:, V_BOUT:V_BOUT + KC]
                    coef_op(dve.tensor_tensor, small[:, 56:64], gate, bias, ALU.mult)
                    coef_op(dve.tensor_tensor, ab, ab, small[:, 56:64], ALU.add)
                else:
                    coef_op(dve.tensor_scalar, gate, gate, 0.5, None, ALU.mult)

            def total(s):
                h = s % 2
                dve.tensor_reduce(scratch[:, 0, 0:H], acc[:, :, tok(h)].rearrange("p c n -> p n c"), AX.X, ALU.add).then_inc(ln_sum, 1)

            def add_square(s, c):
                sq, sq_sum = scratch[:, 1 + c % 2, H:], scratch[:, 0, H:]
                dve.wait_ge(ln_sq, KC * s + c + 1)
                if c == 0:
                    dve.tensor_copy(sq_sum, sq).then_inc(sq_used, 1)
                else:
                    dve.wait_ge(sq_used, KC * s + c)
                    dve.tensor_tensor(sq_sum, sq_sum, sq, ALU.add).then_inc(sq_used, 1)

            def centre(s, c0=0, c1=KC):
                h = s % 2
                dve.wait_ge(ln_mean, s + 1)
                for c in range(c0, c1):
                    dve.tensor_tensor(acc[:, c, tok(h)], acc[:, c, tok(h)], ps[:, 6], ALU.subtract).then_inc(ln_cent, 1)
                    if c >= 2:
                        add_square(s, c - 2)
                if c1 == KC:
                    add_square(s, KC - 2)
                    add_square(s, KC - 1)

            def deviation(s):
                dve.wait_ge(ln_var, s + 1)
                dve.tensor_scalar(var_eps, ps[:, 7, 0:4], EPS, None, ALU.add).then_inc(ln_veps, 1)

            def diagonal(s):
                dve.wait_ge(ln_rstd, s + 1)
                dve.tensor_tensor(scratch[:, 1, 0:H].rearrange("p (b n) -> p b n", b=4),
                                  ident[:, :].unsqueeze(1).broadcast_to([P, 4, P]),
                                  rstd.unsqueeze(2).broadcast_to([P, 4, P]), ALU.mult).then_inc(ln_diag, 1)

            def normal(s, c):
                if c == 0:
                    dve.wait_ge(ln_bc, s + 1)
                src = acc[:, c, tok(s % 2)]
                dve.tensor_tensor(src, src, ps[:, 7], ALU.mult).then_inc(ln_t, 1)

            def input_chunks(st, c0=0, c1=KC):
                h, cf = st % 2, C_N * (st // 2)

                def low(c):
                    dve.wait_ge(uh_ok, KC * st + c + 1)
                    dve.wait_ge(u32_ok, KC * st + c + 1)
                    dve.tensor_tensor(u_lo[:, c, tok(h)], new_input(st, c), u_hi[:, c, tok(h)].bitcast(f),
                                      ALU.subtract).then_inc(ul_ok, 1)

                for c in range(c0, c1):
                    if st < 2:
                        low(c)
                        continue
                    normal(st - 2, c)
                    if c >= 1:
                        low(c - 1)
                if c1 == KC and st >= 2:
                    low(KC - 1)

            def finish(r):
                dve.wait_ge(fin_t, r + 1)
                above(dve, stored[r % 4], 16 * (r // 4))
                dve.tensor_copy(w_raw[0][:, r % 4 // 2, 4 * (r % 2):4 * (r % 2) + 4],
                                ps[:, r % 4].rearrange("p (b n) -> p b n", b=4)).then_inc(fin_sb[r % 2], 1)

            for j in range(2):
                w_low(j, j)
            dve.wait_ge(cact_ok, 1)
            for q in range(4):
                for k in range(KC):
                    for v in range(2):
                        partial = scratch[:, 2, q % 2 * H + v * QW:q % 2 * H + (v + 1) * QW]
                        row_block = early_part(v, q)[:, k]
                        if k % 4 == 0:
                            dve.wait_ge(ada_in[4 * q + k // 4 * 2 + v], 16)
                        if k == 0:
                            dve.tensor_scalar(partial, row_block, c_act[:, k:k + 1], None, ALU.mult).then_inc(early_acc, 1)
                        else:
                            dve.wait_ge(early_acc, 2 * (KC * q + k) + v - 1)
                            dve.scalar_tensor_tensor(partial, row_block, c_act[:, k:k + 1], partial, ALU.mult, ALU.add).then_inc(early_acc, 1)
                    if q and k in (1, 3):
                        input_chunks(0, 2 * q - 2 + k // 2, 2 * q - 1 + k // 2)
                if q == 0:
                    dve.wait_ge(vec_t, 1)
                    dve.tensor_copy(vec[:, 0:V_LN], ps[:, 7, 0:V_LN]).then_inc(vec_ok, 1)
                    dve.wait_ge(vec_ok, 1)
                if q == 3:
                    dve.wait_ge(vec_t, 2)
                    dve.tensor_copy(vec[:, V_LN:], ps[:, 7, 2 * P:2 * P + NV - V_LN]).then_inc(vec_ok, 1)
                dve.wait_ge(early_ps, q + 1)
                for v, c0, plus in ((1, C_A, 1.0), (0, C_B, 0.0)):
                    dve.scalar_tensor_tensor(coef[:, c0 + 2 * q:c0 + 2 * q + 2], ps[:, 7, v * KC + 2 * q:v * KC + 2 * q + 2], plus,
                                             vec[:, v * KC + 2 * q:v * KC + 2 * q + 2], ALU.add, ALU.add).then_inc(early_ok, 1)
            input_chunks(0, 6, KC)
            dve.wait_ge(sink_in, 16)
            dve.tensor_scalar(neg_sinks, sinks, -1.0, None, ALU.mult).then_inc(sink_ok, 1)
            dve.wait_ge(vec_ok, 2)

            def ffn(f_):
                last = ITER - 1
                if f_ == 0:
                    ada_step(0, 0)
                    input_chunks(1, 0, 1)
                    ada_step(0, 1)
                    input_chunks(1, 1, 3)
                    gated(0, 0, 0, 0)
                    gated(0, 0, 1, 0)
                    input_chunks(1, 3, 4)
                    ada_step(0, 2)
                    input_chunks(1, 4, 6)
                    ada_step(0, 3)
                    input_chunks(1, 6, KC)
                    ada_step(0, 4)
                    w2_low(0, 0)
                    for k in range(5, 7):
                        ada_step(0, k)
                    gated(0, 0, 0, 1)
                    ada_step(0, 7)
                    w_low(0, 2)
                    gated(0, 0, 1, 1)
                    ada_store(0)
                    dve.wait_ge(mod_ok, 1)
                    coef_op(dve.tensor_scalar, coef[:, C_GATE:C_GATE + KC], mods[:, 2 * KC:3 * KC], 1.0, None, ALU.add)
                    coef_op(dve.tensor_scalar, coef[:, C_GATE:C_GATE + KC], coef[:, C_GATE:C_GATE + KC], 0.5, None, ALU.mult)
                else:
                    centre(3)
                    gated(1, 0, 0, 0)
                    w2_low(1, 0)
                    deviation(3)
                    diagonal(3)
                    gated(1, 0, 1, 0)
                    dve.wait_ge(acc_ok, KC * 5)
                    for c in range(KC):
                        residual(1, 0, 0, c, c + 1)
                        if c % 2 == 1:
                            input_chunks(5, c // 2, c // 2 + 1)
                    input_chunks(5, 4, KC)
                    dve.wait_ge(acc_ok, KC * 6)

                def half1(i, ada=False):
                    gated(f_, i, 0, 1)
                    w_low(0, PAIR0[f_] + 2 * i + 2)
                    if ada:
                        for k in range(6, KC):
                            ada_step(i, k)
                    if isinstance(i, int):
                        gated(f_, i, 1, 1)
                    else:
                        gated(f_, i, 1, 1, between=lambda: residual(f_, i, 0, 0, 1))
                        residual(f_, i, 0, 1, KC)
                    w_low(1, PAIR0[f_] + 2 * i + 3)

                if f_ == 0:
                    residual(0, 0, 0)
                    w_low(1, 3)
                else:
                    half1(0)

                def steady(i, ada):
                    gated(f_, i, 0, 0)
                    if ada:
                        for k in range(0, 3):
                            ada_step(i, k)
                    gated(f_, i, 1, 0, between=lambda: residual(f_, i - 1, 1, 0, 1))
                    residual(f_, i - 1, 1, 1, KC)
                    w2_low(f_, i)
                    if ada:
                        for k in range(3, 6):
                            ada_step(i, k)
                    half1(i, ada)
                    if ada:
                        ada_store(i)

                if f_ == 0:
                    with dve.Fori(1, ADA_UNITS) as i:
                        steady(i, True)
                    dve.wait_ge(mod_ok, ADA_UNITS)
                    coefs(1)
                    coefs(2)
                with dve.Fori(ADA_UNITS if f_ == 0 else 1, last) as i:
                    steady(i, False)
                s = 4 * f_
                gated(f_, last, 0, 0)
                gated(f_, last, 1, 0, between=lambda: residual(f_, last - 1, 1, 0, 1))
                residual(f_, last - 1, 1, 1, KC)
                w2_low(f_, last)
                residual(f_, last, 0, s=s)
                centre(s, 0, 4)
                gated(f_, last, 0, 1)
                centre(s, 4, KC)
                gated(f_, last, 1, 1)
                residual(f_, last, 1, 0, 1)
                deviation(s)
                diagonal(s)
                if f_ == 0:
                    residual(0, last, 1, 1, 4)
                    for c in range(4, KC):
                        residual(0, last, 1, c, c + 1)
                        input_chunks(2, c - 4, c - 3)
                    input_chunks(2, 4, KC)
                else:
                    residual(1, last, 1, 1, 3)
                    for c in range(3, KC):
                        residual(1, last, 1, c, c + 1)
                        normal(4, c - 3)

            ffn(0)

            def rotate(r, x):
                h = r // 5
                dve.wait_ge(rope_in, 32 * (h + 1))
                tmp = hid[:, 0, 0:H]
                above(dve, rope_ok, r)
                half = HEAD // 8
                swap = [i + half for i in range(half)] + list(range(half)) + list(range(2 * half, 32))
                dve.stream_shuffle(in_=x, out=tmp, mask=swap).then_inc(shuf_ok, 1)
                dve.wait_ge(shuf_ok, r + 1)
                dve.tensor_tensor(tmp, tmp, rope[:, 1], ALU.mult).then_inc(rope_s, 1)
                dve.tensor_tensor(x, x, rope[:, 0], ALU.mult).then_inc(rope_c, 1)
                dve.wait_ge(rope_s, r + 1)
                dve.wait_ge(rope_c, r + 1)
                dve.tensor_tensor(x, x, tmp, ALU.add).then_inc(rope_ok, 1)

            def rotate_unit(m):
                h = m // NZ
                kind, c = Z_ORDER[h][m % NZ]
                dve.wait_ge(z_used, m + 1)
                rotate(5 * h + (0 if kind == K else 1 + c), k_sb[:, tok(h)] if kind == K else q_sb[:, c])

            shorts = [0]

            def differences(r):
                h, g = r // 4, r % 4
                x, src, out = pool_in[:, g], hid[:, 3 - r % 2], hid[:, 2 + r % 2]
                dve.wait_ge(win_ok, win_count(r))
                first = PAD if h == 0 else 0
                if h == 0:
                    dve.wait_ge(tab_in, 32)
                    dve.tensor_tensor(out[:, PAD:2 * PAD], src[:, PAD:2 * PAD], inv_cnt[:, g], ALU.mult).then_inc(short_ok, 1)
                    shorts[0] += 1
                    dve.wait_ge(short_ok, shorts[0])
                    dve.tensor_tensor(out[:, PAD:2 * PAD], out[:, PAD:2 * PAD], x[:, PAD:2 * PAD], ALU.subtract).then_inc(short_ok, 1)
                    shorts[0] += 1
                dve.scalar_tensor_tensor(out[:, PAD + first:], src[:, PAD + first:], 1.0 / WIN[g], x[:, PAD + first:],
                                         ALU.mult, ALU.subtract).then_inc(diff_ok, 1)
                if h == 0:
                    dve.wait_ge(diff_ok, r + 1)
                    dve.tensor_copy(x[:, 0:PAD], x[:, H:H + PAD]).then_inc(carry_ok, 1)

            def pool_low(r):
                h, g = r // 4, r % 4
                dve.wait_ge(ph_ok, r + 1)
                dve.scalar_tensor_tensor(u_lo[:, 4 + g, tok(h)], ps[:, 7], vec[:, V_PS + g:V_PS + g + 1],
                                         u_hi[:, 4 + g, tok(h)].bitcast(f), ALU.mult, ALU.subtract).then_inc(pl_ok, 1)

            def softmax(n):
                kv = n % 2
                own = ps[:, 2:4].rearrange("p b (c k) -> p (b c) k", c=2)[:, :, P:2 * P]
                dve.wait_ge(sc_done, n + 1)
                if n < 2:
                    dve.memset(probs[:, n % 2], -1e30).then_inc(prev_ok, 1)
                dve.wait_ge(prev_ok, n + 1)
                dve.copy_predicated(out=probs[:, n % 2], mask=own_mask[:, :].bitcast(u32).unsqueeze(1).broadcast_to([P, 4, P]),
                                    data=own).then_inc(sel_ok, 1)
                dve.wait_ge(sel_ok, n + 1)
                dve.tensor_reduce(row_max, probs[:, n % 2], AX.X, ALU.max).then_inc(max_ok, 1)
                dve.wait_ge(max_ok, n + 1)
                dve.scalar_tensor_tensor(neg_max, row_max, -HEAD ** -0.5, neg_sinks[:, 4 * kv:4 * kv + 4],
                                         ALU.mult, ALU.min).then_inc(neg_ok, 1)
                dve.wait_ge(neg_ok, n + 1)
                dve.tensor_tensor(sink_sh, neg_max, sinks[:, 4 * kv:4 * kv + 4], ALU.add).then_inc(sd_ok, 1)

            def normalise(n):
                dve.wait_ge(exp_ok, 5 * (n + 1))
                dve.tensor_tensor(denom, row_sum, sink_exp, ALU.add).then_inc(den_ok, 1)
                dve.wait_ge(den_ok, n + 1)
                dve.reciprocal(recip, denom).then_inc(rec_ok, 1)
                dve.wait_ge(rec_ok, n + 1)
                dve.tensor_tensor(probs[:, n % 2], probs[:, n % 2], recip.unsqueeze(2).broadcast_to([P, 4, P]),
                                  ALU.mult).then_inc(prob_ok, 1)

            def masked_t(n):
                dve.wait_ge(t_done, n + 1)
                above(dve, pv_done, n)
                for a in range(2):
                    dve.tensor_tensor(pt[:, a], ps[:, 4].rearrange("p (c q) -> p c q", c=4),
                                      own_t[:, a].unsqueeze(1).broadcast_to([P, 4, P]), ALU.mult).then_inc(pt_ok, 1)

            def attn_low(n):
                b, rows = n // 2, slice(n % 2 * HEAD, (n % 2 + 1) * HEAD)
                dve.wait_ge(yh_ok, n + 1)
                dve.tensor_tensor(u_lo[rows, 0:4, b * P:(b + 1) * P], ps[rows, 5].rearrange("p (c q) -> p c q", c=4),
                                  u_hi[rows, 0:4, b * P:(b + 1) * P].bitcast(f), ALU.subtract).then_inc(yl_ok, 1)

            def out_residual(m):
                d, h = (m - OUT0) % KC, (m - OUT0) // KC
                dve.wait_ge(z_done, m + 1)
                dve.wait_ge(acc_ok, KC * 4)
                dve.scalar_tensor_tensor(acc[:, d, tok(h)], ps[:, m % 2], coef[:, C_N + C_GATE + d:C_N + C_GATE + d + 1],
                                         acc[:, d, tok(h)], ALU.mult, ALU.add).then_inc(o_used, 1)
                add_total(2 + h, d, (o_used, m - OUT0 + 1))

            total(1)
            rotate_unit(0)
            centre(1)
            deviation(1)
            diagonal(1)
            rotate_unit(2)
            for m in range(3, 6):
                input_chunks(3, 2 * m - 6, 2 * m - 4)
                rotate_unit(m)
            input_chunks(3, 6, KC)
            dve.wait_ge(sink_ok, 1)
            dve.wait_ge(mask_ok, 6)
            for x in range(SLOTS):
                if x in GROUP_SLOT:
                    softmax(GROUP_SLOT[x])
                if x == 1:
                    rotate_unit(NZ)
                if x in GROUP_SLOT:
                    normalise(GROUP_SLOT[x])
                if x in (8, 9):
                    rotate_unit(NZ + x - 2)
                if x == 9:
                    rotate_unit(2 * NZ - 2)
                if x in OUT_SLOT:
                    out_residual(OUT0 + OUT_SLOT[x])
                if x in POOL_SLOT:
                    pool_low(POOL_SLOT[x])
                if x - 2 in GROUP_SLOT:
                    attn_low(GROUP_SLOT[x - 2])
                if x - 1 in GROUP_SLOT:
                    masked_t(GROUP_SLOT[x - 1])
                if x + 1 in POOL_SLOT:
                    differences(POOL_SLOT[x + 1])
                if x == 9:
                    rotate_unit(2 * NZ - 1)
            attn_low(15)
            centre(2, 0, 4)
            out_residual(OUT0 + KC)
            centre(2, 4, KC)
            out_residual(OUT0 + KC + 1)
            out_residual(OUT0 + KC + 2)
            deviation(2)
            diagonal(2)
            out_residual(OUT0 + KC + 3)
            input_chunks(4, 0, 3)
            out_residual(OUT0 + KC + 4)
            input_chunks(4, 3, 6)
            out_residual(OUT0 + KC + 5)
            input_chunks(4, 6, KC)
            out_residual(OUT0 + KC + 6)
            out_residual(OUT0 + KC + 7)

            ffn(1)
            for c in range(KC - 3, KC):
                normal(4, c)
            dve.wait_ge(ln_mean, 6)
            even = scratch[:, 0, H:]
            for c in range(KC):
                dve.tensor_tensor(acc[:, c, tok(1)], acc[:, c, tok(1)], ps[:, 6], ALU.subtract).then_inc(ln_cent, 1)
                if c in (3, 5, 7):
                    dve.wait_ge(ln_sq, KC * 5 + c)
                    above(dve, even_sum, c // 2 - 1)
                    dve.tensor_tensor(even, even if c > 3 else hid[:, 0, 0:H], hid[:, (c - 1) % 4, 0:H], ALU.add).then_inc(even_sum, 1)
            dve.wait_ge(odd_sum, 3)
            dve.wait_ge(even_sum, 3)
            dve.tensor_tensor(even, even, scratch[:, 2, 0:H], ALU.add).then_inc(even_sum, 1)
            deviation(5)
            diagonal(5)
            for c in range(KC):
                normal(5, c)
                if c >= 3 and c % 2 == 1:
                    finish(KC + c - 2)
            finish(2 * KC - 1)


_PARAMS = ["w_ada", "b_ada", "ffn1_w1", "ffn1_w3", "ffn1_w2", "ln1_g", "ln1_b", "w_in", "b_in", "attn_sinks", "w_pool",
           "pool_scale", "w_out", "b_out", "ln2_g", "ln2_b", "ffn2_w1", "ffn2_w3", "ffn2_w2", "ln3_g", "ln3_b"]


def _tables():
    import numpy as np
    rot = HEAD // 4
    freq = (500000.0 ** (-np.arange(0, rot, 2, dtype=np.float64) / rot)).astype(np.float32)
    ang = (np.arange(S, dtype=np.float32)[None, :] * freq[:, None]).astype(np.float64)
    cos, sin = np.ones((P, S), np.float32), np.zeros((P, S), np.float32)
    for base in (0, HEAD):
        for sign, at in ((-1.0, 0), (1.0, rot // 2)):
            cos[base + at:base + at + rot // 2] = np.cos(ang)
            sin[base + at:base + at + rot // 2] = sign * np.sin(ang)
    cnt = np.stack([1.0 / np.minimum(np.arange(PAD) + 1, w) for w in WIN])
    return {"rope_cos": cos, "rope_sin": sin,
            "inv_count": np.ascontiguousarray(np.broadcast_to(cnt[None], (P, 4, PAD))).astype(np.float32)}


def kernel(**inputs):
    import numpy as np
    import concourse.bacc as bacc
    from concourse.bass_utils import run_bass_kernel_spmd

    nc = bacc.Bacc("TRN2", target_bir_lowering=False, num_devices=1)
    arrays = {"x": np.ascontiguousarray(inputs["x"]).reshape(S, D), "c": np.ascontiguousarray(inputs["c"])}
    for name in _PARAMS:
        a = np.ascontiguousarray(inputs[name])
        arrays[name] = a if a.ndim == 2 else a.reshape(a.shape[1:])
    arrays.update(_tables())
    t = {name: nc.dram_tensor(name, a.shape, mybir.dt.from_np(a.dtype), kind="ExternalInput").ap() for name, a in arrays.items()}
    out = nc.dram_tensor("out", (S, D), mybir.dt.float32, kind="ExternalOutput").ap()
    layer(nc, t, out)
    r = run_bass_kernel_spmd(nc, [arrays], core_ids=[0])
    return r.results[0]["out"].reshape(1, S, D)
```
